# Optimizing a Trainium2 kernel written in Bass

```python
import math
import jax, jax.numpy as jnp
from jax import lax
import numpy as np

D_MODEL = 1024
BATCH = 1
SEQ = 512
DEPTH = 2
DEC_BATCH = 8
DEC_SEQ = 8
PAST_LEN = 4096
PAGE_SIZE = 128

ROPE_THETA = 500000.0
NORM_EPS = 1e-6
NEG_INF = -1e30
N_MLA_LAYERS = (DEPTH + 1) // 2
N_SWA_LAYERS = DEPTH // 2

MLA_HEADS = 16
MLA_Q_LORA = 384
MLA_KV_LORA = 256
MLA_NOPE = 64
MLA_ROPE = 32
MLA_V = 64
MLA_QBLK = 128
MLA_SCALE = (MLA_NOPE + MLA_ROPE) ** -0.5

SWA_HEADS = 16
SWA_KV_HEADS = 4
SWA_GROUP = SWA_HEADS // SWA_KV_HEADS
SWA_HEAD_DIM = D_MODEL // SWA_HEADS
SWA_ROT = SWA_HEAD_DIM // 4
SWA_SCALE = SWA_HEAD_DIM ** -0.5
WINDOW = 128

PEER_HEADS = 8
PEER_N_KEYS = 128
PEER_N_EXPERTS = PEER_N_KEYS * PEER_N_KEYS
PEER_TOPK = 16
PEER_KEY_DIM = 256
PEER_HALF = PEER_KEY_DIM // 2
PEER_BLOCK = 64

kernel_name = 'hybrid_mla_swa_peer_adaln_step'

def rmsnorm(x, g):
    xf = x.astype(jnp.float32)
    y = xf * lax.rsqrt(jnp.mean(xf * xf, axis=-1, keepdims=True) + NORM_EPS)
    return (y * g.astype(jnp.float32)).astype(x.dtype)

def rope(x, pos, rot_dim):
    half = rot_dim // 2
    inv_freq = ROPE_THETA ** (-jnp.arange(half, dtype=jnp.float32) * 2.0 / rot_dim)
    ang = pos.astype(jnp.float32)[:, None] * inv_freq[None, :]
    shape = (pos.shape[0],) + (1,) * (x.ndim - 3) + (half,)
    cos = jnp.cos(ang).reshape(shape)
    sin = jnp.sin(ang).reshape(shape)
    xf = x[..., :rot_dim].astype(jnp.float32)
    x1, x2 = xf[..., :half], xf[..., half:]
    rot = jnp.concatenate([x1 * cos - x2 * sin, x2 * cos + x1 * sin], axis=-1).astype(x.dtype)
    return jnp.concatenate([rot, x[..., rot_dim:]], axis=-1)

def modulation(c, w, b):
    m = jax.nn.silu(c) @ w + b
    return jnp.split(m[:, None, :], 6, axis=-1)

def modulate(x, g, shift, scale):
    return rmsnorm(x, g) * (1.0 + scale) + shift

def mla_project(h, pos, w_in, q_norm, kv_norm, w_uq):
    B, T, _ = h.shape
    z = h @ w_in
    cq = rmsnorm(z[..., :MLA_Q_LORA], q_norm)
    ckv = rmsnorm(z[..., MLA_Q_LORA:MLA_Q_LORA + MLA_KV_LORA], kv_norm)
    kpe = rope(z[..., MLA_Q_LORA + MLA_KV_LORA:], pos, MLA_ROPE)
    q = (cq @ w_uq).reshape(B, T, MLA_HEADS, MLA_NOPE + MLA_ROPE)
    q_nope = q[..., :MLA_NOPE]
    q_pe = rope(q[..., MLA_NOPE:], pos, MLA_ROPE)
    return q_nope, q_pe, ckv, kpe

def mla_prompt(h, pos, w_in, q_norm, kv_norm, w_uq, w_uk, w_uv, w_o):
    B, S, _ = h.shape
    q_nope, q_pe, ckv, kpe = mla_project(h, pos, w_in, q_norm, kv_norm, w_uq)
    k_nope = jnp.einsum('bsl,lhn->bshn', ckv, w_uk)
    v = jnp.einsum('bsl,lhd->bshd', ckv, w_uv)
    nb = S // MLA_QBLK
    to_blocks = lambda t: jnp.moveaxis(t.reshape((B, nb, MLA_QBLK) + t.shape[2:]), 1, 0)
    k_pos = jnp.arange(S)

    def block(args):
        qn, qp, n = args
        q_pos = n * MLA_QBLK + jnp.arange(MLA_QBLK)
        s = (jnp.einsum('bqhn,bkhn->bhqk', qn, k_nope)
             + jnp.einsum('bqhr,bkr->bhqk', qp, kpe)).astype(jnp.float32) * MLA_SCALE
        s = jnp.where(k_pos[None, :] <= q_pos[:, None], s, NEG_INF)
        p = jax.nn.softmax(s, axis=-1).astype(v.dtype)
        return jnp.einsum('bhqk,bkhd->bqhd', p, v)

    o = lax.map(block, (to_blocks(q_nope), to_blocks(q_pe), jnp.arange(nb)))
    o = jnp.moveaxis(o, 0, 1).reshape(B, S, MLA_HEADS * MLA_V)
    return o @ w_o, ckv, kpe

def mla_sample(h, pos, cache_ckv, cache_kpe, page_table, w_in, q_norm, kv_norm, w_uq, w_uk, w_uv, w_o):
    DB, T, _ = h.shape
    q_nope, q_pe, ckv, kpe = mla_project(h, pos, w_in, q_norm, kv_norm, w_uq)
    past_ckv = cache_ckv[page_table].reshape(DB, -1, MLA_KV_LORA)
    past_kpe = cache_kpe[page_table].reshape(DB, -1, MLA_ROPE)
    keys_ckv = jnp.concatenate([past_ckv, ckv], axis=1)
    keys_kpe = jnp.concatenate([past_kpe, kpe], axis=1)
    k_pos = jnp.arange(keys_ckv.shape[1])
    q_lat = jnp.einsum('bqhn,lhn->bqhl', q_nope, w_uk)
    s = (jnp.einsum('bqhl,bkl->bhqk', q_lat, keys_ckv)
         + jnp.einsum('bqhr,bkr->bhqk', q_pe, keys_kpe)).astype(jnp.float32) * MLA_SCALE
    s = jnp.where(k_pos[None, :] <= pos[:, None], s, NEG_INF)
    p = jax.nn.softmax(s, axis=-1).astype(keys_ckv.dtype)
    o_lat = jnp.einsum('bhqk,bkl->bqhl', p, keys_ckv)
    o = jnp.einsum('bqhl,lhd->bqhd', o_lat, w_uv).reshape(DB, T, MLA_HEADS * MLA_V)
    return o @ w_o, ckv, kpe

def sink_attention(q, k, v, mask, sinks):
    s = jnp.einsum('nqkgd,nskd->nkgqs', q, k).astype(jnp.float32) * SWA_SCALE
    s = jnp.where(mask[:, None, None], s, NEG_INF)
    sink = jnp.broadcast_to(sinks.astype(jnp.float32).reshape(1, SWA_KV_HEADS, SWA_GROUP, 1, 1),
                            s.shape[:-1] + (1,))
    p = jax.nn.softmax(jnp.concatenate([s, sink], axis=-1), axis=-1)[..., :-1]
    return jnp.einsum('nkgqs,nskd->nqkgd', p.astype(v.dtype), v)

def swa_project(h, pos, w_qkv, b_qkv):
    B, T, _ = h.shape
    z = h @ w_qkv + b_qkv
    nq = SWA_HEADS * SWA_HEAD_DIM
    nk = SWA_KV_HEADS * SWA_HEAD_DIM
    q = z[..., :nq].reshape(B, T, SWA_KV_HEADS, SWA_GROUP, SWA_HEAD_DIM)
    k = z[..., nq:nq + nk].reshape(B, T, SWA_KV_HEADS, SWA_HEAD_DIM)
    v = z[..., nq + nk:].reshape(B, T, SWA_KV_HEADS, SWA_HEAD_DIM)
    return rope(q, pos, SWA_ROT), rope(k, pos, SWA_ROT), v

def swa_prompt(h, pos, w_qkv, b_qkv, sinks, w_o):
    B, S, _ = h.shape
    q, k, v = swa_project(h, pos, w_qkv, b_qkv)
    nb = S // WINDOW
    qb = q.reshape(B * nb, WINDOW, SWA_KV_HEADS, SWA_GROUP, SWA_HEAD_DIM)

    def band(t):
        tb = t.reshape(B, nb, WINDOW, SWA_KV_HEADS, SWA_HEAD_DIM)
        prev = jnp.concatenate([jnp.zeros_like(tb[:, :1]), tb[:, :-1]], axis=1)
        return jnp.concatenate([prev, tb], axis=2).reshape(B * nb, 2 * WINDOW, SWA_KV_HEADS, SWA_HEAD_DIM)

    blk = jnp.arange(nb)[:, None, None]
    q_pos = blk * WINDOW + jnp.arange(WINDOW)[None, :, None]
    k_pos = (blk - 1) * WINDOW + jnp.arange(2 * WINDOW)[None, None, :]
    mask = (k_pos >= 0) & (k_pos <= q_pos) & (q_pos - k_pos < WINDOW)
    mask = jnp.broadcast_to(mask[None], (B,) + mask.shape).reshape(B * nb, WINDOW, 2 * WINDOW)
    o = sink_attention(qb, band(k), band(v), mask, sinks).reshape(B, S, SWA_HEADS * SWA_HEAD_DIM)
    n_buf = min(WINDOW, S)
    return o @ w_o, k[:, S - n_buf:], v[:, S - n_buf:]

def swa_sample(h, pos, buf_k, buf_v, w_qkv, b_qkv, sinks, w_o):
    DB, T, _ = h.shape
    q, k, v = swa_project(h, pos, w_qkv, b_qkv)
    n_buf = buf_k.shape[1]
    k_all = jnp.concatenate([buf_k, k], axis=1)
    v_all = jnp.concatenate([buf_v, v], axis=1)
    k_pos = PAST_LEN - n_buf + jnp.arange(n_buf + T)
    mask = (k_pos[None, :] <= pos[:, None]) & (pos[:, None] - k_pos[None, :] < WINDOW)
    o = sink_attention(q, k_all, v_all, mask[None], sinks).reshape(DB, T, SWA_HEADS * SWA_HEAD_DIM)
    return o @ w_o, k_all[:, -n_buf:], v_all[:, -n_buf:]

def peer(h, w_q, sub_keys, u_tab, v_tab):
    B, T, D = h.shape
    n = B * T
    xt = h.reshape(n, D)
    q = (xt @ w_q).reshape(n, PEER_HEADS, 2, PEER_HALF)
    s = jnp.einsum('nhpd,hpkd->nhpk', q, sub_keys).astype(jnp.float32)
    s_top, i_top = lax.top_k(s, PEER_TOPK)
    cand_s = (s_top[:, :, 0, :, None] + s_top[:, :, 1, None, :]).reshape(n, PEER_HEADS, PEER_TOPK * PEER_TOPK)
    cand_i = (i_top[:, :, 0, :, None] * PEER_N_KEYS + i_top[:, :, 1, None, :]).reshape(n, PEER_HEADS, PEER_TOPK * PEER_TOPK)
    best_s, best_pos = lax.top_k(cand_s, PEER_TOPK)
    experts = jnp.take_along_axis(cand_i, best_pos, axis=-1)
    gates = jax.nn.softmax(best_s, axis=-1).astype(h.dtype)
    pad = (-n) % PEER_BLOCK
    nb = (n + pad) // PEER_BLOCK
    xb = jnp.pad(xt, ((0, pad), (0, 0))).reshape(nb, PEER_BLOCK, D)
    eb = jnp.pad(experts, ((0, pad), (0, 0), (0, 0))).reshape(nb, PEER_BLOCK, PEER_HEADS, PEER_TOPK)
    gb = jnp.pad(gates, ((0, pad), (0, 0), (0, 0))).reshape(nb, PEER_BLOCK, PEER_HEADS, PEER_TOPK)

    def block(args):
        x_b, e_b, g_b = args
        u = u_tab[e_b]
        act = jax.nn.gelu(jnp.einsum('td,thkd->thk', x_b, u), approximate=False)
        return jnp.einsum('thk,thkd->td', g_b * act, v_tab[e_b])

    out = lax.map(block, (xb, eb, gb))
    return out.reshape(nb * PEER_BLOCK, D)[:n].reshape(B, T, D)

def setup_inputs(seed: int = 0) -> dict:
    key = jax.random.key(seed)
    ks = jax.random.split(key, 30)

    def nrm(k, shape, scale):
        return jax.random.normal(k, shape, jnp.float32) * scale

    d = D_MODEL
    n_pages = PAST_LEN // PAGE_SIZE
    used = DEC_BATCH * n_pages
    n_pool = used + max(1, used // 4)
    page_table = jax.random.permutation(ks[0], n_pool)[:used].reshape(DEC_BATCH, n_pages).astype(jnp.int32)
    n_buf = min(WINDOW, PAST_LEN)
    mla_in = MLA_Q_LORA + MLA_KV_LORA + MLA_ROPE
    swa_in = (SWA_HEADS + 2 * SWA_KV_HEADS) * SWA_HEAD_DIM
    return {
        'x_prompt': nrm(ks[1], (BATCH, SEQ, d), 1.0),
        'x_sample': nrm(ks[2], (DEC_BATCH, DEC_SEQ, d), 1.0),
        'cache_mla_ckv': nrm(ks[3], (N_MLA_LAYERS, n_pool, PAGE_SIZE, MLA_KV_LORA), 1.0),
        'cache_mla_kpe': nrm(ks[4], (N_MLA_LAYERS, n_pool, PAGE_SIZE, MLA_ROPE), 1.0),
        'cache_swa_k': nrm(ks[5], (N_SWA_LAYERS, DEC_BATCH, n_buf, SWA_KV_HEADS, SWA_HEAD_DIM), 1.0),
        'cache_swa_v': nrm(ks[6], (N_SWA_LAYERS, DEC_BATCH, n_buf, SWA_KV_HEADS, SWA_HEAD_DIM), 1.0),
        'page_table': page_table,
        'c_prompt': nrm(ks[7], (BATCH, d), 1.0),
        'c_sample': nrm(ks[8], (DEC_BATCH, d), 1.0),
        'ln1_g': 1.0 + nrm(ks[9], (DEPTH, d), 0.02),
        'ln2_g': 1.0 + nrm(ks[10], (DEPTH, d), 0.02),
        'w_mod': nrm(ks[11], (DEPTH, d, 6 * d), 0.5 * d ** -0.5),
        'b_mod': nrm(ks[12], (DEPTH, 6 * d), 0.01),
        'mla_w_in': nrm(ks[13], (N_MLA_LAYERS, d, mla_in), d ** -0.5),
        'mla_q_norm': 1.0 + nrm(ks[14], (N_MLA_LAYERS, MLA_Q_LORA), 0.02),
        'mla_kv_norm': 1.0 + nrm(ks[15], (N_MLA_LAYERS, MLA_KV_LORA), 0.02),
        'mla_w_uq': nrm(ks[16], (N_MLA_LAYERS, MLA_Q_LORA, MLA_HEADS * (MLA_NOPE + MLA_ROPE)), MLA_Q_LORA ** -0.5),
        'mla_w_uk': nrm(ks[17], (N_MLA_LAYERS, MLA_KV_LORA, MLA_HEADS, MLA_NOPE), MLA_KV_LORA ** -0.5),
        'mla_w_uv': nrm(ks[18], (N_MLA_LAYERS, MLA_KV_LORA, MLA_HEADS, MLA_V), MLA_KV_LORA ** -0.5),
        'mla_w_o': nrm(ks[19], (N_MLA_LAYERS, MLA_HEADS * MLA_V, d), (MLA_HEADS * MLA_V) ** -0.5),
        'swa_w_qkv': nrm(ks[20], (N_SWA_LAYERS, d, swa_in), d ** -0.5),
        'swa_b_qkv': nrm(ks[21], (N_SWA_LAYERS, swa_in), 0.01),
        'swa_sinks': nrm(ks[22], (N_SWA_LAYERS, SWA_HEADS), 1.0),
        'swa_w_o': nrm(ks[23], (N_SWA_LAYERS, SWA_HEADS * SWA_HEAD_DIM, d), (SWA_HEADS * SWA_HEAD_DIM) ** -0.5),
        'peer_w_q': nrm(ks[24], (DEPTH, d, PEER_HEADS * PEER_KEY_DIM), d ** -0.5),
        'peer_sub_keys': nrm(ks[25], (DEPTH, PEER_HEADS, 2, PEER_N_KEYS, PEER_HALF), PEER_HALF ** -0.5),
        'peer_u': nrm(ks[26], (DEPTH, PEER_N_EXPERTS, d), d ** -0.5),
        'peer_v': nrm(ks[27], (DEPTH, PEER_N_EXPERTS, d), PEER_HEADS ** -0.5),
        'final_g': 1.0 + nrm(ks[28], (d,), 0.02),
    }

def reference(x_prompt, x_sample, cache_mla_ckv, cache_mla_kpe, cache_swa_k, cache_swa_v, page_table,
              c_prompt, c_sample, ln1_g, ln2_g, w_mod, b_mod,
              mla_w_in, mla_q_norm, mla_kv_norm, mla_w_uq, mla_w_uk, mla_w_uv, mla_w_o,
              swa_w_qkv, swa_b_qkv, swa_sinks, swa_w_o,
              peer_w_q, peer_sub_keys, peer_u, peer_v, final_g):
    pos_p = jnp.arange(x_prompt.shape[1])
    pos_s = PAST_LEN + jnp.arange(x_sample.shape[1])
    x_p, x_s = x_prompt, x_sample
    ckv_p, kpe_p, ckv_s, kpe_s = [], [], [], []
    swk_p, swv_p, swk_s, swv_s = [], [], [], []
    for i in range(DEPTH):
        j = i // 2
        sh1p, sc1p, g1p, sh2p, sc2p, g2p = modulation(c_prompt, w_mod[i], b_mod[i])
        sh1s, sc1s, g1s, sh2s, sc2s, g2s = modulation(c_sample, w_mod[i], b_mod[i])
        hp = modulate(x_p, ln1_g[i], sh1p, sc1p)
        hs = modulate(x_s, ln1_g[i], sh1s, sc1s)
        if i % 2 == 0:
            op, a, b = mla_prompt(hp, pos_p, mla_w_in[j], mla_q_norm[j], mla_kv_norm[j], mla_w_uq[j],
                                  mla_w_uk[j], mla_w_uv[j], mla_w_o[j])
            os_, c, d = mla_sample(hs, pos_s, cache_mla_ckv[j], cache_mla_kpe[j], page_table,
                                   mla_w_in[j], mla_q_norm[j], mla_kv_norm[j], mla_w_uq[j],
                                   mla_w_uk[j], mla_w_uv[j], mla_w_o[j])
            ckv_p.append(a); kpe_p.append(b); ckv_s.append(c); kpe_s.append(d)
        else:
            op, a, b = swa_prompt(hp, pos_p, swa_w_qkv[j], swa_b_qkv[j], swa_sinks[j], swa_w_o[j])
            os_, c, d = swa_sample(hs, pos_s, cache_swa_k[j], cache_swa_v[j],
                                   swa_w_qkv[j], swa_b_qkv[j], swa_sinks[j], swa_w_o[j])
            swk_p.append(a); swv_p.append(b); swk_s.append(c); swv_s.append(d)
        x_p = x_p + g1p * op
        x_s = x_s + g1s * os_
        x_p = x_p + g2p * peer(modulate(x_p, ln2_g[i], sh2p, sc2p), peer_w_q[i], peer_sub_keys[i], peer_u[i], peer_v[i])
        x_s = x_s + g2s * peer(modulate(x_s, ln2_g[i], sh2s, sc2s), peer_w_q[i], peer_sub_keys[i], peer_u[i], peer_v[i])
    y_prompt = rmsnorm(x_p, final_g)
    y_sample = rmsnorm(x_s, final_g)
    return (y_prompt, y_sample,
            jnp.stack(ckv_p), jnp.stack(kpe_p), jnp.stack(ckv_s), jnp.stack(kpe_s),
            jnp.stack(swk_p), jnp.stack(swv_p), jnp.stack(swk_s), jnp.stack(swv_s))


_drawn_inputs = setup_inputs


def setup_inputs(seed=0):
    import zlib

    import numpy as np

    out = dict(_drawn_inputs(seed))
    spreads = {}
    factors = {'cache_mla_ckv': 5.002,
     'cache_mla_kpe': 7.565,
     'ln1_g': 2.765,
     'ln2_g': 4.71,
     'b_mod': 3.744,
     'mla_q_norm': 8.0,
     'mla_kv_norm': 3.013,
     'swa_b_qkv': 6.093,
     'swa_sinks': 8.0,
     'final_g': 2.739}
    for name, (base, spread) in spreads.items():
        noise = np.random.default_rng([zlib.crc32(name.encode()), seed]).standard_normal(out[name].shape)
        drawn = base * np.exp(spread * noise) if base else spread * noise
        out[name] = __import__('jax').numpy.asarray(drawn.astype(out[name].dtype))
    for name, factor in factors.items():
        out[name] = (out[name] * factor).astype(out[name].dtype)
    return out
```

```python
from contextlib import ExitStack

import numpy as np

import concourse.bass as bass
from concourse import mybir

ALU = mybir.AluOpType
ACT = mybir.ActivationFunctionType
F32 = mybir.dt.float32
I32 = mybir.dt.int32
U32 = mybir.dt.uint32
AX_X = mybir.AxisListType.X

P = 128
D = 1024
DC = D // P
SEQ = 512
NTP = SEQ // P
NT = NTP + 1
DB = 8
DS = 8
NS = DB * DS
PAST = 4096
PAGE = 128
NPG = PAST // PAGE
EPS = 1e-6
NEG = -1e30
H = 16
QL, KL, NOPE, ROPE = 384, 256, 64, 32
QH = NOPE + ROPE
MLA_SCALE = float(QH) ** -0.5
HD = 64
KVH = 4
GRP = H // KVH
ROT = HD // 4
SWA_SCALE = float(HD) ** -0.5
SWA_N = (H + 2 * KVH) * HD
PH, NK, TOPK, HALF = 8, 128, 16, 128
HK = PH * TOPK
GP = 4
NG = NPG // GP
RING = 8
SLOTS = HK // RING
LAG = 2


START = 1


class Chain:

    def __init__(self, eng, done):
        self.eng, self.done, self.base, self.n = eng, done, 0, 0

    def round(self, base):
        self.base, self.n = base, 0

    def step(self, ins):
        ins.then_inc(self.done, 1)
        self.n += 1
        self.eng.wait_ge(self.done, self.base + self.n)

    def inc(self, ins):
        ins.then_inc(self.done, 1)
        self.n += 1

    def end(self, per):
        assert self.n == per, (self.n, per)
        self.eng.wait_ge(self.done, self.base + self.n)


def wait_apart(eng, sem, value, settled):
    if not isinstance(value, int):
        value = eng.to_reg(value)
    eng.wait_ge(*settled)
    eng.wait_ge(sem, value)


def build(nc, a, o):
    with ExitStack() as ctx:
        def sbuf(stack, name, shape, dt=F32):
            return stack.enter_context(nc.sbuf_tensor(name, shape, dt))

        live = []

        def sem(name):
            live.append(nc.alloc_semaphore(name=name))
            return live[-1]

        def renew_semaphores():
            with nc.Block() as block:
                @block.gpsimd
                def _(pool):
                    numbers = sorted(s.num for s in live)
                    first = numbers[0]
                    for n, nxt in zip(numbers, numbers[1:] + [None]):
                        if nxt != n + 1:
                            pool.sem_clear(range(first, n + 1))
                            first = nxt
            for s in live:
                nc.release_semaphore(s)
            live.clear()

        sb = lambda name, shape, dt=F32: sbuf(ctx, name, shape, dt)
        bank = [ctx.enter_context(nc.psum_tensor(f"bank{i}", [P, 512], F32)) for i in range(8)]

        x = sb("x", [P, NT, D])
        ident = sb("ident", [P, P])
        sel = sb("sel", [DB + 1, 2, P])
        cT = sb("cT", [P, DC, DB + 1])
        mod = sb("mod", [P, 2, 3 * D])
        stat = sb("stat", [P, 6])
        rstd = sb("rstd", [P, 4])
        junk = sb("junk", [P, D])

        def tiles(eng, body):
            with eng.Fori(0, NTP) as t:
                body(t, 0)
            body(NTP, 1)

        scratch = nc.dram_tensor("swa_scratch", (DB, DS, H, HD), F32).ap()
        setup(nc, a, sbuf, sem, bank, x, ident, sel, cT, stat)
        modulation(nc, a, sbuf, sem, bank, cT, sel, mod, 0, 0)
        mla(nc, a, o, sbuf, sem, bank, x, ident, mod, stat, rstd, junk, tiles)
        modulation(nc, a, sbuf, sem, bank, cT, sel, mod, 0, 1)
        peer(nc, a, sbuf, sem, bank, x, ident, mod, stat, rstd, junk, tiles, 0)
        renew_semaphores()
        modulation(nc, a, sbuf, sem, bank, cT, sel, mod, 1, 0)
        swa(nc, a, o, scratch, sbuf, sem, bank, x, ident, mod, stat, rstd, junk, tiles)
        modulation(nc, a, sbuf, sem, bank, cT, sel, mod, 1, 1)
        peer(nc, a, sbuf, sem, bank, x, ident, mod, stat, rstd, junk, tiles, 1)
        final_norm(nc, a, o, sbuf, sem, x, stat, rstd, junk, tiles)


def setup(nc, a, sbuf, sem, bank, x, ident, sel, cT, stat):
    s = ExitStack()
    c9 = sbuf(s, "c9", [DB + 1, D])
    e9 = sbuf(s, "e9", [DB + 1, D])
    loaded, zeroed, c_in = sem("su_loaded"), sem("su_zeroed"), sem("su_c_in")
    e_done, silu_done, cT_ps, cT_done = sem("su_e"), sem("su_silu"), sem("su_cT_ps"), sem("su_cT")
    with nc.Block() as block:
        @block.sync
        def _(sp):
            sp.dma_start(c9[0:1, :], a["c_prompt"]).then_inc(c_in, 16)
            sp.dma_start(c9[1:DB + 1, :], a["c_sample"]).then_inc(c_in, 16)
            sp.dma_start(ident[:], a["k_ident"]).then_inc(c_in, 16)
            sp.dma_start(sel[:], a["k_sel"]).then_inc(loaded, 16)
            sp.dma_start(x[:, 0:NTP, :], a["x_prompt"].rearrange("b (t p) d -> p (b t) d", p=P)).then_inc(loaded, 16)
            sp.wait_ge(zeroed, 1)
            sp.dma_start(x[0:NS, NTP, :], a["x_sample"].rearrange("b t d -> (b t) d")).then_inc(loaded, 16)
            sp.wait_ge(loaded, 48)

        @block.scalar
        def _(act):
            act.wait_ge(c_in, 48)
            nc.scalar.activation(e9[:], c9[:], ACT.Exp, scale=-1.0).then_inc(e_done, 1)
            act.wait_ge(cT_ps, 1)
            nc.scalar.copy(cT[:], bank[0][:, 0:DC * (DB + 1)].rearrange("p (c n) -> p c n", c=DC)).then_inc(cT_done, 1)

        @block.vector
        def _(dve):
            ch = Chain(dve, silu_done)
            nc.vector.memset(x[:, NTP, :], 0.0).then_inc(zeroed, 1)
            nc.vector.memset(stat[:, 3:4], EPS)
            nc.vector.memset(stat[:, 4:6], -0.5)
            dve.wait_ge(e_done, 1)
            ch.step(nc.vector.tensor_scalar(e9[:], e9[:], 1.0, None, ALU.add))
            ch.step(nc.vector.reciprocal(e9[:], e9[:]))
            ch.inc(nc.vector.tensor_tensor(c9[:], c9[:], e9[:], ALU.mult))

        @block.tensor
        def _(pe):
            pe.wait_ge(silu_done, 3)
            for c in range(DC):
                last = pe.transpose(bank[0][:, c * (DB + 1):(c + 1) * (DB + 1)], c9[:, c * P:(c + 1) * P],
                                    ident[0:DB + 1, 0:DB + 1])
            last.then_inc(cT_ps, 1)
    s.close()


def modulation(nc, a, sbuf, sem, bank, cT, sel, mod, layer, sub):
    tag = f"m{layer}{sub}_"
    NCH = 3 * D // 512
    s = ExitStack()
    w = [sbuf(s, tag + f"w{i}", [P, DC, 512]) for i in range(2)]
    bias = sbuf(s, tag + "bias", [DB + 1, 3 * D])
    gain = sbuf(s, tag + "gain", [DB + 1, D])
    rows = sbuf(s, tag + "rows", [DB + 1, 3 * D])
    w_in = [sem(tag + f"w_in{i}") for i in range(2)]
    vec_in, row_ps, row_done, scaled = sem(tag + "vec_in"), sem(tag + "row_ps"), sem(tag + "row"), sem(tag + "scaled")
    wide_ps, wide_act, wide_dve = sem(tag + "wide_ps"), sem(tag + "wide_act"), sem(tag + "wide_dve")
    w_src = a["w_mod"][layer][:, sub * 3 * D:(sub + 1) * 3 * D].rearrange("(c p) n -> p c n", p=P)
    g_src = a["ln1_g" if sub == 0 else "ln2_g"][layer:layer + 1, :]
    with nc.Block() as block:
        @block.sync
        def _(sp):
            sp.dma_start(bias[:], a["b_mod"][layer:layer + 1, sub * 3 * D:(sub + 1) * 3 * D].to_broadcast([DB + 1, 3 * D])).then_inc(vec_in, 16)
            sp.dma_start(gain[:], g_src.to_broadcast([DB + 1, D])).then_inc(vec_in, 16)
            for n in range(NCH):
                if n >= 2:
                    sp.wait_ge(row_ps, n - 1)
                sp.dma_start(w[n % 2][:], w_src[:, :, n * 512:(n + 1) * 512]).then_inc(w_in[n % 2], 16)

        @block.tensor
        def _(pe):
            for n in range(NCH):
                pe.wait_ge(w_in[n % 2], 16 * (n // 2 + 1))
                if n >= 2:
                    pe.wait_ge(row_done, n - 1)
                for c in range(DC):
                    last = pe.matmul(bank[n % 2][0:DB + 1, :], cT[:, c, :], w[n % 2][:, c, :],
                                     start=(c == 0), stop=(c == DC - 1))
                last.then_inc(row_ps, 1)
            pe.wait_ge(scaled, 1)
            for kind in range(2):
                for n in range(NCH):
                    if kind:
                        pe.wait_ge(wide_act if n % 2 else wide_dve, n // 2 + 1)
                    pe.matmul(bank[2 + n][:, :], sel[:, kind, :], rows[:, n * 512:(n + 1) * 512],
                              start=True, stop=True).then_inc(wide_ps, 1)

        def widen(eng, copy, done, odd):
            for kind in range(2):
                for n in range(odd, NCH, 2):
                    eng.wait_ge(wide_ps, kind * NCH + n + 1)
                    copy(mod[:, kind, n * 512:(n + 1) * 512], bank[2 + n][:, :]).then_inc(done, 1)

        @block.vector
        def _(dve):
            dve.wait_ge(vec_in, 32)
            for n in range(NCH):
                dve.wait_ge(row_ps, n + 1)
                part = slice(n * 512, (n + 1) * 512)
                nc.vector.tensor_tensor(rows[:, part], bank[n % 2][0:DB + 1, :], bias[:, part],
                                        ALU.add).then_inc(row_done, 1)
            dve.wait_ge(row_done, NCH)
            nc.vector.scalar_tensor_tensor(out=rows[:, D:2 * D], in0=rows[:, D:2 * D], scalar=1.0, in1=gain[:],
                                           op0=ALU.add, op1=ALU.mult).then_inc(scaled, 1)
            widen(dve, nc.vector.tensor_copy, wide_dve, 0)

        @block.scalar
        def _(act):
            widen(act, nc.scalar.copy, wide_act, 1)
    s.close()


def rms(nc, rstd, stat, cols, added, count):
    n = cols.stop - cols.start
    nc.gpsimd.tensor_tensor(rstd[:, cols], stat[:, cols], stat[:, 3:4].to_broadcast([P, n]), ALU.add).then_inc(added, 1)
    nc.gpsimd.wait_ge(added, count)
    return nc.gpsimd.tensor_tensor(rstd[:, cols], rstd[:, cols], stat[:, 4:4 + n], ALU.pow)


def norm_steps(nc, ch, x, mod, rstd, h, t, kind):
    ch.step(nc.vector.scalar_tensor_tensor(out=h[:], in0=x[:, t, :], scalar=rstd[:, 0:1], in1=mod[:, kind, D:2 * D],
                                           op0=ALU.mult, op1=ALU.mult))
    ch.step(nc.vector.tensor_tensor(h[:], h[:], mod[:, kind, 0:D], ALU.add))


def mla(nc, a, o, sbuf, sem, bank, x, ident, mod, stat, rstd, junk, tiles):
    s = ExitStack()
    ckv = sbuf(s, "ckv", [P, NT, KL])
    ckvT = sbuf(s, "ckvT", [P, 2, NT * P])
    kpe = sbuf(s, "kpe", [P, NT, ROPE])
    o_tok = sbuf(s, "o_tok", [P, NT, D])
    wuk = sbuf(s, "wuk", [P, 2, H * NOPE])
    wuv = sbuf(s, "wuv", [P, 2, H * HD])
    kT = sbuf(s, "kT", [QH, NT * P])
    s1 = ExitStack()
    q = sbuf(s1, "q", [P, NT, H * QH])
    mla_project(nc, a, o, sbuf, sem, bank, x, ident, mod, stat, rstd, junk, tiles, q, ckv, ckvT, kpe, kT, wuk, wuv)
    mla_prompt(nc, a, sbuf, sem, bank, ident, q, ckvT, kT, wuk, wuv, o_tok)
    qlT = sbuf(s1, "qlT", [P, 2, DB, P])
    qpT = sbuf(s1, "qpT", [ROPE, DB, P])
    kpeT = sbuf(s1, "kpeT", [ROPE, NS])
    mla_sample_queries(nc, sbuf, sem, bank, ident, q, kpe, wuk, qlT, qpT, kpeT)
    mla_sample(nc, a, sbuf, sem, bank, ident, ckv, ckvT, kpeT, qlT, qpT, wuv, o_tok)
    s1.close()
    project_out(nc, a["mla_w_o"][0], "mo_", sbuf, sem, bank, x, ident, mod, junk, tiles, o_tok)
    s.close()


def mla_project(nc, a, o, sbuf, sem, bank, x, ident, mod, stat, rstd, junk, tiles, q, ckv, ckvT, kpe, kT, wuk, wuv):
    s = ExitStack()
    ZN = QL + KL + ROPE
    w_in = sbuf(s, "mp_w_in", [P, DC, ZN])
    w_uq = sbuf(s, "mp_w_uq", [P, QL // P, H * QH])
    qn = sbuf(s, "mp_qn", [P, QL])
    kvn = sbuf(s, "mp_kvn", [P, KL])
    cos = sbuf(s, "mp_cos", [P, NT, ROPE])
    sin = sbuf(s, "mp_sin", [P, NT, ROPE])
    h = sbuf(s, "mp_h", [P, D])
    hT = sbuf(s, "mp_hT", [P, DC, P])
    cq = sbuf(s, "mp_cq", [P, QL])
    cqT = sbuf(s, "mp_cqT", [P, QL // P, P])
    ks = sbuf(s, "mp_ks", [P, KL])
    kp96 = sbuf(s, "mp_kp96", [P, QH])
    ta = sbuf(s, "mp_ta", [P, H, ROPE])
    tb = sbuf(s, "mp_tb", [P, H, ROPE])
    names = "w_in vec_in x_ss h_ready hT_ps hT_ready z_ps z_ss latT_ps latT_ready q_ps q_copied dve_step stored later kept x_rms z_rms first added"
    (S_w, S_vec, S_xss, S_h, S_hTps, S_hT, S_zps, S_zss, S_latTps, S_latT, S_qps, S_qcp, S_dve,
     S_st, S_later, S_kept, S_xr, S_zr, S_1, S_add) = [sem("mp_s_" + n) for n in names.split()]
    HB = ROPE // 2
    H_AT, LAT_AT, PER = 2, 2 + 2 + 4, 2 + 2 + 4 + 4
    with nc.Block() as block:
        @block.sync
        def _(sp):
            sp.dma_start(qn[:], a["mla_q_norm"][0:1, :].to_broadcast([P, QL])).then_inc(S_vec, 16)
            sp.dma_start(kvn[:], a["mla_kv_norm"][0:1, :].to_broadcast([P, KL])).then_inc(S_vec, 16)
            sp.dma_start(cos[:], a["k_cos32"]).then_inc(S_vec, 16)
            sp.dma_start(sin[:], a["k_sin32"]).then_inc(S_vec, 16)
            sp.dma_start(w_in[:], a["mla_w_in"][0].rearrange("(c p) n -> p c n", p=P)).then_inc(S_w, 16)
            sp.dma_start(w_uq[:], a["mla_w_uq"][0].rearrange("(c p) n -> p c n", p=P)).then_inc(S_w, 16)
            sp.dma_start(wuk[:], a["mla_w_uk"][0].rearrange("(c p) h n -> p c (h n)", p=P)).then_inc(S_later, 16)
            sp.dma_start(wuv[:], a["mla_w_uv"][0].rearrange("(c p) h n -> p c (h n)", p=P)).then_inc(S_later, 16)
            sp.wait_ge(S_kept, NT + START)
            sp.dma_start(o["ckv_p"][0, 0].rearrange("(t p) l -> p t l", p=P), ckv[:, 0:NTP, :]).then_inc(S_st, 16)
            sp.dma_start(o["ckv_s"][0].rearrange("b t l -> (b t) l"), ckv[0:NS, NTP, :]).then_inc(S_st, 16)
            sp.dma_start(o["kpe_p"][0, 0].rearrange("(t p) l -> p t l", p=P), kpe[:, 0:NTP, :]).then_inc(S_st, 16)
            sp.dma_start(o["kpe_s"][0].rearrange("b t l -> (b t) l"), kpe[0:NS, NTP, :]).then_inc(S_st, 16)
            sp.wait_ge(S_later, 32)
            sp.wait_ge(S_st, 64)

        @block.gpsimd
        def _(pool):
            nc.gpsimd.memset(rstd[:], 0.0).then_inc(S_1, 1)

            def body(t, kind):
                wait_apart(pool, S_xss, t + 1, (S_1, 1))
                rms(nc, rstd, stat, slice(0, 1), S_add, 2 * t + 1).then_inc(S_xr, 1)
                wait_apart(pool, S_zss, 2 * t + 2, (S_1, 1))
                rms(nc, rstd, stat, slice(1, 3), S_add, 2 * t + 2).then_inc(S_zr, 1)
                pool.wait_ge(S_dve, t * PER + LAT_AT)
                nc.gpsimd.tensor_copy(ckv[:, t, :], ks[:])
                nc.gpsimd.tensor_copy(kpe[:, t, :], kp96[:, NOPE:QH]).then_inc(S_kept, 1)
            tiles(pool, body)

        @block.scalar
        def _(act):
            def body(t, kind):
                nc.scalar.activation(junk[:], x[:, t, :], ACT.Square, scale=D ** -0.5,
                                     accum_out=stat[:, 0:1]).then_inc(S_xss, 1)
                for half in range(2):
                    act.wait_ge(S_hTps, 2 * t + half + 1)
                    nc.scalar.copy(hT[:, 4 * half:4 * half + 4, :],
                                   bank[half][:].rearrange("p (c n) -> p c n", c=4)).then_inc(S_hT, 1)
                act.wait_ge(S_zps, t + 1)
                nc.scalar.activation(junk[:, 0:QL], bank[2][:, 0:QL], ACT.Square, scale=QL ** -0.5,
                                     accum_out=stat[:, 1:2]).then_inc(S_zss, 1)
                nc.scalar.activation(junk[:, QL:QL + KL], bank[3][:, 0:KL], ACT.Square, scale=KL ** -0.5,
                                     accum_out=stat[:, 2:3]).then_inc(S_zss, 1)
                act.wait_ge(S_latTps, t + 1)
                nc.scalar.copy(cqT[:], bank[4][:, 0:QL].rearrange("p (c n) -> p c n", c=QL // P)).then_inc(S_latT, 1)
                nc.scalar.copy(ckvT[:, :, bass.ds(t * P, P)],
                               bank[5][:, 0:KL].rearrange("p (c n) -> p c n", c=2)).then_inc(S_latT, 1)
                nc.scalar.copy(kT[NOPE:QH, bass.ds(t * P, P)], bank[5][NOPE:QH, KL:KL + P]).then_inc(S_latT, 1)
                act.wait_ge(S_qps, t + 1)
                for i, b in enumerate((6, 7, 2)):
                    nc.scalar.copy(q[:, t, i * 512:(i + 1) * 512], bank[b][:]).then_inc(S_qcp, 1)
            tiles(act, body)

        @block.vector
        def _(dve):
            ch = Chain(dve, S_dve)
            nc.vector.memset(kp96[:], 0.0)
            dve.sem_inc(S_kept, START)
            dve.wait_ge(S_vec, 64)

            def rotate(src, dst, c, sn, n):
                A, B = ta[:, 0:n, :], tb[:, 0:n, :]
                ch.inc(nc.vector.tensor_tensor(A, src, c.to_broadcast([P, n, ROPE]), ALU.mult))
                ch.inc(nc.vector.tensor_tensor(B[:, :, 0:HB], src[:, :, HB:ROPE], sn[:, :, 0:HB].to_broadcast([P, n, HB]), ALU.mult))
                ch.step(nc.vector.tensor_tensor(B[:, :, HB:ROPE], src[:, :, 0:HB], sn[:, :, HB:ROPE].to_broadcast([P, n, HB]), ALU.mult))
                ch.inc(nc.vector.tensor_tensor(dst, A, B, ALU.add))

            def body(t, kind):
                ch.round(t * PER)
                dve.wait_ge(S_xr, t + 1)
                norm_steps(nc, ch, x, mod, rstd, h, t, kind)
                dve.wait_ge(S_zr, t + 1)
                ch.inc(nc.vector.scalar_tensor_tensor(out=cq[:], in0=bank[2][:, 0:QL], scalar=rstd[:, 1:2], in1=qn[:],
                                                      op0=ALU.mult, op1=ALU.mult))
                dve.wait_ge(S_kept, t + START)
                ch.inc(nc.vector.scalar_tensor_tensor(out=ks[:], in0=bank[3][:, 0:KL], scalar=rstd[:, 2:3], in1=kvn[:],
                                                      op0=ALU.mult, op1=ALU.mult))
                rotate(bank[3][:, KL:KL + ROPE].rearrange("p (a r) -> p a r", a=1),
                       kp96[:, NOPE:QH].rearrange("p (a r) -> p a r", a=1),
                       cos[:, bass.ds(t, 1), :], sin[:, bass.ds(t, 1), :], 1)
                dve.wait_ge(S_qcp, 3 * t + 3)
                qv = q[:, t, :].rearrange("p (h r) -> p h r", h=H)[:, :, NOPE:QH]
                rotate(qv, qv, cos[:, bass.ds(t, 1), :], sin[:, bass.ds(t, 1), :], H)
                ch.end(PER)
            tiles(dve, body)

        @block.tensor
        def _(pe):
            pe.wait_ge(S_w, 32)

            def body(t, kind):
                pe.wait_ge(S_dve, t * PER + H_AT)
                for half in range(2):
                    for c in range(4):
                        last = pe.transpose(bank[half][:, c * P:(c + 1) * P],
                                            h[:, (4 * half + c) * P:(4 * half + c + 1) * P], ident[:])
                    last.then_inc(S_hTps, 1)
                pe.wait_ge(S_hT, 2 * t + 2)
                for c in range(DC):
                    pe.matmul(bank[2][:, 0:QL], hT[:, c, :], w_in[:, c, 0:QL], start=(c == 0), stop=(c == DC - 1))
                for c in range(DC):
                    last = pe.matmul(bank[3][:, 0:KL + ROPE], hT[:, c, :], w_in[:, c, QL:ZN],
                                     start=(c == 0), stop=(c == DC - 1))
                last.then_inc(S_zps, 1)
                pe.wait_ge(S_dve, t * PER + LAT_AT)
                for c in range(QL // P):
                    pe.transpose(bank[4][:, c * P:(c + 1) * P], cq[:, c * P:(c + 1) * P], ident[:])
                for c in range(2):
                    pe.transpose(bank[5][:, c * P:(c + 1) * P], ks[:, c * P:(c + 1) * P], ident[:])
                pe.transpose(bank[5][0:QH, KL:KL + P], kp96[:], ident[:]).then_inc(S_latTps, 1)
                pe.wait_ge(S_latT, 3 * t + 3)
                for i, b in enumerate((6, 7, 2)):
                    for c in range(QL // P):
                        last = pe.matmul(bank[b][:], cqT[:, c, :], w_uq[:, c, i * 512:(i + 1) * 512],
                                         start=(c == 0), stop=(c == QL // P - 1))
                last.then_inc(S_qps, 1)
            tiles(pe, body)
    s.close()


def attend(nc, sbuf, sem, bank, s, tag, rounds, units, scale, prep, v_of, out_of, sink_of=None):
    U = len(units)
    KMAX = max(u["n"] for u in units)
    probs = [sbuf(s, tag + f"probs{i}", [P, KMAX]) for i in range(2)]
    probsT = [sbuf(s, tag + f"probsT{i}", [P, KMAX]) for i in range(2)]
    top = sbuf(s, tag + "top", [P, U])
    bias = sbuf(s, tag + "bias", [P, U])
    total = sbuf(s, tag + "total", [P, U])
    esink = sbuf(s, tag + "esink", [P, U])
    inv = sbuf(s, tag + "inv", [P, U])
    names = "scores_ps bias_ready probs_ready probsT_ps probsT_ready out_ps out_free dve_step"
    S_sc, S_bias, S_pr, S_ptps, S_pt, S_ops, S_ofree, S_dve = [sem(tag + n) for n in names.split()]
    sink = sink_of is not None
    PER = sum(len(u["masks"]) + (4 if sink else 2) for u in units)

    def pool_body(pool):
        with pool.Fori(0, rounds) as i:
            prep["pool"](pool, i)

    def pe_body(pe):
        with pe.Fori(0, rounds) as i:
            prep["pe"](pe, i)

            def scores(u):
                un = units[u]
                pe.matmul(bank[2 + u % 2][:, 0:un["n"]], un["q"], un["k"], start=True, stop=True).then_inc(S_sc, 1)

            scores(0)
            for u, un in enumerate(units):
                if u + 1 < U:
                    scores(u + 1)
                pe.wait_ge(S_pr, i * U + u + 1)
                for j in range(un["n"] // P):
                    last = pe.transpose(bank[4 + u % 2][:, j * P:(j + 1) * P], probs[u % 2][:, j * P:(j + 1) * P], prep["ident"])
                last.then_inc(S_ptps, 1)
                pe.wait_ge(S_ofree, i * U + u + 1)
                pe.wait_ge(S_pt, i * U + u + 1)
                for j, kt in enumerate(un["keys"]):
                    last = pe.matmul(bank[6 + u % 2][:, 0:HD], probsT[u % 2][:, j * P:(j + 1) * P], v_of(i, u, kt),
                                     start=(j == 0), stop=(j == len(un["keys"]) - 1))
                last.then_inc(S_ops, 1)

    def act_body(act):
        with act.Fori(0, rounds) as i:
            prep["act"](act, i)
            for u, un in enumerate(units):
                wait_apart(act, S_bias, i * U + u + 1, prep["settled"])
                if sink:
                    nc.scalar.activation(esink[:, u:u + 1], sink_of(i, u), ACT.Exp, bias=bias[:, u:u + 1])
                nc.scalar.activation(probs[u % 2][:, 0:un["n"]], bank[2 + u % 2][:, 0:un["n"]], ACT.Exp,
                                     bias=bias[:, u:u + 1], scale=scale, accum_out=total[:, u:u + 1]).then_inc(S_pr, 1)

    def dve_body(dve):
        ch = Chain(dve, S_dve)
        nc.vector.memset(inv[:], 0.0).then_inc(S_ofree, 2)
        with dve.Fori(0, rounds) as i:
            ch.round(i * PER)

            def biases(u):
                un, b = units[u], bank[2 + u % 2]
                dve.wait_ge(S_sc, i * U + u + 1)
                for cols, mask in un["masks"]:
                    ch.step(nc.vector.tensor_tensor(b[:, cols], b[:, cols], mask, ALU.add))
                ch.step(nc.vector.tensor_reduce(top[:, u:u + 1], b[:, 0:un["n"]], AX_X, ALU.max))
                if sink:
                    ch.step(nc.vector.tensor_scalar(top[:, u:u + 1], top[:, u:u + 1], scale, sink_of(i, u), ALU.mult, ALU.max))
                nc.vector.tensor_scalar(bias[:, u:u + 1], top[:, u:u + 1], -1.0 if sink else -scale, None,
                                        ALU.mult).then_inc(S_bias, 1)

            biases(0)
            for u, un in enumerate(units):
                if u + 1 < U:
                    biases(u + 1)
                dve.wait_ge(S_ptps, i * U + u + 1)
                nc.vector.tensor_copy(probsT[u % 2][:, 0:un["n"]], bank[4 + u % 2][:, 0:un["n"]]).then_inc(S_pt, 1)
                dve.wait_ge(S_ops, i * U + u + 1)
                if sink:
                    ch.step(nc.vector.tensor_tensor(total[:, u:u + 1], total[:, u:u + 1], esink[:, u:u + 1], ALU.add))
                ch.step(nc.vector.reciprocal(inv[:, u:u + 1], total[:, u:u + 1]))
                nc.vector.tensor_scalar(out_of(i, u), bank[6 + u % 2][:, 0:HD], inv[:, u:u + 1], None,
                                        ALU.mult).then_inc(S_ofree, 1)
            ch.end(PER)

    return pool_body, pe_body, act_body, dve_body


def mla_prompt(nc, a, sbuf, sem, bank, ident, q, ckvT, kT, wuk, wuv, o_tok):
    s = ExitStack()
    v = sbuf(s, "at_v", [P, NTP, H * HD])
    qs = sbuf(s, "at_qs", [P, NTP, QH])
    wks = sbuf(s, "at_wks", [P, 2, NOPE])
    qT = sbuf(s, "at_qT", [QH, SEQ])
    causal = sbuf(s, "at_causal", [P, P])
    S_in, S_copied, S_qkps, S_qk, S_vps, S_v = [sem("at_" + n) for n in "mask_in copied qk_ps qk_ready v_ps v_ready".split()]

    def pool_prep(pool, i):
        pool.wait_ge(S_qkps, i + START)
        nc.gpsimd.tensor_copy(qs[:], q[:, 0:NTP, bass.ds(i * QH, QH)])
        nc.gpsimd.tensor_copy(wks[:], wuk[:, :, bass.ds(i * NOPE, NOPE)]).then_inc(S_copied, 1)

    def pe_prep(pe, i):
        pe.wait_ge(S_copied, i + 1)
        for t in range(NTP):
            pe.transpose(bank[0][0:QH, t * P:(t + 1) * P], qs[:, t, :], ident[:])
        for c in range(2):
            last = pe.matmul(bank[1][0:NOPE, :], wks[:, c, :], ckvT[:, c, 0:SEQ], start=(c == 0), stop=(c == 1))
        last.then_inc(S_qkps, 1)
        pe.wait_ge(S_qk, 2 * i + 2)

    def act_prep(act, i):
        act.wait_ge(S_qkps, i + 1 + START)
        nc.scalar.copy(qT[:], bank[0][0:QH, :]).then_inc(S_qk, 1)
        nc.scalar.copy(kT[0:NOPE, 0:SEQ], bank[1][0:NOPE, :]).then_inc(S_qk, 1)

    units = [dict(q=qT[:, n * P:(n + 1) * P], k=kT[:, 0:(n + 1) * P], n=(n + 1) * P,
                  masks=[(slice(n * P, (n + 1) * P), causal[:])], keys=list(range(n + 1))) for n in range(NTP)]
    pool_body, pe_body, act_body, dve_body = attend(
        nc, sbuf, sem, bank, s, "at_", H, units, MLA_SCALE,
        dict(pool=pool_prep, pe=pe_prep, act=act_prep, ident=ident[:], settled=(S_in, 16)),
        v_of=lambda i, u, kt: v[:, kt, bass.ds(i * HD, HD)],
        out_of=lambda i, u: o_tok[:, u, bass.ds(i * HD, HD)])
    with nc.Block() as block:
        @block.sync
        def _(sp):
            sp.dma_start(causal[:], a["k_causal"]).then_inc(S_in, 16)
            sp.wait_ge(S_in, 16)

        @block.gpsimd
        def _(pool):
            pool.sem_inc(S_qkps, START)
            pool_body(pool)

        @block.tensor
        def _(pe):
            for kt in range(NTP):
                for half in range(2):
                    for c in range(2):
                        last = pe.matmul(bank[2 * (kt % 4) + half][:], ckvT[:, c, kt * P:(kt + 1) * P],
                                         wuv[:, c, half * 512:(half + 1) * 512], start=(c == 0), stop=(c == 1))
                    last.then_inc(S_vps, 1)
            pe.wait_ge(S_v, 8)
            pe_body(pe)

        @block.scalar
        def _(act):
            for n in range(8):
                act.wait_ge(S_vps, n + 1)
                nc.scalar.copy(v[:, n // 2, (n % 2) * 512:(n % 2 + 1) * 512], bank[n][:]).then_inc(S_v, 1)
            act_body(act)

        @block.vector
        def _(dve):
            dve.wait_ge(S_in, 16)
            dve_body(dve)
    s.close()


def mla_sample_queries(nc, sbuf, sem, bank, ident, q, kpe, wuk, qlT, qpT, kpeT):
    s = ExitStack()
    wukT = sbuf(s, "sq_wukT", [P, H // 2, KL])
    qn = sbuf(s, "sq_qn", [NS, H, NOPE])
    qp = sbuf(s, "sq_qp", [NS, H, ROPE])
    qnT = sbuf(s, "sq_qnT", [P, H // 2, NS])
    S_cp, S_ps, S_w, S_ps2, S_rd, S_qlps = [sem("sq_" + n) for n in "copied w_ps w_ready q_ps q_ready ql_ps".split()]
    S_out = sem("sq_out")
    with nc.Block() as block:
        @block.gpsimd
        def _(pool):
            qv = q[0:NS, NTP, :].rearrange("p (h r) -> p h r", h=H)
            nc.gpsimd.tensor_copy(qn[:], qv[:, :, 0:NOPE]).then_inc(S_cp, 1)
            nc.gpsimd.tensor_copy(qp[:], qv[:, :, NOPE:QH]).then_inc(S_cp, 1)

        @block.tensor
        def _(pe):
            for j in range(H // 2):
                for c in range(2):
                    n = 2 * j + c
                    last = pe.transpose(bank[n // 4][:, (n % 4) * P:(n % 4 + 1) * P], wuk[:, c, j * P:(j + 1) * P], ident[:])
            last.then_inc(S_ps, 1)
            pe.wait_ge(S_cp, 2)
            for j in range(H // 2):
                pe.transpose(bank[4][:, j * NS:(j + 1) * NS], qn[:, 2 * j:2 * j + 2, :].rearrange("p h n -> p (h n)"),
                             ident[0:NS, 0:NS])
            for h in range(H):
                pe.transpose(bank[5 + h // 8][0:ROPE, (h % 8) * NS:(h % 8 + 1) * NS], qp[:, h, :], ident[0:NS, 0:NS])
            pe.transpose(bank[7][0:ROPE, 0:NS], kpe[0:NS, NTP, :], ident[0:NS, 0:NS]).then_inc(S_ps2, 1)
            pe.wait_ge(S_w, 4)
            pe.wait_ge(S_rd, 1)
            for h in range(H):
                r = slice((h % 2) * NOPE, (h % 2 + 1) * NOPE)
                for c in range(2):
                    last = pe.matmul(bank[2 * c + h % 2][:, (h // 2) * NS:(h // 2 + 1) * NS], wukT[r, h // 2, c * P:(c + 1) * P],
                                     qnT[r, h // 2, :], start=True, stop=True)
            last.then_inc(S_qlps, 1)

        @block.scalar
        def _(act):
            act.wait_ge(S_ps, 1)
            for n in range(4):
                nc.scalar.copy(wukT[:, 2 * n:2 * n + 2, :].rearrange("p a b -> p (a b)"), bank[n][:]).then_inc(S_w, 1)

        @block.vector
        def _(dve):
            dve.wait_ge(S_ps2, 1)
            nc.vector.tensor_copy(qnT[:], bank[4][:].rearrange("p (j n) -> p j n", j=H // 2)).then_inc(S_rd, 1)
            qpv = qpT[:].rearrange("p b (h t) -> p h b t", h=H)
            for n in range(2):
                nc.vector.tensor_copy(qpv[:, 8 * n:8 * n + 8], bank[5 + n][0:ROPE, :].rearrange("p (h b t) -> p h b t", h=8, b=DB))
            nc.vector.tensor_copy(kpeT[:], bank[7][0:ROPE, 0:NS])
            dve.wait_ge(S_qlps, 1)
            for c in range(2):
                qlv = qlT[:, c].rearrange("p b (h e t) -> p e h b t", e=2, h=H // 2)
                for n in range(2):
                    nc.vector.tensor_copy(qlv[:, n],
                                          bank[2 * c + n][:].rearrange("p (h b t) -> p h b t", h=8, b=DB)).then_inc(S_out, 1)
    s.close()


def mla_sample(nc, a, sbuf, sem, bank, ident, ckv, ckvT, kpeT, qlT, qpT, wuv, o_tok):
    s = ExitStack()
    PC = NG + 1
    KR = 4
    n_pool = a["cache_mla_ckv"].shape[1]
    kv = [sbuf(s, f"sa_kv{i}", [P, GP, KL + ROPE]) for i in range(KR)]
    kt = [sbuf(s, f"sa_kt{i}", [P, 3, GP * P]) for i in range(2)]
    probs = [sbuf(s, f"sa_probs{i}", [P, GP * P]) for i in range(2)]
    probsT = [sbuf(s, f"sa_probsT{i}", [P, GP * P]) for i in range(2)]
    qb = sbuf(s, "sa_qb", [P, 3, P])
    part = sbuf(s, "sa_part", [P, PC, KL])
    ntop = sbuf(s, "sa_ntop", [P, PC])
    bias = sbuf(s, "sa_bias", [P, PC])
    total = sbuf(s, "sa_total", [P, PC])
    wgt = sbuf(s, "sa_wgt", [P, PC])
    one = sbuf(s, "sa_one", [P, 4])
    olat = sbuf(s, "sa_olat", [P, KL])
    olT = sbuf(s, "sa_olT", [P, 2, H, NS])
    mask = sbuf(s, "sa_mask", [P, DB, NS])
    kv_in = [sem(f"sa_kv_in{i}") for i in range(KR)]
    names = "mask_in copied kT_ps kT_dve kT_act scores_ps bias_ready probs_ready probsT_ps probsT_ready part_ps part_done dve_step"
    (S_in, S_cp, S_ktps, S_ktd, S_kta, S_sc, S_bias, S_pr, S_ptps, S_pt, S_pps, S_pd, S_dve) = [sem("sa_" + n) for n in names.split()]
    S_join, S_wgt, S_ol, S_olps, S_olT, S_ops, S_zero = [sem("sa_" + n) for n in "join_ready wgt_ready olat_ready olat_ps olatT_ready o_ps zeroed".split()]
    PER = PC + 1 + 1 + 3 + (PC - 1)
    with nc.Block() as block:
        @block.sync
        def _(sp):
            sp.dma_start(mask[:], a["k_mask_new"]).then_inc(S_in, 16)
            with sp.Fori(0, DB) as b:
                for g in range(NG):
                    slot = g % KR
                    wait_apart(sp, S_pd, b * PC + (g if g < KR else g + 1) + START, (S_in, 16))
                    for j in range(GP):
                        page = sp.value_load(a["page_table"][bass.ds(b, 1), g * GP + j:g * GP + j + 1], min_val=0, max_val=n_pool - 1)
                        sp.dma_start(kv[slot][:, j, 0:KL], a["cache_mla_ckv"][0, bass.ds(page, 1)].rearrange("a p l -> p (a l)")).then_inc(kv_in[slot], 16)
                        sp.dma_start(kv[slot][:, j, KL:KL + ROPE], a["cache_mla_kpe"][0, bass.ds(page, 1)].rearrange("a p l -> p (a l)")).then_inc(kv_in[slot], 16)

        @block.gpsimd
        def _(pool):
            nc.gpsimd.memset(o_tok[:, NTP, :], 0.0).then_inc(S_zero, 1)
            pool.sem_inc(S_sc, START)
            with pool.Fori(0, DB) as b:
                pool.wait_ge(S_sc, b * PC + START)
                nc.gpsimd.tensor_copy(qb[:, 0, :], qlT[:, 0, bass.ds(b, 1), :].rearrange("p a n -> p (a n)"))
                nc.gpsimd.tensor_copy(qb[:, 1, :], qlT[:, 1, bass.ds(b, 1), :].rearrange("p a n -> p (a n)"))
                nc.gpsimd.tensor_copy(qb[0:ROPE, 2, :], qpT[:, bass.ds(b, 1), :].rearrange("p a n -> p (a n)")).then_inc(S_cp, 1)

        @block.tensor
        def _(pe):
            pe.sem_inc(S_olT, START)
            with pe.Fori(0, DB) as b:
                def turn(g):
                    slot = g % KR
                    pe.wait_ge(kv_in[slot], (b * (NG // KR) + g // KR + 1) * 2 * GP * 16)
                    for j in range(GP):
                        for c in range(2):
                            pe.transpose(bank[c][:, j * P:(j + 1) * P], kv[slot][:, j, c * P:(c + 1) * P], ident[:])
                        last = pe.transpose(bank[2][0:ROPE, j * P:(j + 1) * P], kv[slot][:, j, KL:KL + ROPE], ident[:])
                    last.then_inc(S_ktps, 1)

                def scores(g):
                    out = bank[6 if g % 2 else 3]
                    if g < NG:
                        pe.wait_ge(S_ktd, b * NG + g + 1)
                        pe.wait_ge(S_kta, b * NG + g + 1)
                        k = kt[g % 2]
                        pe.matmul(out[:], qb[:, 0, :], k[:, 0, :], start=True, stop=False)
                        pe.matmul(out[:], qb[:, 1, :], k[:, 1, :], start=False, stop=False)
                        pe.matmul(out[:], qb[0:ROPE, 2, :], k[0:ROPE, 2, :], start=False, stop=True).then_inc(S_sc, 1)
                    else:
                        pe.matmul(out[:, 0:NS], qb[:, 0, :], ckvT[:, 0, SEQ:SEQ + NS], start=True, stop=False)
                        pe.matmul(out[:, 0:NS], qb[:, 1, :], ckvT[:, 1, SEQ:SEQ + NS], start=False, stop=False)
                        pe.matmul(out[:, 0:NS], qb[0:ROPE, 2, :], kpeT[:], start=False, stop=True).then_inc(S_sc, 1)

                def turn_probs(g):
                    wait_apart(pe, S_pr, b * PC + g + 1, (S_in, 16))
                    if g == 0:
                        pe.wait_ge(S_olT, b + START)
                    if g < NG:
                        for j in range(GP):
                            last = pe.transpose(bank[4][:, j * P:(j + 1) * P], probs[g % 2][:, j * P:(j + 1) * P], ident[:])
                    else:
                        last = pe.transpose(bank[4][0:NS, 0:P], probs[g % 2][:, 0:NS], ident[:])
                    last.then_inc(S_ptps, 1)

                def values(g):
                    out = bank[7 if g % 2 else 5]
                    pe.wait_ge(S_pt, b * PC + g + 1)
                    if g >= 2:
                        pe.wait_ge(S_pd, b * PC + g - 1 + KR + START)
                    if g < NG:
                        for j in range(GP):
                            last = pe.matmul(out[:, 0:KL], probsT[g % 2][:, j * P:(j + 1) * P], kv[g % KR][:, j, 0:KL],
                                             start=(j == 0), stop=(j == GP - 1))
                    else:
                        last = pe.matmul(out[:, 0:KL], probsT[g % 2][0:NS, 0:P], ckv[0:NS, NTP, :], start=True, stop=True)
                    last.then_inc(S_pps, 1)

                pe.wait_ge(S_cp, b + 1)
                turn(0)
                scores(0)
                for g in range(PC):
                    if g + 1 < NG:
                        turn(g + 1)
                    if g + 1 < PC:
                        scores(g + 1)
                    turn_probs(g)
                    values(g)
                pe.wait_ge(S_ol, b + 1)
                for c in range(2):
                    last = pe.transpose(bank[4][:, c * P:(c + 1) * P], olat[:, c * P:(c + 1) * P], ident[:])
                last.then_inc(S_olps, 1)
            pe.wait_ge(S_olT, DB + START)
            for h in range(H):
                for c in range(2):
                    last = pe.matmul(bank[h // 8][0:NS, (h % 8) * HD:(h % 8 + 1) * HD], olT[:, c, h, :], wuv[:, c, h * HD:(h + 1) * HD],
                                     start=(c == 0), stop=(c == 1))
                if h % 8 == 7:
                    last.then_inc(S_ops, 1)

        @block.scalar
        def _(act):
            with act.Fori(0, DB) as b:
                def keys(g):
                    act.wait_ge(S_ktps, b * NG + g + 1)
                    nc.scalar.copy(kt[g % 2][:, 1, :], bank[1][:])
                    nc.scalar.copy(kt[g % 2][0:ROPE, 2, :], bank[2][0:ROPE, :]).then_inc(S_kta, 1)

                def exps(g):
                    n = GP * P if g < NG else NS
                    act.wait_ge(S_bias, b * PC + g + 1)
                    nc.scalar.activation(probs[g % 2][:, 0:n], bank[6 if g % 2 else 3][:, 0:n], ACT.Exp, bias=bias[:, g:g + 1],
                                         scale=MLA_SCALE, accum_out=total[:, g:g + 1]).then_inc(S_pr, 1)

                keys(0)
                for g in range(PC):
                    if g + 1 < NG:
                        keys(g + 1)
                    exps(g)
                act.wait_ge(S_join, b + 1)
                nc.scalar.activation(wgt[:], ntop[:], ACT.Exp, bias=one[:, 0:1], scale=-MLA_SCALE).then_inc(S_wgt, 1)
                act.wait_ge(S_olps, b + 1)
                for c in range(2):
                    last = nc.scalar.copy(olT[:, c, :, bass.ds(b * DS, DS)], bank[4][:, c * P:(c + 1) * P].rearrange("p (h t) -> p h t", h=H))
                last.then_inc(S_olT, 1)
            act.wait_ge(S_ops, 2)
            act.wait_ge(S_zero, 1)
            for n in range(2):
                nc.scalar.copy(o_tok[0:NS, NTP, n * 512:(n + 1) * 512], bank[n][0:NS, :])

        @block.vector
        def _(dve):
            ch = Chain(dve, S_dve)
            dve.wait_ge(S_in, 16)
            nc.vector.memset(one[:], 0.0).then_inc(S_pd, KR + START)
            with dve.Fori(0, DB) as b:
                ch.round(b * PER)

                def keys(g):
                    dve.wait_ge(S_ktps, b * NG + g + 1)
                    nc.vector.tensor_copy(kt[g % 2][:, 0, :], bank[0][:]).then_inc(S_ktd, 1)

                def biases(g):
                    src = bank[6 if g % 2 else 3]
                    n = GP * P if g < NG else NS
                    dve.wait_ge(S_sc, b * PC + g + 1 + START)
                    if g == NG:
                        ch.step(nc.vector.tensor_tensor(src[:, 0:n], src[:, 0:n], mask[:, bass.ds(b, 1), :].rearrange("p a n -> p (a n)"), ALU.add))
                    ch.step(nc.vector.tensor_reduce(ntop[:, g:g + 1], src[:, 0:n], AX_X, ALU.max, negate=True))
                    nc.vector.tensor_scalar(bias[:, g:g + 1], ntop[:, g:g + 1], MLA_SCALE, None, ALU.mult).then_inc(S_bias, 1)

                def parts(g):
                    dve.wait_ge(S_pps, b * PC + g + 1)
                    nc.vector.tensor_copy(part[:, g, :], bank[7 if g % 2 else 5][:, 0:KL]).then_inc(S_pd, 1)

                keys(0)
                biases(0)
                for g in range(PC):
                    if g + 1 < NG:
                        keys(g + 1)
                    if g >= 1:
                        parts(g - 1)
                    if g + 1 < PC:
                        biases(g + 1)
                    n = GP * P if g < NG else P
                    r = P if g < NG else NS
                    dve.wait_ge(S_ptps, b * PC + g + 1)
                    nc.vector.tensor_copy(probsT[g % 2][0:r, 0:n], bank[4][0:r, 0:n]).then_inc(S_pt, 1)
                ch.step(nc.vector.tensor_reduce(one[:, 1:2], ntop[:], AX_X, ALU.min))
                nc.vector.tensor_scalar(one[:, 0:1], one[:, 1:2], MLA_SCALE, None, ALU.mult).then_inc(S_join, 1)
                parts(NG)
                dve.wait_ge(S_wgt, b + 1)
                ch.step(nc.vector.scalar_tensor_tensor(out=total[:], in0=total[:], scalar=1.0, in1=wgt[:], op0=ALU.mult, op1=ALU.mult,
                                                       accum_out=one[:, 2:3]))
                ch.step(nc.vector.reciprocal(one[:, 3:4], one[:, 2:3]))
                ch.step(nc.vector.tensor_scalar(wgt[:], wgt[:], one[:, 3:4], None, ALU.mult))
                dve.wait_ge(S_pd, (b + 1) * PC + KR + START)
                ch.step(nc.vector.tensor_scalar(olat[:], part[:, 0, :], wgt[:, 0:1], None, ALU.mult))
                for g in range(1, PC):
                    join = nc.vector.scalar_tensor_tensor(out=olat[:], in0=part[:, g, :], scalar=wgt[:, g:g + 1], in1=olat[:],
                                                          op0=ALU.mult, op1=ALU.add)
                    if g < PC - 1:
                        ch.step(join)
                join.then_inc(S_ol, 1)
                ch.end(PER)
    s.close()


def project_out(nc, w_o, tag, sbuf, sem, bank, x, ident, mod, junk, tiles, o_tok):
    s = ExitStack()
    w = sbuf(s, tag + "w", [P, DC, D])
    os_ = sbuf(s, tag + "o", [P, D])
    oT = sbuf(s, tag + "oT", [P, DC, P])
    S_w, S_cp, S_tps, S_t, S_yps, S_dve = [sem(tag + n) for n in "w_in copied oT_ps oT_ready y_ps dve_step".split()]
    with nc.Block() as block:
        @block.sync
        def _(sp):
            sp.dma_start(w[:], w_o.rearrange("(c p) n -> p c n", p=P)).then_inc(S_w, 16)

        @block.gpsimd
        def _(pool):
            pool.sem_inc(S_tps, START)

            def body(t, kind):
                pool.wait_ge(S_tps, 2 * t + START)
                nc.gpsimd.tensor_copy(os_[:], o_tok[:, t, :]).then_inc(S_cp, 1)
            tiles(pool, body)

        @block.tensor
        def _(pe):
            pe.wait_ge(S_w, 16)

            def body(t, kind):
                pe.wait_ge(S_cp, t + 1)
                for half in range(2):
                    for c in range(4):
                        last = pe.transpose(bank[half][:, c * P:(c + 1) * P], os_[:, (4 * half + c) * P:(4 * half + c + 1) * P], ident[:])
                    last.then_inc(S_tps, 1)
                pe.wait_ge(S_t, 2 * t + 2)
                pe.wait_ge(S_dve, 3 * t + START)
                for n in range(2):
                    for c in range(DC):
                        last = pe.matmul(bank[2 + n][:], oT[:, c, :], w[:, c, n * 512:(n + 1) * 512], start=(c == 0), stop=(c == DC - 1))
                last.then_inc(S_yps, 1)
            tiles(pe, body)

        @block.scalar
        def _(act):
            def body(t, kind):
                for half in range(2):
                    act.wait_ge(S_tps, 2 * t + half + 1 + START)
                    act.wait_ge(S_yps, t + START)
                    nc.scalar.copy(oT[:, 4 * half:4 * half + 4, :], bank[half][:].rearrange("p (c n) -> p c n", c=4)).then_inc(S_t, 1)
            tiles(act, body)

        @block.vector
        def _(dve):
            dve.sem_inc(S_dve, START)
            dve.sem_inc(S_yps, START)

            def body(t, kind):
                dve.wait_ge(S_yps, t + 1 + START)
                for n in range(2):
                    nc.vector.tensor_tensor(junk[:, n * 512:(n + 1) * 512], bank[2 + n][:], mod[:, kind, 2 * D + n * 512:2 * D + (n + 1) * 512],
                                            ALU.mult).then_inc(S_dve, 1)
                dve.wait_ge(S_dve, 3 * t + 2 + START)
                nc.vector.tensor_tensor(x[:, t, :], x[:, t, :], junk[:], ALU.add).then_inc(S_dve, 1)
                dve.wait_ge(S_dve, 3 * t + 3 + START)
            tiles(dve, body)
    s.close()


def swa(nc, a, o, scratch, sbuf, sem, bank, x, ident, mod, stat, rstd, junk, tiles):
    s = ExitStack()
    o_tok = sbuf(s, "o_tok1", [P, NT, D])
    qkv = sbuf(s, "qkv", [P, NT, SWA_N])
    swa_project(nc, a, o, sbuf, sem, bank, x, ident, mod, stat, rstd, junk, tiles, qkv)
    swa_prompt(nc, a, sbuf, sem, bank, ident, qkv, o_tok)
    swa_sample(nc, a, o, scratch, sbuf, sem, bank, ident, qkv, o_tok)
    project_out(nc, a["swa_w_o"][0], "so_", sbuf, sem, bank, x, ident, mod, junk, tiles, o_tok)
    s.close()


def swa_project(nc, a, o, sbuf, sem, bank, x, ident, mod, stat, rstd, junk, tiles, qkv):
    s = ExitStack()
    w = sbuf(s, "sp_w", [P, DC, SWA_N])
    bq = sbuf(s, "sp_b", [P, SWA_N])
    cos = sbuf(s, "sp_cos", [P, NT, ROT])
    sin = sbuf(s, "sp_sin", [P, NT, ROT])
    h = sbuf(s, "sp_h", [P, D])
    hT = sbuf(s, "sp_hT", [P, DC, P])
    NR = H + KVH
    ta = sbuf(s, "sp_ta", [P, NR, ROT])
    tb = sbuf(s, "sp_tb", [P, NR, ROT])
    names = "w_in vec_in x_ss hT_ps hT_ready z_ps dve_step stored x_rms first added"
    S_w, S_vec, S_xss, S_hTps, S_hT, S_zps, S_dve, S_st, S_xr, S_1, S_add = [sem("sp_s_" + n) for n in names.split()]
    HB = ROT // 2
    PER = 2 + 3 + 4
    KC, VC, NKV = H * HD, (H + KVH) * HD, KVH * HD
    keep = SEQ - P
    with nc.Block() as block:
        @block.sync
        def _(sp):
            sp.dma_start(bq[:], a["swa_b_qkv"][0:1, :].to_broadcast([P, SWA_N])).then_inc(S_vec, 16)
            sp.dma_start(cos[:], a["k_cos16"]).then_inc(S_vec, 16)
            sp.dma_start(sin[:], a["k_sin16"]).then_inc(S_vec, 16)
            sp.dma_start(w[:], a["swa_w_qkv"][0].rearrange("(c p) n -> p c n", p=P)).then_inc(S_w, 16)
            for name, src in (("swk_s", a["cache_swa_k"]), ("swv_s", a["cache_swa_v"])):
                sp.dma_start(o[name][0][:, 0:P - DS].rearrange("b t g d -> b (t g d)"),
                             src[0][:, DS:P].rearrange("b t g d -> b (t g d)")).then_inc(S_st, 16)
            sp.wait_ge(S_dve, NT * PER)
            for name, c in (("p", KC), ("p", VC)):
                out = o["swk_p" if c == KC else "swv_p"][0, 0].rearrange("t g d -> t (g d)")
                sp.dma_start(out, qkv[:, NTP - 1, c:c + NKV]).then_inc(S_st, 16)
            for b in range(DB):
                for name, c in (("swk_s", KC), ("swv_s", VC)):
                    sp.dma_start(o[name][0, b, P - DS:P].rearrange("t g d -> t (g d)"),
                                 qkv[b * DS:(b + 1) * DS, NTP, c:c + NKV]).then_inc(S_st, 16)
            sp.wait_ge(S_st, 16 * (4 + 2 * DB))

        @block.gpsimd
        def _(pool):
            nc.gpsimd.memset(rstd[:], 0.0).then_inc(S_1, 1)

            def body(t, kind):
                wait_apart(pool, S_xss, t + 1, (S_1, 1))
                rms(nc, rstd, stat, slice(0, 1), S_add, t + 1).then_inc(S_xr, 1)
            tiles(pool, body)

        @block.scalar
        def _(act):
            def body(t, kind):
                nc.scalar.activation(junk[:], x[:, t, :], ACT.Square, scale=D ** -0.5,
                                     accum_out=stat[:, 0:1]).then_inc(S_xss, 1)
                for half in range(2):
                    act.wait_ge(S_hTps, 2 * t + half + 1)
                    nc.scalar.copy(hT[:, 4 * half:4 * half + 4, :],
                                   bank[half][:].rearrange("p (c n) -> p c n", c=4)).then_inc(S_hT, 1)
            tiles(act, body)

        @block.vector
        def _(dve):
            ch = Chain(dve, S_dve)
            dve.wait_ge(S_vec, 48)

            def body(t, kind):
                ch.round(t * PER)
                dve.wait_ge(S_xr, t + 1)
                norm_steps(nc, ch, x, mod, rstd, h, t, kind)
                dve.wait_ge(S_zps, t + 1)
                for n in range(3):
                    add = nc.vector.tensor_tensor(qkv[:, t, n * 512:(n + 1) * 512], bank[2 + n][:], bq[:, n * 512:(n + 1) * 512], ALU.add)
                    ch.step(add) if n == 2 else ch.inc(add)
                v = qkv[:, t, 0:NR * HD].rearrange("p (h r) -> p h r", h=NR)[:, :, 0:ROT]
                c, sn = cos[:, bass.ds(t, 1), :], sin[:, bass.ds(t, 1), :]
                ch.inc(nc.vector.tensor_tensor(ta[:], v, c.to_broadcast([P, NR, ROT]), ALU.mult))
                ch.inc(nc.vector.tensor_tensor(tb[:, :, 0:HB], v[:, :, HB:ROT], sn[:, :, 0:HB].to_broadcast([P, NR, HB]), ALU.mult))
                ch.step(nc.vector.tensor_tensor(tb[:, :, HB:ROT], v[:, :, 0:HB], sn[:, :, HB:ROT].to_broadcast([P, NR, HB]), ALU.mult))
                ch.inc(nc.vector.tensor_tensor(v, ta[:], tb[:], ALU.add))
                ch.end(PER)
            tiles(dve, body)

        @block.tensor
        def _(pe):
            pe.wait_ge(S_w, 16)

            def body(t, kind):
                pe.wait_ge(S_dve, t * PER + 2)
                for half in range(2):
                    for c in range(4):
                        last = pe.transpose(bank[half][:, c * P:(c + 1) * P],
                                            h[:, (4 * half + c) * P:(4 * half + c + 1) * P], ident[:])
                    last.then_inc(S_hTps, 1)
                pe.wait_ge(S_hT, 2 * t + 2)
                for n in range(3):
                    for c in range(DC):
                        last = pe.matmul(bank[2 + n][:], hT[:, c, :], w[:, c, n * 512:(n + 1) * 512],
                                         start=(c == 0), stop=(c == DC - 1))
                last.then_inc(S_zps, 1)
            tiles(pe, body)
    s.close()


def swa_prompt(nc, a, sbuf, sem, bank, ident, qkv, o_tok):
    s = ExitStack()
    qs = sbuf(s, "wt_qs", [P, NTP, GRP * HD])
    ks = sbuf(s, "wt_ks", [P, NTP, HD])
    qT = sbuf(s, "wt_qT", [HD, GRP, SEQ])
    kT = sbuf(s, "wt_kT", [HD, SEQ])
    band = sbuf(s, "wt_band", [P, 2 * P])
    sinks = sbuf(s, "wt_sinks", [P, H])
    S_in, S_cp, S_ps, S_rd = [sem("wt_" + n) for n in "mask_in copied qk_ps qk_ready".split()]

    def pool_prep(pool, i):
        pool.wait_ge(S_ps, i + START)
        nc.gpsimd.tensor_copy(qs[:], qkv[:, 0:NTP, bass.ds(i * GRP * HD, GRP * HD)])
        nc.gpsimd.tensor_copy(ks[:], qkv[:, 0:NTP, bass.ds(i * HD + H * HD, HD)]).then_inc(S_cp, 1)

    def pe_prep(pe, i):
        wait_apart(pe, S_cp, i + 1, (S_in, 32))
        for t in range(NTP):
            pe.transpose(bank[0][0:HD, t * P:(t + 1) * P], ks[:, t, :], ident[:])
        for j in range(GRP):
            for t in range(NTP):
                last = pe.transpose(bank[1 + j][0:HD, t * P:(t + 1) * P], qs[:, t, j * HD:(j + 1) * HD], ident[:])
        last.then_inc(S_ps, 1)
        pe.wait_ge(S_rd, i + 1)

    def act_prep(act, i):
        act.wait_ge(S_ps, i + 1 + START)
        nc.scalar.copy(kT[:], bank[0][0:HD, :])
        for j in range(GRP):
            last = nc.scalar.copy(qT[:, j, :], bank[1 + j][0:HD, :])
        last.then_inc(S_rd, 1)

    units = []
    for j in range(GRP):
        for n in range(NTP):
            k0 = max(n - 1, 0)
            m = band[:] if n else band[:, P:2 * P]
            units.append(dict(j=j, t=n, q=qT[:, j, n * P:(n + 1) * P], k=kT[:, k0 * P:(n + 1) * P], n=(n + 1 - k0) * P,
                              masks=[(slice(0, (n + 1 - k0) * P), m)], keys=list(range(k0, n + 1))))
    pool_body, pe_body, act_body, dve_body = attend(
        nc, sbuf, sem, bank, s, "wt_", KVH, units, SWA_SCALE,
        dict(pool=pool_prep, pe=pe_prep, act=act_prep, ident=ident[:], settled=(S_in, 32)),
        v_of=lambda i, u, kt: qkv[:, kt, bass.ds(i * HD + (H + KVH) * HD, HD)],
        out_of=lambda i, u: o_tok[:, units[u]["t"], bass.ds(i * GRP * HD + units[u]["j"] * HD, HD)],
        sink_of=lambda i, u: sinks[:, bass.ds(i * GRP + units[u]["j"], 1)])
    with nc.Block() as block:
        @block.sync
        def _(sp):
            sp.dma_start(band[:], a["k_band"]).then_inc(S_in, 16)
            sp.dma_start(sinks[:], a["swa_sinks"][0:1, :].to_broadcast([P, H])).then_inc(S_in, 16)

        @block.gpsimd
        def _(pool):
            pool.sem_inc(S_ps, START)
            pool_body(pool)

        @block.tensor
        def _(pe):
            pe_body(pe)

        @block.scalar
        def _(act):
            act_body(act)

        @block.vector
        def _(dve):
            dve.wait_ge(S_in, 32)
            dve_body(dve)
    s.close()


def swa_sample(nc, a, o, scratch, sbuf, sem, bank, ident, qkv, o_tok):
    s = ExitStack()
    NKV = KVH * HD
    TK = P + DS
    qt = sbuf(s, "ws_qt", [NS, 2, GRP, 2, HD])
    qbd = sbuf(s, "ws_qbd", [P, DB, 2, KVH, GRP, DS])
    qb = sbuf(s, "ws_qb", [P, 2, P])
    ka = [sbuf(s, f"ws_ka{i}", [P, NKV]) for i in range(2)]
    va = [sbuf(s, f"ws_va{i}", [P, NKV]) for i in range(2)]
    kb = [sbuf(s, f"ws_kb{i}", [DS, NKV]) for i in range(2)]
    vb = [sbuf(s, f"ws_vb{i}", [DS, NKV]) for i in range(2)]
    kT = sbuf(s, "ws_kT", [P, 2, TK])
    mask = sbuf(s, "ws_mask", [P, TK])
    snk = sbuf(s, "ws_sink", [P, 1])
    probs = sbuf(s, "ws_probs", [P, TK])
    pT = sbuf(s, "ws_pT", [P, 2 * P])
    st = sbuf(s, "ws_st", [P, 6])
    ow = [sbuf(s, f"ws_o{i}", [P, HD]) for i in range(2)]
    names = "const_in qt_ready q_ps q_ready zeroed qb_ready kT_ps kT_ready scores_ps bias_ready probs_ready pT_ps pT_ready o_ps o_ready dve_step joined"
    (S_in, S_qt, S_qps, S_q, S_z, S_qb, S_ktps, S_kt, S_sc, S_bias, S_pr, S_ptps, S_pt, S_ops, S_o, S_dve, S_join) = [
        sem("ws_" + n) for n in names.split()]
    kv_in = [sem(f"ws_kv_in{i}") for i in range(2)]
    stored = [sem(f"ws_stored{i}") for i in range(2)]
    PER = 6
    with nc.Block() as block:
        @block.sync
        def _(sp):
            sp.dma_start(mask[:], a["k_mask_win"]).then_inc(S_in, 16)
            sp.dma_start(snk[:], a["swa_sinks"].rearrange("a (h u) -> (a h) u", u=1).to_broadcast([H, DS]).rearrange("h (t u) -> h t u", u=1)).then_inc(S_in, 16)
            sp.sem_inc(S_ops, START)
            with sp.Fori(0, DB // 2) as i:
                for p in range(2):
                    b = i * 2 + p
                    sp.wait_ge(S_ops, i * 2 + START)
                    for dst, src in ((ka, o["swk_s"]), (va, o["swv_s"])):
                        sp.dma_start(dst[p][:], src[0, bass.ds(b, 1)].rearrange("b t g d -> (b t) (g d)")).then_inc(kv_in[p], 16)
                    for dst, src in ((kb, a["cache_swa_k"]), (vb, a["cache_swa_v"])):
                        sp.dma_start(dst[p][:], src[0, bass.ds(b, 1), 0:DS].rearrange("b t g d -> (b t) (g d)")).then_inc(kv_in[p], 16)
                for p in range(2):
                    b = i * 2 + p
                    sp.wait_ge(S_o, i * 2 + p + 1)
                    sp.dma_start(scratch[bass.ds(b, 1)].rearrange("b t h d -> h (b t) d"), ow[p][:]).then_inc(stored[p], 16)
            sp.wait_ge(stored[0], 16 * DB // 2 + START)
            sp.wait_ge(stored[1], 16 * DB // 2 + START)
            sp.dma_start(o_tok[0:NS, NTP, :], scratch.rearrange("b t h d -> (b t) (h d)")).then_inc(S_join, 16)
            sp.wait_ge(S_join, 16)

        @block.gpsimd
        def _(pool):
            qv = qkv[0:NS, NTP, 0:H * HD].rearrange("p (c e j d) -> p c e j d", c=2, e=2, j=GRP)
            for c in range(2):
                for e in range(2):
                    nc.gpsimd.tensor_copy(qt[:, c, :, e, :], qv[:, c, e]).then_inc(S_qt, 1)
            nc.gpsimd.memset(qbd[:], 0.0).then_inc(S_z, 1)
            pool.wait_ge(S_q, 4)
            pool.sem_inc(S_sc, START)
            with pool.Fori(0, DB) as b:
                pool.wait_ge(S_sc, b + START)
                nc.gpsimd.tensor_copy(qb[:], qbd[:, bass.ds(b, 1)].rearrange("p b c g j t -> p (b c) (g j t)")).then_inc(S_qb, 1)

        @block.tensor
        def _(pe):
            pe.wait_ge(S_qt, 4)
            for c in range(2):
                for j in range(GRP):
                    n = c * GRP + j
                    last = pe.transpose(bank[0][:, n * NS:(n + 1) * NS], qt[:, c, j, :, :].rearrange("p e d -> p (e d)"), ident[0:NS, 0:NS])
            last.then_inc(S_qps, 1)
            pe.wait_ge(S_q, 4)
            with pe.Fori(0, DB // 2) as i:
                for p in range(2):
                    b = i * 2 + p
                    pe.wait_ge(kv_in[p], (i + 1) * 64)
                    for c in range(2):
                        pe.transpose(bank[1][:, c * P:(c + 1) * P], ka[p][:, c * P:(c + 1) * P], ident[:])
                        last = pe.transpose(bank[1][:, 2 * P + c * DS:2 * P + (c + 1) * DS], kb[p][:, c * P:(c + 1) * P], ident[0:DS, 0:DS])
                    last.then_inc(S_ktps, 1)
                    pe.wait_ge(S_kt, b + 1)
                    pe.wait_ge(S_qb, b + 1)
                    for c in range(2):
                        last = pe.matmul(bank[2][:, 0:TK], qb[:, c, :], kT[:, c, :], start=(c == 0), stop=(c == 1))
                    last.then_inc(S_sc, 1)
                    pe.wait_ge(S_pr, b + 1)
                    pe.transpose(bank[3][:, 0:P], probs[:, DS:TK], ident[:])
                    pe.transpose(bank[3][0:DS, P:2 * P], probs[:, 0:DS], ident[:]).then_inc(S_ptps, 1)
                    pe.wait_ge(S_pt, b + 1)
                    pe.matmul(bank[4][:, 0:NKV], pT[:, 0:P], va[p][:], start=True, stop=False)
                    pe.matmul(bank[4][:, 0:NKV], pT[0:DS, P:2 * P], vb[p][:], start=False, stop=True).then_inc(S_ops, 1)

        @block.scalar
        def _(act):
            with act.Fori(0, DB) as b:
                act.wait_ge(S_ktps, b + 1)
                nc.scalar.copy(kT[:, :, DS:TK], bank[1][:, 0:2 * P].rearrange("p (c n) -> p c n", c=2))
                nc.scalar.copy(kT[:, :, 0:DS], bank[1][:, 2 * P:2 * P + 2 * DS].rearrange("p (c n) -> p c n", c=2)).then_inc(S_kt, 1)
                act.wait_ge(S_bias, b + 1)
                nc.scalar.activation(st[:, 3:4], snk[:], ACT.Exp, bias=st[:, 1:2])
                nc.scalar.activation(probs[:], bank[2][:, 0:TK], ACT.Exp, bias=st[:, 1:2], scale=SWA_SCALE,
                                     accum_out=st[:, 2:3]).then_inc(S_pr, 1)

        @block.vector
        def _(dve):
            ch = Chain(dve, S_dve)
            nc.vector.memset(o_tok[NS:P, NTP, :], 0.0)
            dve.sem_inc(stored[0], START)
            dve.sem_inc(stored[1], START)
            dve.wait_ge(S_z, 1)
            dve.wait_ge(S_qps, 1)
            for c in range(2):
                for e in range(2):
                    src = bank[0][e * HD:(e + 1) * HD, c * GRP * NS:(c + 1) * GRP * NS].rearrange("p (j b t) -> p b j t", j=GRP, b=DB)
                    nc.vector.tensor_copy(qbd[e * HD:(e + 1) * HD, :, c, 2 * c + e], src).then_inc(S_q, 1)
            dve.wait_ge(S_in, 32)
            with dve.Fori(0, DB // 2) as i:
                ch.round(i * 2 * PER)
                for p in range(2):
                    b = i * 2 + p
                    dve.wait_ge(S_sc, b + 1 + START)
                    sc = bank[2][:, 0:TK]
                    ch.step(nc.vector.tensor_tensor(sc, sc, mask[:], ALU.add))
                    ch.step(nc.vector.tensor_reduce(st[:, 0:1], sc, AX_X, ALU.max))
                    ch.step(nc.vector.tensor_scalar(st[:, 0:1], st[:, 0:1], SWA_SCALE, snk[:], ALU.mult, ALU.max))
                    nc.vector.tensor_scalar(st[:, 1:2], st[:, 0:1], -1.0, None, ALU.mult).then_inc(S_bias, 1)
                    dve.wait_ge(S_ptps, b + 1)
                    ch.inc(nc.vector.tensor_copy(pT[:, 0:P], bank[3][:, 0:P]))
                    nc.vector.tensor_copy(pT[0:DS, P:2 * P], bank[3][0:DS, P:2 * P]).then_inc(S_pt, 1)
                    ch.step(nc.vector.tensor_tensor(st[:, 4:5], st[:, 2:3], st[:, 3:4], ALU.add))
                    ch.step(nc.vector.reciprocal(st[:, 5:6], st[:, 4:5]))
                    dve.wait_ge(S_ops, b + 1 + START)
                    dve.wait_ge(stored[p], i * 16 + START)
                    for g in range(KVH):
                        rows = slice(g * GRP * DS, (g + 1) * GRP * DS)
                        last = nc.vector.tensor_scalar(ow[p][rows, :], bank[4][rows, g * HD:(g + 1) * HD], st[rows, 5:6], None, ALU.mult)
                    last.then_inc(S_o, 1)
                    dve.wait_ge(S_o, b + 1)
                ch.end(2 * PER)
    s.close()


def peer(nc, a, sbuf, sem, bank, x, ident, mod, stat, rstd, junk, tiles, layer):
    s = ExitStack()
    h2 = sbuf(s, f"h2_{layer}", [P, NT, D])
    best = sbuf(s, f"best{layer}", [P, NT, 2 * PH, TOPK])
    key = sbuf(s, f"key{layer}", [P, NT, 2 * PH, TOPK])
    peer_keys(nc, a, sbuf, sem, bank, x, ident, mod, stat, rstd, junk, tiles, layer, h2, best, key)
    peer_mix(nc, a, sbuf, sem, bank, x, ident, mod, layer, h2, best, key)
    s.close()


def peer_keys(nc, a, sbuf, sem, bank, x, ident, mod, stat, rstd, junk, tiles, layer, h2, best, key):
    tag = f"pk{layer}_"
    s = ExitStack()
    hs = sbuf(s, tag + "hs", [P, D])
    hT = sbuf(s, tag + "hT", [P, DC, NT * P])
    w = [sbuf(s, tag + f"w{i}", [P, DC, HALF]) for i in range(2)]
    sk = [sbuf(s, tag + f"sk{i}", [NK, HALF]) for i in range(2)]
    skT = [sbuf(s, tag + f"skT{i}", [HALF, NK]) for i in range(2)]
    qT = [sbuf(s, tag + f"qT{i}", [HALF, NT * P]) for i in range(2)]
    sc = [sbuf(s, tag + f"sc{i}", [P, NT, NK]) for i in range(2)]
    sc2 = sbuf(s, tag + "sc2", [P, NT, NK])
    bv = [sbuf(s, tag + f"bv{i}", [P, NT, TOPK]) for i in range(2)]
    bi = [sbuf(s, tag + f"bi{i}", [P, NT, TOPK], U32) for i in range(2)]
    names = "x_ss hT_ps hT_ready kept norm_step q_ps q_ready scores_ps scores_ready dve_step x_rms first added"
    S_xss, S_hTps, S_hT, S_kept, S_n, S_qps, S_q, S_sps, S_s, S_dve, S_xr, S_1, S_add = [sem(tag + n) for n in names.split()]
    w_in = [sem(tag + f"w_in{i}") for i in range(2)]
    PER = 5 * NT
    wq = a["peer_w_q"][layer].rearrange("(c p) n -> p c n", p=P)
    skeys = a["peer_sub_keys"][layer].rearrange("h s k d -> (h s) k d")
    with nc.Block() as block:
        @block.sync
        def _(sp):
            sp.sem_inc(S_sps, START)
            with sp.Fori(0, PH) as i:
                for p in range(2):
                    sp.wait_ge(S_sps, 2 * i + START)
                    sp.dma_start(w[p][:], wq[:, :, bass.ds((2 * i + p) * HALF, HALF)]).then_inc(w_in[p], 16)
                    sp.dma_start(sk[p][:], skeys[bass.ds(2 * i + p, 1)].rearrange("a k d -> (a k) d")).then_inc(w_in[p], 16)

        @block.gpsimd
        def _(pool):
            nc.gpsimd.memset(rstd[:], 0.0).then_inc(S_1, 1)

            def body(t, kind):
                wait_apart(pool, S_xss, t + 1, (S_1, 1))
                rms(nc, rstd, stat, slice(0, 1), S_add, t + 1).then_inc(S_xr, 1)
                pool.wait_ge(S_n, t * 2 + 2)
                nc.gpsimd.tensor_copy(h2[:, t, :], hs[:]).then_inc(S_kept, 1)
            tiles(pool, body)

        @block.scalar
        def _(act):
            def body(t, kind):
                nc.scalar.activation(junk[:], x[:, t, :], ACT.Square, scale=D ** -0.5,
                                     accum_out=stat[:, 0:1]).then_inc(S_xss, 1)
                for half in range(2):
                    act.wait_ge(S_hTps, 2 * t + half + 1)
                    nc.scalar.copy(hT[:, 4 * half:4 * half + 4, bass.ds(t * P, P)],
                                   bank[half][:].rearrange("p (c n) -> p c n", c=4)).then_inc(S_hT, 1)
            tiles(act, body)
            with act.Fori(0, PH) as i:
                for p in range(2):
                    act.wait_ge(S_qps, 2 * i + p + 1)
                    nc.scalar.copy(skT[p][:], bank[2][:, P:2 * P])
                    nc.scalar.copy(qT[p][:, 0:SEQ], bank[1][:])
                    nc.scalar.copy(qT[p][:, SEQ:NT * P], bank[2][:, 0:P]).then_inc(S_q, 1)
                    act.wait_ge(S_sps, 2 * i + p + 1 + START)
                    act.wait_ge(S_dve, 2 * i * PER + START)
                    nc.scalar.copy(sc[p][:, 0:NTP, :], bank[3][:].rearrange("p (t n) -> p t n", t=NTP))
                    nc.scalar.copy(sc[p][:, NTP, :], bank[4][:, 0:P]).then_inc(S_s, 1)

        @block.vector
        def _(dve):
            ch = Chain(dve, S_n)
            dve.sem_inc(S_kept, START)
            dve.sem_inc(S_hT, START)

            def body(t, kind):
                ch.round(t * 2)
                dve.wait_ge(S_xr, t + 1)
                dve.wait_ge(S_kept, t + START)
                dve.wait_ge(S_hT, 2 * t + START)
                norm_steps(nc, ch, x, mod, rstd, hs, t, kind)
                ch.end(2)
            tiles(dve, body)
            ch = Chain(dve, S_dve)
            dve.sem_inc(S_dve, START)
            with dve.Fori(0, PH) as i:
                ch.round(2 * i * PER + START)
                for p in range(2):
                    wait_apart(dve, S_s, 2 * i + p + 1 + START, (S_n, 1))

                    def each(f):
                        for t in range(NT):
                            ch.inc(f(t))
                        wait_apart(dve, S_dve, ch.base + ch.n, (S_n, 1))

                    each(lambda t: nc.vector.max(bv[p][:, t, 0:8], sc[p][:, t, :]))
                    each(lambda t: nc.vector.max_index(bi[p][:, t, 0:8], bv[p][:, t, 0:8], sc[p][:, t, :]))
                    each(lambda t: nc.vector.match_replace(sc2[:, t, :], bv[p][:, t, 0:8], sc[p][:, t, :], -3e38))
                    each(lambda t: nc.vector.max(bv[p][:, t, 8:16], sc2[:, t, :]))
                    each(lambda t: nc.vector.max_index(bi[p][:, t, 8:16], bv[p][:, t, 8:16], sc2[:, t, :]))
                    nc.vector.tensor_copy(best[:, :, bass.ds(2 * i + p, 1), :].rearrange("p t a k -> p t (a k)"), bv[p][:])
                    nc.vector.tensor_copy(key[:, :, bass.ds(2 * i + p, 1), :].rearrange("p t a k -> p t (a k)"), bi[p][:])

        @block.tensor
        def _(pe):
            def body(t, kind):
                pe.wait_ge(S_n, t * 2 + 2)
                for half in range(2):
                    for c in range(4):
                        last = pe.transpose(bank[half][:, c * P:(c + 1) * P],
                                            hs[:, (4 * half + c) * P:(4 * half + c + 1) * P], ident[:])
                    last.then_inc(S_hTps, 1)
            tiles(pe, body)
            pe.wait_ge(S_hT, 2 * NT + START)
            pe.sem_inc(S_s, START)
            with pe.Fori(0, PH) as i:
                for p in range(2):
                    pe.wait_ge(w_in[p], (i + 1) * 32)
                    pe.transpose(bank[2][:, P:2 * P], sk[p][:], ident[:])
                    for c in range(DC):
                        pe.matmul(bank[1][:], w[p][:, c, :], hT[:, c, 0:SEQ], start=(c == 0), stop=(c == DC - 1))
                    for c in range(DC):
                        last = pe.matmul(bank[2][:, 0:P], w[p][:, c, :], hT[:, c, SEQ:NT * P], start=(c == 0), stop=(c == DC - 1))
                    last.then_inc(S_qps, 1)
                    pe.wait_ge(S_q, 2 * i + p + 1)
                    pe.wait_ge(S_s, 2 * i + p + START)
                    for t in range(NT):
                        last = pe.matmul(bank[3 + t // 4][:, (t % 4) * P:(t % 4 + 1) * P], qT[p][:, t * P:(t + 1) * P], skT[p][:],
                                         start=True, stop=True)
                    last.then_inc(S_sps, 1)
    s.close()


def peer_mix(nc, a, sbuf, sem, bank, x, ident, mod, layer, h2, best, key):
    tag = f"px{layer}_"
    s = ExitStack()
    ND = 2 * RING
    ur = [sbuf(s, tag + f"u{i}", [P, D]) for i in range(RING)]
    vr = [sbuf(s, tag + f"v{i}", [P, D]) for i in range(RING)]
    diag = [sbuf(s, tag + f"d{i}", [P, P]) for i in range(ND)]
    uid = [sbuf(s, tag + f"uid{i}", [P, RING], I32) for i in range(2)]
    vid = [sbuf(s, tag + f"vid{i}", [P, RING], I32) for i in range(2)]
    experts = sbuf(s, tag + "experts", [P, NT * HK], I32)
    e = sbuf(s, tag + "e", [P, NT, HK])
    dots = sbuf(s, tag + "dots", [P, NT, HK])
    gelus = sbuf(s, tag + "gelus", [P, HK])
    coef = sbuf(s, tag + "coef", [P, HK])
    esum = sbuf(s, tag + "esum", [P, PH, 1])
    zero = sbuf(s, tag + "zero", [P, 512])
    y = sbuf(s, tag + "y", [P, D])
    cand = sbuf(s, tag + "cand", [P, TOPK, TOPK])
    cand2 = sbuf(s, tag + "cand2", [P, TOPK * TOPK])
    bv = sbuf(s, tag + "bv", [P, TOPK])
    bp = sbuf(s, tag + "bp", [P, TOPK], U32)
    bvt = sbuf(s, tag + "bvt", [P, HK])
    bpt = sbuf(s, tag + "bpt", [P, HK], U32)
    ij = sbuf(s, tag + "ij", [P, 2, HK], U32)
    ijf = sbuf(s, tag + "ijf", [P, 2, HK])
    iota = sbuf(s, tag + "iota", [P, 1, TOPK])
    hot = sbuf(s, tag + "hot", [P, HK, TOPK])
    num = sbuf(s, tag + "num", [P, 2, HK])
    u_in = [sem(tag + f"u_in{i}") for i in range(RING)]
    v_in = [sem(tag + f"v_in{i}") for i in range(RING)]
    names = "zeroed u_free v_free uid_ready vid_ready gelu coef diag_ready out_ps out_step experts_ready rank_step iota_in shifted exp_ready gate_step"
    (S_z, S_uf, S_vf, S_uid, S_vid, S_g, S_c, S_d, S_ops, S_out, S_ex, S_rank, S_in, S_sub, S_exp, S_gate) = [
        sem(tag + n) for n in names.split()]
    u_tab, v_tab = a["peer_u"].rearrange("l e d -> (l e) d"), a["peer_v"].rearrange("l e d -> (l e) d")
    offset = bass.IndirectOffsetOnAxis
    OUT_FREE = 2 * 3
    HEAD, PER = 8, 8 * PH + 2 + 1 + 2 * 3 + 1
    bestv = best[:].rearrange("p t h k -> p (t h) k")
    with nc.Block() as block:
        @block.sync
        def _(sp):
            sp.dma_start(iota[:], a["k_iota"]).then_inc(S_in, 16)

        @block.gpsimd
        def _(pool):
            nc.gpsimd.memset(zero[:], 0.0).then_inc(S_z, 1)
            nc.gpsimd.memset(y[:], 0.0).then_inc(S_vf, ND)

            def fetch(table, ring, ids, ready, free, spare, landed, it, odd, rows):
                nc.gpsimd.tensor_copy(ids[odd][0:rows, :], experts[0:rows, bass.ds(it * RING, RING)]).then_inc(ready, 1)
                wait_apart(pool, ready, it + 1, (S_z, 1))
                for r in range(RING):
                    wait_apart(pool, free, it * RING + r + 1 + spare, (S_z, 1))
                    pool.indirect_dma_start(ring[r][0:rows, :], None, table,
                                            offset(ap=ids[odd][0:rows, r:r + 1], axis=0)).then_inc(landed[r], 16)

            def u_rows(it, odd, rows=P):
                fetch(u_tab, ur, uid, S_uid, S_uf, 0, u_in, it, odd, rows)

            def v_rows(it, odd, rows=P):
                fetch(v_tab, vr, vid, S_vid, S_vf, ND - RING, v_in, it, odd, rows)

            def rounds(first, last, u=None, v=None):
                with pool.Fori(first // 2, last // 2) as i:
                    for odd in range(2):
                        if u:
                            u_rows(2 * i + odd, odd, u)
                        if v:
                            v_rows(2 * i + odd - BEHIND, odd, v)

            BEHIND = SLOTS + LAG
            pool.wait_ge(S_ex, 1)
            rounds(0, SLOTS, u=P)
            pool.wait_ge(S_ex, 2)
            rounds(SLOTS, BEHIND, u=P)
            rounds(BEHIND, 2 * SLOTS, u=P, v=P)
            for t in range(2, NTP):
                pool.wait_ge(S_ex, t + 1)
                rounds(t * SLOTS, (t + 1) * SLOTS, u=P, v=P)
            pool.wait_ge(S_ex, NT)
            rounds(NTP * SLOTS, NT * SLOTS, u=NS, v=P)
            rounds(NT * SLOTS, NTP * SLOTS + BEHIND, v=P)
            rounds(NTP * SLOTS + BEHIND, NT * SLOTS + BEHIND, v=NS)

        @block.vector
        def _(dve):
            nc.vector.memset(coef[:], 0.0).then_inc(S_uf, RING)
            dve.sem_inc(S_d, START)
            dve.wait_ge(S_in, 16)
            ch = Chain(dve, S_rank)

            def dot(t, j, rows):
                for r in range(RING):
                    dve.wait_ge(u_in[r], (t * SLOTS + j + 1) * 16)
                    nc.vector.scalar_tensor_tensor(out=ur[r][0:rows, :], in0=ur[r][0:rows, :], scalar=1.0, in1=h2[0:rows, t, :],
                                                   op0=ALU.mult, op1=ALU.mult,
                                                   accum_out=dots[0:rows, t, bass.ds(j * RING + r, 1)]).then_inc(S_uf, 1)

            def rank_head(t, hd):
                ch.round(t * PER + hd * HEAD)
                first = lambda half: bestv[:, bass.ds(t * 2 * PH + hd * 2 + half, 1), :].rearrange("p a k -> p (a k)")
                def ranked(ins):
                    ch.inc(ins)
                    wait_apart(dve, S_rank, ch.base + ch.n, (S_in, 16))
                ranked(nc.vector.tensor_tensor(cand[:], first(0).unsqueeze(2).to_broadcast([P, TOPK, TOPK]),
                                               first(1).unsqueeze(1).to_broadcast([P, TOPK, TOPK]), ALU.add))
                flat = cand[:].rearrange("p i j -> p (i j)")
                ranked(nc.vector.max(bv[:, 0:8], flat))
                ranked(nc.vector.max_index(bp[:, 0:8], bv[:, 0:8], flat))
                ranked(nc.vector.match_replace(cand2[:], bv[:, 0:8], flat, -3e38))
                ranked(nc.vector.max(bv[:, 8:16], cand2[:]))
                ranked(nc.vector.max_index(bp[:, 8:16], bv[:, 8:16], cand2[:]))
                ch.inc(nc.vector.tensor_copy(bvt[:, bass.ds(hd * TOPK, TOPK)], bv[:]))
                ch.step(nc.vector.tensor_copy(bpt[:, bass.ds(hd * TOPK, TOPK)], bp[:]))

            def key_numbers(t, half):
                if half == 0:
                    ch.round(t * PER + PH * HEAD)
                    ch.inc(nc.vector.tensor_scalar(ij[:, 0, :], bpt[:], 4, None, ALU.logical_shift_right))
                    ch.step(nc.vector.tensor_scalar(ij[:, 1, :], bpt[:], TOPK - 1, None, ALU.bitwise_and))
                    ch.step(nc.vector.tensor_copy(ijf[:], ij[:]))
                kt = key[:, bass.ds(t, 1)].rearrange("p a (h s) k -> p (a h) s k", s=2)
                pos = ijf[:, half, :].unsqueeze(2).to_broadcast([P, HK, TOPK])
                hotv = hot[:].rearrange("p (h k) i -> p h k i", h=PH)
                ch.step(nc.vector.tensor_tensor(hot[:], pos, iota[:].to_broadcast([P, HK, TOPK]), ALU.is_equal))
                ch.step(nc.vector.tensor_tensor(hotv, hotv, kt[:, :, half, :].unsqueeze(2).to_broadcast([P, PH, TOPK, TOPK]), ALU.mult))
                ch.step(nc.vector.tensor_reduce(num[:, half, :], hot[:], AX_X, ALU.add))

            def number(t):
                bt = bvt[:].rearrange("p (h k) -> p h k", h=PH)
                nc.vector.tensor_tensor(e[:, t, :].rearrange("p (h k) -> p h k", h=PH), bt,
                                        bt[:, :, 0:1].to_broadcast([P, PH, TOPK]), ALU.subtract).then_inc(S_sub, 1)
                ch.step(nc.vector.scalar_tensor_tensor(out=num[:, 0, :], in0=num[:, 0, :], scalar=float(NK), in1=num[:, 1, :],
                                                       op0=ALU.mult, op1=ALU.add))
                assert ch.n == PER - PH * HEAD
                nc.vector.tensor_scalar(experts[:, bass.ds(t * HK, HK)], num[:, 0, :], float(layer * NK * NK), None, ALU.add).then_inc(S_ex, 1)

            def gate(t, rows):
                ev = e[:, t, :].rearrange("p (h k) -> p h k", h=PH)
                dve.wait_ge(S_exp, t + 1)
                nc.vector.tensor_reduce(esum[:, :, 0], ev, AX_X, ALU.add).then_inc(S_gate, 1)
                dve.wait_ge(S_gate, t * 3 + 1)
                nc.vector.reciprocal(esum[:], esum[:]).then_inc(S_gate, 1)
                dve.wait_ge(S_gate, t * 3 + 2)
                nc.vector.tensor_tensor(ev, ev, esum[:].to_broadcast([P, PH, TOPK]), ALU.mult).then_inc(S_gate, 1)
                dve.wait_ge(S_gate, t * 3 + 3)
                dve.wait_ge(S_g, t + 1)
                dve.wait_ge(S_d, t * HK + START)
                nc.vector.tensor_tensor(coef[0:rows, :], gelus[0:rows, :], e[0:rows, t, :], ALU.mult).then_inc(S_c, 1)

            def add(t, kind, rows, banks):
                dve.wait_ge(S_ops, t + 1)
                for n in range(2):
                    nc.vector.tensor_tensor(y[0:rows, n * 512:(n + 1) * 512], bank[banks + n][0:rows, :],
                                            mod[0:rows, kind, 2 * D + n * 512:2 * D + (n + 1) * 512], ALU.mult).then_inc(S_out, 1)
                dve.wait_ge(S_out, 3 * t + 2 + OUT_FREE)
                nc.vector.tensor_tensor(x[0:rows, t, :], x[0:rows, t, :], y[0:rows, :], ALU.add).then_inc(S_out, 1)
                dve.wait_ge(S_out, 3 * t + 3 + OUT_FREE)

            def rank_tile(t):
                with dve.Fori(0, PH) as hd:
                    rank_head(t, hd)
                key_numbers(t, 0)
                key_numbers(t, 1)
                number(t)

            def tile(t, rows, parity, gated, added, ranked):
                dot(t, 0, rows)
                if gated:
                    gate(t - 1, P)
                with dve.Fori(0, PH) as hd:
                    dot(t, hd + 1, rows)
                    if ranked:
                        rank_head(t + 1, hd)
                dot(t, PH + 1, rows)
                if added:
                    add(t - 2, 0, P, 2 * parity)
                if ranked:
                    key_numbers(t + 1, 0)
                dot(t, PH + 2, rows)
                if ranked:
                    key_numbers(t + 1, 1)
                dot(t, PH + 3, rows)
                if ranked:
                    number(t + 1)
                with dve.Fori(PH + 4, SLOTS) as j:
                    dot(t, j, rows)

            rank_tile(0)
            tile(0, P, 0, False, False, True)
            tile(1, P, 1, True, False, True)
            for t in range(2, NTP):
                tile(t, P, t % 2, True, True, True)
            tile(NTP, NS, 0, True, True, False)
            gate(NTP, NS)
            add(NTP - 1, 0, P, 2)
            add(NTP, 1, NS, 0)

        @block.scalar
        def _(act):
            def exps(t):
                act.wait_ge(S_sub, t + 1)
                nc.scalar.activation(e[:, t, :], e[:, t, :], ACT.Exp).then_inc(S_exp, 1)

            def gelu(t, rows):
                act.wait_ge(S_uf, (t + 1) * HK + RING)
                nc.scalar.activation(gelus[0:rows, :], dots[0:rows, t, :], ACT.Gelu).then_inc(S_g, 1)

            def diagonals(t, rows):
                act.wait_ge(S_c, t + 1)
                with act.Fori(0, HK // ND) as j:
                    for r in range(ND):
                        wait_apart(act, S_vf, t * HK + j * ND + r + 1, (S_z, 1))
                        nc.scalar.activation(diag[r][0:rows, 0:rows], ident[0:rows, 0:rows], ACT.Copy,
                                             scale=coef[0:rows, bass.ds(j * ND + r, 1)]).then_inc(S_d, 1)

            exps(0)
            with act.Fori(0, NTP) as t:
                exps(t + 1)
                gelu(t, P)
                diagonals(t, P)
            gelu(NTP, NS)
            diagonals(NTP, NS)

        @block.tensor
        def _(pe):
            pe.wait_ge(S_z, 1)
            pe.sem_inc(S_out, OUT_FREE)

            def mix(t, rows, banks):
                lo, hi = bank[banks], bank[banks + 1]
                pe.wait_ge(S_out, 3 * t + OUT_FREE - 3)
                for b in (lo, hi):
                    pe.matmul(b[0:rows, :], zero[:, 0:rows], zero[:], start=True, stop=False)
                with pe.Fori(0, HK // ND) as j:
                    for r in range(ND):
                        v = r % RING
                        d_at = t * HK + j * ND + r + 1 + START
                        v_at = (t * SLOTS + j * (ND // RING) + r // RING + 1) * 16
                        if not isinstance(t, int) or rows < P:
                            d_at, v_at = pe.to_reg(d_at), pe.to_reg(v_at)
                        pe.wait_ge(S_z, 1)
                        pe.wait_ge(S_d, d_at)
                        pe.wait_ge(v_in[v], v_at)
                        pe.matmul(lo[0:rows, :], diag[r][0:rows, 0:rows], vr[v][0:rows, 0:512], start=False, stop=False)
                        pe.matmul(hi[0:rows, :], diag[r][0:rows, 0:rows], vr[v][0:rows, 512:D], start=False, stop=False).then_inc(S_vf, 1)
                for b in (lo, hi):
                    last = pe.matmul(b[0:rows, :], zero[:, 0:rows], zero[:], start=False, stop=True)
                last.then_inc(S_ops, 1)

            with pe.Fori(0, NTP, 2) as t:
                mix(t, P, 0)
                mix(t + 1, P, 2)
            mix(NTP, NS, 0)
    s.close()


def final_norm(nc, a, o, sbuf, sem, x, stat, rstd, junk, tiles):
    s = ExitStack()
    g = sbuf(s, "fn_g", [P, D])
    y = [sbuf(s, f"fn_y{i}", [P, D]) for i in range(2)]
    S_in, S_ss, S_r, S_dve, S_st, S_add = [sem("fn_" + n) for n in "gain_in x_ss x_rms dve_step stored added".split()]
    with nc.Block() as block:
        @block.sync
        def _(sp):
            sp.dma_start(g[:], a["final_g"].rearrange("(a d) -> a d", a=1).to_broadcast([P, D])).then_inc(S_in, 16)
            for t in range(NT):
                sp.wait_ge(S_dve, t + 1)
                if t < NTP:
                    sp.dma_start(o["y_p"][0, t * P:(t + 1) * P, :], y[t % 2][:]).then_inc(S_st, 16)
                else:
                    sp.dma_start(o["y_s"].rearrange("b t d -> (b t) d"), y[t % 2][0:NS, :]).then_inc(S_st, 16)
                sp.wait_ge(S_st, 16 * (t + 1))

        @block.scalar
        def _(act):
            for t in range(NT):
                act.wait_ge(S_r, t)
                nc.scalar.activation(junk[:], x[:, t, :], ACT.Square, scale=D ** -0.5, accum_out=stat[:, 0:1]).then_inc(S_ss, 1)

        @block.gpsimd
        def _(pool):
            for t in range(NT):
                pool.wait_ge(S_ss, t + 1)
                pool.wait_ge(S_dve, t)
                rms(nc, rstd, stat, slice(0, 1), S_add, t + 1).then_inc(S_r, 1)

        @block.vector
        def _(dve):
            dve.wait_ge(S_in, 16)
            for t in range(NT):
                dve.wait_ge(S_r, t + 1)
                if t >= 2:
                    dve.wait_ge(S_st, 16 * (t - 1))
                nc.vector.scalar_tensor_tensor(out=y[t % 2][:], in0=x[:, t, :], scalar=rstd[:, 0:1], in1=g[:],
                                               op0=ALU.mult, op1=ALU.mult).then_inc(S_dve, 1)
    s.close()


def constants():
    f = np.float32
    c = {"k_ident": np.eye(P, dtype=f), "k_iota": np.tile(np.arange(TOPK, dtype=f), (P, 1)).reshape(P, 1, TOPK)}
    r = np.arange(P)
    sel = np.zeros((DB + 1, 2, P), f)
    sel[0, 0, :] = 1
    for b in range(DB):
        sel[1 + b, 1, b * DS:(b + 1) * DS] = 1
    c["k_sel"] = sel
    c["k_causal"] = np.where(r[None, :] <= r[:, None], 0, NEG).astype(f)
    c["k_band"] = np.concatenate([np.where(r[None, :] > r[:, None], 0, NEG), c["k_causal"]], axis=1).astype(f)
    step = (r % DS)[:, None, None]
    new = np.arange(NS)[None, None, :]
    c["k_mask_new"] = np.where((new // DS == np.arange(DB)[None, :, None]) & (new % DS <= step), 0, NEG).astype(f)
    j = np.arange(P + DS)[None, :]
    t = (r % DS)[:, None]
    c["k_mask_win"] = np.where((j <= P + t) & (j > t), 0, NEG).astype(f)
    pos = np.concatenate([np.arange(SEQ), PAST + r % DS]).astype(f)
    for n in (ROPE, ROT):
        half = n // 2
        e = (-np.arange(half, dtype=f) * f(2.0) / f(n)).astype(np.float64)
        inv = np.power(500000.0, e).astype(f)
        ang = (pos[:, None] * inv[None, :]).astype(f).astype(np.float64)
        cos, sin = np.cos(ang).astype(f), np.sin(ang).astype(f)
        lay = lambda v: np.ascontiguousarray(v.reshape(NT, P, n).transpose(1, 0, 2))
        c[f"k_cos{n}"] = lay(np.concatenate([cos, cos], 1))
        c[f"k_sin{n}"] = lay(np.concatenate([-sin, sin], 1))
    return c


_INS = ['x_prompt', 'x_sample', 'cache_mla_ckv', 'cache_mla_kpe', 'cache_swa_k', 'cache_swa_v', 'page_table',
        'c_prompt', 'c_sample', 'ln1_g', 'ln2_g', 'w_mod', 'b_mod', 'mla_w_in', 'mla_q_norm', 'mla_kv_norm',
        'mla_w_uq', 'mla_w_uk', 'mla_w_uv', 'mla_w_o', 'swa_w_qkv', 'swa_b_qkv', 'swa_sinks', 'swa_w_o',
        'peer_w_q', 'peer_sub_keys', 'peer_u', 'peer_v', 'final_g']
_OUTS = [('y_p', (1, SEQ, D)), ('y_s', (DB, DS, D)), ('ckv_p', (1, 1, SEQ, KL)), ('kpe_p', (1, 1, SEQ, ROPE)),
         ('ckv_s', (1, DB, DS, KL)), ('kpe_s', (1, DB, DS, ROPE)), ('swk_p', (1, 1, P, KVH, HD)),
         ('swv_p', (1, 1, P, KVH, HD)), ('swk_s', (1, DB, P, KVH, HD)), ('swv_s', (1, DB, P, KVH, HD))]


def kernel(**inputs):
    import concourse.bacc as _bacc
    from concourse.bass_utils import run_bass_kernel_spmd as _run

    nc = _bacc.Bacc("TRN2", target_bir_lowering=False, num_devices=1)
    arrays = {name: np.ascontiguousarray(inputs[name]) for name in _INS}
    arrays.update(constants())
    args = {name: nc.dram_tensor(f"in_{name}", v.shape, mybir.dt.from_np(v.dtype), kind="ExternalInput").ap()
            for name, v in arrays.items()}
    outs = {name: nc.dram_tensor(f"out_{name}", shape, F32, kind="ExternalOutput").ap() for name, shape in _OUTS}
    build(nc, args, outs)
    r = _run(nc, [{f"in_{name}": v for name, v in arrays.items()}], core_ids=[0])
    return tuple(r.results[0][f"out_{name}"] for name, _ in _OUTS)
```

```python
from contextlib import ExitStack

import numpy as np

import concourse.bass as bass
from concourse import mybir

ALU = mybir.AluOpType
ACT = mybir.ActivationFunctionType
F32 = mybir.dt.float32
I32 = mybir.dt.int32
U32 = mybir.dt.uint32
AX_X = mybir.AxisListType.X

P = 128
D = 1024
DC = D // P
SEQ = 512
NTP = SEQ // P
NT = NTP + 1
DB = 8
DS = 8
NS = DB * DS
PAST = 4096
PAGE = 128
NPG = PAST // PAGE
EPS = 1e-6
NEG = -1e30
H = 16
QL, KL, NOPE, ROPE = 384, 256, 64, 32
QH = NOPE + ROPE
MLA_SCALE = float(QH) ** -0.5
HD = 64
KVH = 4
GRP = H // KVH
ROT = HD // 4
SWA_SCALE = float(HD) ** -0.5
SWA_N = (H + 2 * KVH) * HD
PH, NK, TOPK, HALF = 8, 128, 16, 128
HK = PH * TOPK
GP = 4
NG = NPG // GP
RING = 8
SLOTS = HK // RING
PAIRED = HK // 2
HEAD = 8
LAG = 2


START = 1


class Chain:

    def __init__(self, eng, done):
        self.eng, self.done, self.base, self.n = eng, done, 0, 0

    def round(self, base):
        self.base, self.n = base, 0

    def step(self, ins):
        ins.then_inc(self.done, 1)
        self.n += 1
        self.eng.wait_ge(self.done, self.base + self.n)

    def inc(self, ins):
        ins.then_inc(self.done, 1)
        self.n += 1

    def end(self, per):
        assert self.n == per, (self.n, per)
        self.eng.wait_ge(self.done, self.base + self.n)


def wait_apart(eng, sem, value, settled):
    if not isinstance(value, int):
        value = eng.to_reg(value)
    eng.wait_ge(*settled)
    eng.wait_ge(sem, value)


def build(nc, a, o):
    with ExitStack() as ctx:
        def sbuf(stack, name, shape, dt=F32):
            return stack.enter_context(nc.sbuf_tensor(name, shape, dt))

        live = []

        def sem(name):
            live.append(nc.alloc_semaphore(name=name))
            return live[-1]

        def renew_semaphores():
            with nc.Block() as block:
                @block.gpsimd
                def _(pool):
                    numbers = sorted(s.num for s in live)
                    first = numbers[0]
                    for n, nxt in zip(numbers, numbers[1:] + [None]):
                        if nxt != n + 1:
                            pool.sem_clear(range(first, n + 1))
                            first = nxt
            for s in live:
                nc.release_semaphore(s)
            live.clear()

        sb = lambda name, shape, dt=F32: sbuf(ctx, name, shape, dt)
        bank = [ctx.enter_context(nc.psum_tensor(f"bank{i}", [P, 512], F32)) for i in range(8)]

        x = sb("x", [P, NT, D])
        ident = sb("ident", [P, P])
        sel = sb("sel", [DB + 1, 2, P])
        cT = sb("cT", [P, DC, DB + 1])
        mod = sb("mod", [P, 2, 3 * D])
        stat = sb("stat", [P, 6])
        rstd = sb("rstd", [P, 4])
        junk = sb("junk", [P, D])

        def tiles(eng, body):
            with eng.Fori(0, NTP) as t:
                body(t, 0)
            body(NTP, 1)

        scratch = nc.dram_tensor("swa_scratch", (DB, DS, H, HD), F32).ap()
        mod_rows = nc.dram_tensor("mod_rows", (DB + 1, 6 * D), F32).ap()
        setup(nc, a, sbuf, sem, bank, x, ident, sel, cT, stat)
        modulation(nc, a, sbuf, sem, bank, cT, sel, mod, 0, 0)
        mla(nc, a, o, sbuf, sem, bank, x, ident, mod, stat, rstd, junk, tiles)
        modulation(nc, a, sbuf, sem, bank, cT, sel, mod, 0, 1)
        peer(nc, a, sbuf, sem, bank, x, ident, mod, stat, rstd, junk, tiles, 0,
             ahead=(cT, mod_rows))
        renew_semaphores()
        modulation_from_rows(nc, a, sbuf, sem, mod, mod_rows, 1, 0)
        swa(nc, a, o, scratch, sbuf, sem, bank, x, ident, mod, stat, rstd, junk, tiles)
        modulation_from_rows(nc, a, sbuf, sem, mod, mod_rows, 1, 1)
        peer(nc, a, sbuf, sem, bank, x, ident, mod, stat, rstd, junk, tiles, 1)
        final_norm(nc, a, o, sbuf, sem, x, stat, rstd, junk, tiles)


def setup(nc, a, sbuf, sem, bank, x, ident, sel, cT, stat):
    s = ExitStack()
    c9 = sbuf(s, "c9", [DB + 1, D])
    e9 = sbuf(s, "e9", [DB + 1, D])
    loaded, zeroed, c_in = sem("su_loaded"), sem("su_zeroed"), sem("su_c_in")
    e_done, silu_done, cT_ps, cT_done = sem("su_e"), sem("su_silu"), sem("su_cT_ps"), sem("su_cT")
    with nc.Block() as block:
        @block.sync
        def _(sp):
            sp.dma_start(c9[0:1, :], a["c_prompt"]).then_inc(c_in, 16)
            sp.dma_start(c9[1:DB + 1, :], a["c_sample"]).then_inc(c_in, 16)
            sp.dma_start(ident[:], a["k_ident"]).then_inc(c_in, 16)
            sp.dma_start(sel[:], a["k_sel"]).then_inc(loaded, 16)
            sp.dma_start(x[:, 0:NTP, :], a["x_prompt"].rearrange("b (t p) d -> p (b t) d", p=P)).then_inc(loaded, 16)
            sp.wait_ge(zeroed, 1)
            sp.dma_start(x[0:NS, NTP, :], a["x_sample"].rearrange("b t d -> (b t) d")).then_inc(loaded, 16)
            sp.wait_ge(loaded, 48)

        @block.scalar
        def _(act):
            act.wait_ge(c_in, 48)
            nc.scalar.activation(e9[:], c9[:], ACT.Exp, scale=-1.0).then_inc(e_done, 1)
            act.wait_ge(cT_ps, 1)
            nc.scalar.copy(cT[:], bank[0][:, 0:DC * (DB + 1)].rearrange("p (c n) -> p c n", c=DC)).then_inc(cT_done, 1)

        @block.vector
        def _(dve):
            ch = Chain(dve, silu_done)
            nc.vector.memset(x[:, NTP, :], 0.0).then_inc(zeroed, 1)
            nc.vector.memset(stat[:, 3:4], EPS)
            nc.vector.memset(stat[:, 4:6], -0.5)
            dve.wait_ge(e_done, 1)
            ch.step(nc.vector.tensor_scalar(e9[:], e9[:], 1.0, None, ALU.add))
            ch.step(nc.vector.reciprocal(e9[:], e9[:]))
            ch.inc(nc.vector.tensor_tensor(c9[:], c9[:], e9[:], ALU.mult))

        @block.tensor
        def _(pe):
            pe.wait_ge(silu_done, 3)
            for c in range(DC):
                last = pe.transpose(bank[0][:, c * (DB + 1):(c + 1) * (DB + 1)], c9[:, c * P:(c + 1) * P],
                                    ident[0:DB + 1, 0:DB + 1])
            last.then_inc(cT_ps, 1)
    s.close()


def modulation(nc, a, sbuf, sem, bank, cT, sel, mod, layer, sub):
    tag = f"m{layer}{sub}_"
    NCH = 3 * D // 512
    s = ExitStack()
    w = [sbuf(s, tag + f"w{i}", [P, DC, 512]) for i in range(2)]
    bias = sbuf(s, tag + "bias", [DB + 1, 3 * D])
    gain = sbuf(s, tag + "gain", [DB + 1, D])
    rows = sbuf(s, tag + "rows", [DB + 1, 3 * D])
    w_in = [sem(tag + f"w_in{i}") for i in range(2)]
    vec_in, row_ps, row_done, scaled = sem(tag + "vec_in"), sem(tag + "row_ps"), sem(tag + "row"), sem(tag + "scaled")
    wide_ps, wide_act, wide_dve = sem(tag + "wide_ps"), sem(tag + "wide_act"), sem(tag + "wide_dve")
    w_src = a["w_mod"][layer][:, sub * 3 * D:(sub + 1) * 3 * D].rearrange("(c p) n -> p c n", p=P)
    g_src = a["ln1_g" if sub == 0 else "ln2_g"][layer:layer + 1, :]
    with nc.Block() as block:
        @block.sync
        def _(sp):
            sp.dma_start(bias[:], a["b_mod"][layer:layer + 1, sub * 3 * D:(sub + 1) * 3 * D].to_broadcast([DB + 1, 3 * D])).then_inc(vec_in, 16)
            sp.dma_start(gain[:], g_src.to_broadcast([DB + 1, D])).then_inc(vec_in, 16)
            for n in range(NCH):
                if n >= 2:
                    sp.wait_ge(row_ps, n - 1)
                sp.dma_start(w[n % 2][:], w_src[:, :, n * 512:(n + 1) * 512]).then_inc(w_in[n % 2], 16)

        @block.tensor
        def _(pe):
            for n in range(NCH):
                pe.wait_ge(w_in[n % 2], 16 * (n // 2 + 1))
                if n >= 2:
                    pe.wait_ge(row_done, n - 1)
                for c in range(DC):
                    last = pe.matmul(bank[n % 2][0:DB + 1, :], cT[:, c, :], w[n % 2][:, c, :],
                                     start=(c == 0), stop=(c == DC - 1))
                last.then_inc(row_ps, 1)
            pe.wait_ge(scaled, 1)
            for kind in range(2):
                for n in range(NCH):
                    if kind:
                        pe.wait_ge(wide_act if n % 2 else wide_dve, n // 2 + 1)
                    pe.matmul(bank[2 + n][:, :], sel[:, kind, :], rows[:, n * 512:(n + 1) * 512],
                              start=True, stop=True).then_inc(wide_ps, 1)

        def widen(eng, copy, done, odd):
            for kind in range(2):
                for n in range(odd, NCH, 2):
                    eng.wait_ge(wide_ps, kind * NCH + n + 1)
                    copy(mod[:, kind, n * 512:(n + 1) * 512], bank[2 + n][:, :]).then_inc(done, 1)

        @block.vector
        def _(dve):
            dve.wait_ge(vec_in, 32)
            for n in range(NCH):
                dve.wait_ge(row_ps, n + 1)
                part = slice(n * 512, (n + 1) * 512)
                nc.vector.tensor_tensor(rows[:, part], bank[n % 2][0:DB + 1, :], bias[:, part],
                                        ALU.add).then_inc(row_done, 1)
            dve.wait_ge(row_done, NCH)
            nc.vector.scalar_tensor_tensor(out=rows[:, D:2 * D], in0=rows[:, D:2 * D], scalar=1.0, in1=gain[:],
                                           op0=ALU.add, op1=ALU.mult).then_inc(scaled, 1)
            widen(dve, nc.vector.tensor_copy, wide_dve, 0)

        @block.scalar
        def _(act):
            widen(act, nc.scalar.copy, wide_act, 1)
    s.close()


def modulation_from_rows(nc, a, sbuf, sem, mod, mod_rows, layer, sub):
    tag = f"n{layer}{sub}_"
    s = ExitStack()
    bias = sbuf(s, tag + "bias", [P, 3 * D])
    gain = sbuf(s, tag + "gain", [P, D])
    part_in = [sem(tag + f"part_in{i}") for i in range(3)]
    biased, done = sem(tag + "biased"), sem(tag + "done")
    g_src = a["ln1_g" if sub == 0 else "ln2_g"][layer:layer + 1, :]
    SENT = [16 * 4, 16 * 5, 16 * 4]
    with nc.Block() as block:
        @block.sync
        def _(sp):
            for n in range(3):
                cols = slice(n * D, (n + 1) * D)
                src = slice((3 * sub + n) * D, (3 * sub + n + 1) * D)
                sp.dma_start(bias[:, cols], a["b_mod"][layer:layer + 1, src].to_broadcast([P, D])).then_inc(part_in[n], 16)
                sp.dma_start(mod[:, 0, cols], mod_rows[0:1, src].to_broadcast([P, D])).then_inc(part_in[n], 16)
                for half in range(2):
                    sp.dma_start(mod[half * NS:(half + 1) * NS, 1, cols],
                                 mod_rows[1:DB + 1, src].unsqueeze(1).to_broadcast([DB, DS, D])).then_inc(part_in[n], 16)
                if n == 1:
                    sp.dma_start(gain[:], g_src.to_broadcast([P, D])).then_inc(part_in[n], 16)

        @block.vector
        def _(dve):
            for n in range(3):
                cols = slice(n * D, (n + 1) * D)
                dve.wait_ge(part_in[n], SENT[n])
                for kind in range(2):
                    nc.vector.tensor_tensor(mod[:, kind, cols], mod[:, kind, cols], bias[:, cols], ALU.add).then_inc(biased, 1)
            dve.wait_ge(biased, 4)
            for kind in range(2):
                nc.vector.scalar_tensor_tensor(out=mod[:, kind, D:2 * D], in0=mod[:, kind, D:2 * D], scalar=1.0, in1=gain[:],
                                               op0=ALU.add, op1=ALU.mult).then_inc(done, 1)
    s.close()


def rms(nc, rstd, stat, cols, added, count):
    n = cols.stop - cols.start
    nc.gpsimd.tensor_tensor(rstd[:, cols], stat[:, cols], stat[:, 3:4].to_broadcast([P, n]), ALU.add).then_inc(added, 1)
    nc.gpsimd.wait_ge(added, count)
    return nc.gpsimd.tensor_tensor(rstd[:, cols], rstd[:, cols], stat[:, 4:4 + n], ALU.pow)


def squares_of_tiles(nc, x, junk, squares, done):
    for t in range(NT):
        if t:
            nc.scalar.wait_ge(done, t)
        nc.scalar.activation(junk[:], x[:, t, :], ACT.Square, scale=D ** -0.5, accum_out=squares[:, t:t + 1]).then_inc(done, 1)


def rms_of_tiles(nc, rms_inv, squares, stat, squared, added, done):
    nc.gpsimd.wait_ge(squared, NT)
    nc.gpsimd.tensor_tensor(rms_inv[:], squares[:], stat[:, 3:4].to_broadcast([P, NT]), ALU.add).then_inc(added, 1)
    nc.gpsimd.wait_ge(added, 1)
    nc.gpsimd.tensor_tensor(rms_inv[:], rms_inv[:], stat[:, 4:5].to_broadcast([P, NT]), ALU.pow).then_inc(done, 1)


def norm_steps(nc, ch, x, mod, rstd, h, t, kind):
    ch.step(nc.vector.scalar_tensor_tensor(out=h[:], in0=x[:, t, :], scalar=rstd[:, 0:1], in1=mod[:, kind, D:2 * D],
                                           op0=ALU.mult, op1=ALU.mult))
    ch.step(nc.vector.tensor_tensor(h[:], h[:], mod[:, kind, 0:D], ALU.add))


def mla(nc, a, o, sbuf, sem, bank, x, ident, mod, stat, rstd, junk, tiles):
    s = ExitStack()
    ckv = sbuf(s, "ckv", [P, NT, KL])
    ckvT = sbuf(s, "ckvT", [P, 2, NT * P])
    kpe = sbuf(s, "kpe", [P, NT, ROPE])
    o_tok = sbuf(s, "o_tok", [P, NT, D])
    wuk = sbuf(s, "wuk", [P, 2, H * NOPE])
    wuv = sbuf(s, "wuv", [P, 2, H * HD])
    kT = sbuf(s, "kT", [QH, NT * P])
    qlT = sbuf(s, "qlT", [P, 2, DB, P])
    qpT = sbuf(s, "qpT", [ROPE, DB, P])
    kpeT = sbuf(s, "kpeT", [ROPE, NS])
    s1 = ExitStack()
    q = sbuf(s1, "q", [P, NT, H * QH])
    mla_project(nc, a, o, sbuf, sem, bank, x, ident, mod, stat, rstd, junk, tiles, q, ckv, ckvT, kpe, kT, wuk, wuv)
    mla_prompt(nc, a, sbuf, sem, bank, ident, q, ckvT, kT, wuk, wuv, o_tok)
    mla_sample_queries(nc, sbuf, sem, bank, ident, q, kpe, wuk, qlT, qpT, kpeT)
    s1.close()
    mla_sample(nc, a, sbuf, sem, bank, ident, ckv, ckvT, kpeT, qlT, qpT, wuv, o_tok)
    project_out(nc, a["mla_w_o"][0], "mo_", sbuf, sem, bank, x, ident, mod, junk, tiles, o_tok)
    s.close()


def mla_project(nc, a, o, sbuf, sem, bank, x, ident, mod, stat, rstd, junk, tiles, q, ckv, ckvT, kpe, kT, wuk, wuv):
    s = ExitStack()
    ZN = QL + KL + ROPE
    w_in = sbuf(s, "mp_w_in", [P, DC, ZN])
    w_uq = sbuf(s, "mp_w_uq", [P, QL // P, H * QH])
    qn = sbuf(s, "mp_qn", [P, QL])
    kvn = sbuf(s, "mp_kvn", [P, KL])
    cos = sbuf(s, "mp_cos", [P, NT, ROPE])
    sin = sbuf(s, "mp_sin", [P, NT, ROPE])
    h = sbuf(s, "mp_h", [P, D])
    squares = sbuf(s, "mp_squares", [P, NT])
    rms_inv = sbuf(s, "mp_rms_inv", [P, NT])
    hT = sbuf(s, "mp_hT", [P, DC, P])
    cq = sbuf(s, "mp_cq", [P, QL])
    cqT = sbuf(s, "mp_cqT", [P, QL // P, P])
    ks = sbuf(s, "mp_ks", [P, KL])
    kp96 = sbuf(s, "mp_kp96", [P, QH])
    ta = sbuf(s, "mp_ta", [P, H, ROPE])
    tb = sbuf(s, "mp_tb", [P, H, ROPE])
    names = "w_in vec_in x_ss h_ready hT_ps hT_ready z_ps z_ss latT_ps latT_ready q_ps q_copied dve_step stored later kept x_rms z_rms first added rms_step"
    (S_w, S_vec, S_xss, S_h, S_hTps, S_hT, S_zps, S_zss, S_latTps, S_latT, S_qps, S_qcp, S_dve,
     S_st, S_later, S_kept, S_xr, S_zr, S_1, S_add, S_x2) = [sem("mp_s_" + n) for n in names.split()]
    HB = ROPE // 2
    LAT_AT, PER = 2 + 4, 2 + 4 + 4
    with nc.Block() as block:
        @block.sync
        def _(sp):
            sp.dma_start(qn[:], a["mla_q_norm"][0:1, :].to_broadcast([P, QL])).then_inc(S_vec, 16)
            sp.dma_start(kvn[:], a["mla_kv_norm"][0:1, :].to_broadcast([P, KL])).then_inc(S_vec, 16)
            sp.dma_start(cos[:], a["k_cos32"]).then_inc(S_vec, 16)
            sp.dma_start(sin[:], a["k_sin32"]).then_inc(S_vec, 16)
            sp.dma_start(w_in[:], a["mla_w_in"][0].rearrange("(c p) n -> p c n", p=P)).then_inc(S_w, 16)
            sp.dma_start(w_uq[:], a["mla_w_uq"][0].rearrange("(c p) n -> p c n", p=P)).then_inc(S_w, 16)
            sp.dma_start(wuk[:], a["mla_w_uk"][0].rearrange("(c p) h n -> p c (h n)", p=P)).then_inc(S_later, 16)
            sp.dma_start(wuv[:], a["mla_w_uv"][0].rearrange("(c p) h n -> p c (h n)", p=P)).then_inc(S_later, 16)
            sp.wait_ge(S_kept, NT + START)
            sp.dma_start(o["ckv_p"][0, 0].rearrange("(t p) l -> p t l", p=P), ckv[:, 0:NTP, :]).then_inc(S_st, 16)
            sp.dma_start(o["ckv_s"][0].rearrange("b t l -> (b t) l"), ckv[0:NS, NTP, :]).then_inc(S_st, 16)
            sp.dma_start(o["kpe_p"][0, 0].rearrange("(t p) l -> p t l", p=P), kpe[:, 0:NTP, :]).then_inc(S_st, 16)
            sp.dma_start(o["kpe_s"][0].rearrange("b t l -> (b t) l"), kpe[0:NS, NTP, :]).then_inc(S_st, 16)
            sp.wait_ge(S_later, 32)
            sp.wait_ge(S_st, 64)

        @block.gpsimd
        def _(pool):
            nc.gpsimd.memset(rstd[:], 0.0).then_inc(S_1, 1)
            rms_of_tiles(nc, rms_inv, squares, stat, S_xss, S_x2, S_xr)

            def body(t, kind):
                wait_apart(pool, S_zss, 2 * t + 2, (S_1, 1))
                rms(nc, rstd, stat, slice(1, 3), S_add, t + 1).then_inc(S_zr, 1)
                pool.wait_ge(S_dve, t * PER + LAT_AT)
                nc.gpsimd.tensor_copy(ckv[:, t, :], ks[:])
                nc.gpsimd.tensor_copy(kpe[:, t, :], kp96[:, NOPE:QH]).then_inc(S_kept, 1)
            tiles(pool, body)

        @block.scalar
        def _(act):
            squares_of_tiles(nc, x, junk, squares, S_xss)

            def body(t, kind):
                for half in range(2):
                    act.wait_ge(S_hTps, 2 * t + half + 1)
                    nc.scalar.copy(hT[:, 4 * half:4 * half + 4, :],
                                   bank[half][:].rearrange("p (c n) -> p c n", c=4)).then_inc(S_hT, 1)
                act.wait_ge(S_zps, t + 1)
                nc.scalar.activation(junk[:, 0:QL], bank[2][:, 0:QL], ACT.Square, scale=QL ** -0.5,
                                     accum_out=stat[:, 1:2]).then_inc(S_zss, 1)
                nc.scalar.activation(junk[:, QL:QL + KL], bank[3][:, 0:KL], ACT.Square, scale=KL ** -0.5,
                                     accum_out=stat[:, 2:3]).then_inc(S_zss, 1)
                act.wait_ge(S_latTps, t + 1)
                nc.scalar.copy(cqT[:], bank[4][:, 0:QL].rearrange("p (c n) -> p c n", c=QL // P)).then_inc(S_latT, 1)
                nc.scalar.copy(ckvT[:, :, bass.ds(t * P, P)],
                               bank[5][:, 0:KL].rearrange("p (c n) -> p c n", c=2)).then_inc(S_latT, 1)
                nc.scalar.copy(kT[NOPE:QH, bass.ds(t * P, P)], bank[5][NOPE:QH, KL:KL + P]).then_inc(S_latT, 1)
                act.wait_ge(S_qps, t + 1)
                for i, b in enumerate((6, 7, 2)):
                    nc.scalar.copy(q[:, t, i * 512:(i + 1) * 512], bank[b][:]).then_inc(S_qcp, 1)
            tiles(act, body)

        @block.vector
        def _(dve):
            ch = Chain(dve, S_dve)
            nc.vector.memset(kp96[:], 0.0)
            dve.sem_inc(S_kept, START)
            dve.wait_ge(S_vec, 64)

            def rotate(src, dst, c, sn, n):
                A, B = ta[:, 0:n, :], tb[:, 0:n, :]
                ch.inc(nc.vector.tensor_tensor(A, src, c.to_broadcast([P, n, ROPE]), ALU.mult))
                ch.inc(nc.vector.tensor_tensor(B[:, :, 0:HB], src[:, :, HB:ROPE], sn[:, :, 0:HB].to_broadcast([P, n, HB]), ALU.mult))
                ch.step(nc.vector.tensor_tensor(B[:, :, HB:ROPE], src[:, :, 0:HB], sn[:, :, HB:ROPE].to_broadcast([P, n, HB]), ALU.mult))
                ch.inc(nc.vector.tensor_tensor(dst, A, B, ALU.add))

            normed = Chain(dve, S_h)

            def norm(t, kind):
                normed.round(2 * t)
                norm_steps(nc, normed, x, mod, rms_inv[:, bass.ds(t, 1)], h, t, kind)

            def body(t, next_kind):
                ch.round(t * PER)
                dve.wait_ge(S_zr, t + 1)
                ch.inc(nc.vector.scalar_tensor_tensor(out=cq[:], in0=bank[2][:, 0:QL], scalar=rstd[:, 1:2], in1=qn[:],
                                                      op0=ALU.mult, op1=ALU.mult))
                dve.wait_ge(S_kept, t + START)
                ch.inc(nc.vector.scalar_tensor_tensor(out=ks[:], in0=bank[3][:, 0:KL], scalar=rstd[:, 2:3], in1=kvn[:],
                                                      op0=ALU.mult, op1=ALU.mult))
                rotate(bank[3][:, KL:KL + ROPE].rearrange("p (a r) -> p a r", a=1),
                       kp96[:, NOPE:QH].rearrange("p (a r) -> p a r", a=1),
                       cos[:, bass.ds(t, 1), :], sin[:, bass.ds(t, 1), :], 1)
                if next_kind is not None:
                    norm(t + 1, next_kind)
                dve.wait_ge(S_qcp, 3 * t + 3)
                qv = q[:, t, :].rearrange("p (h r) -> p h r", h=H)[:, :, NOPE:QH]
                rotate(qv, qv, cos[:, bass.ds(t, 1), :], sin[:, bass.ds(t, 1), :], H)
                ch.end(PER)

            dve.wait_ge(S_xr, 1)
            norm(0, 0)
            with dve.Fori(0, NTP - 1) as t:
                body(t, 0)
            body(NTP - 1, 1)
            body(NTP, None)

        @block.tensor
        def _(pe):
            pe.wait_ge(S_w, 32)

            def body(t, kind):
                pe.wait_ge(S_h, 2 * t + 2)
                for half in range(2):
                    for c in range(4):
                        last = pe.transpose(bank[half][:, c * P:(c + 1) * P],
                                            h[:, (4 * half + c) * P:(4 * half + c + 1) * P], ident[:])
                    last.then_inc(S_hTps, 1)
                pe.wait_ge(S_hT, 2 * t + 2)
                for c in range(DC):
                    pe.matmul(bank[2][:, 0:QL], hT[:, c, :], w_in[:, c, 0:QL], start=(c == 0), stop=(c == DC - 1))
                for c in range(DC):
                    last = pe.matmul(bank[3][:, 0:KL + ROPE], hT[:, c, :], w_in[:, c, QL:ZN],
                                     start=(c == 0), stop=(c == DC - 1))
                last.then_inc(S_zps, 1)
                pe.wait_ge(S_dve, t * PER + LAT_AT)
                for c in range(QL // P):
                    pe.transpose(bank[4][:, c * P:(c + 1) * P], cq[:, c * P:(c + 1) * P], ident[:])
                for c in range(2):
                    pe.transpose(bank[5][:, c * P:(c + 1) * P], ks[:, c * P:(c + 1) * P], ident[:])
                pe.transpose(bank[5][0:QH, KL:KL + P], kp96[:], ident[:]).then_inc(S_latTps, 1)
                pe.wait_ge(S_latT, 3 * t + 3)
                for i, b in enumerate((6, 7, 2)):
                    for c in range(QL // P):
                        last = pe.matmul(bank[b][:], cqT[:, c, :], w_uq[:, c, i * 512:(i + 1) * 512],
                                         start=(c == 0), stop=(c == QL // P - 1))
                last.then_inc(S_qps, 1)
            tiles(pe, body)
    s.close()


def attend(nc, sbuf, sem, bank, s, tag, rounds, units, scale, prep, v_of, out_of, sink_of=None):
    U = len(units)
    KMAX = max(u["n"] for u in units)
    SB = 3
    sets = prep["sets"]
    probs = [sbuf(s, tag + f"probs{i}", [P, KMAX]) for i in range(SB)]
    probsT = [sbuf(s, tag + f"probsT{i}", [P, KMAX]) for i in range(2)]
    top = sbuf(s, tag + "top", [P, U])
    bias = sbuf(s, tag + "bias", [P, U])
    total = sbuf(s, tag + "total", [P, U])
    esink = sbuf(s, tag + "esink", [P, U])
    inv = sbuf(s, tag + "inv", [P, U])
    score_bank = lambda u: bank[2 + u % SB]
    turned_bank = lambda u: bank[5 + u % 2]
    out_bank = bank[7]
    names = "scores_ps bias_ready probs_ready probsT_ps probsT_ready out_ps out_free dve_step"
    S_sc, S_bias, S_pr, S_ptps, S_pt, S_ops, S_ofree, S_dve = [sem(tag + n) for n in names.split()]
    sink = sink_of is not None
    PER = sum(len(u["masks"]) + (4 if sink else 2) for u in units)

    def all_rounds(eng, name, body):
        if sets == 1:
            with eng.Fori(0, rounds) as i:
                prep[name](eng, i, 0)
                body(i, lambda u: None)
            return

        def run(i, last):
            def amid(u):
                if u == 1:
                    prep[name](eng, 2 * i + 1, 1)
                if u == U // 2 + 1 and not last:
                    prep[name](eng, 2 * i + 2, 0)
            body(i, amid)
        prep[name](eng, 0, 0)
        with eng.Fori(0, rounds - 1) as i:
            run(i, False)
        run(rounds - 1, True)

    def pool_body(pool):
        def body(i, amid):
            for u in range(U):
                amid(u)
        all_rounds(pool, "pool", body)

    def pe_body(pe):
        def body(i, amid):
            def scores(u):
                un = units[u]
                if u % (U // sets) == 0:
                    prep["ready"](pe, sets * i + u // (U // sets))
                pe.matmul(score_bank(u)[:, 0:un["n"]], un["q"], un["k"], start=True, stop=True).then_inc(S_sc, 1)

            def values(u):
                keys = units[u]["keys"]
                wait_apart(pe, S_ofree, i * U + u + 1, prep["settled"])
                wait_apart(pe, S_pt, i * U + u + 1, prep["settled"])
                for j, kt in enumerate(keys):
                    last = pe.matmul(out_bank[:, 0:HD], probsT[u % 2][:, j * P:(j + 1) * P], v_of(i, u, kt),
                                     start=(j == 0), stop=(j == len(keys) - 1))
                last.then_inc(S_ops, 1)

            scores(0)
            scores(1)
            for u, un in enumerate(units):
                if u + 2 < U:
                    scores(u + 2)
                pe.wait_ge(S_pr, i * U + u + 1)
                for j in range(un["n"] // P):
                    last = pe.transpose(turned_bank(u)[:, j * P:(j + 1) * P], probs[u % SB][:, j * P:(j + 1) * P], prep["ident"])
                last.then_inc(S_ptps, 1)
                if u:
                    values(u - 1)
                amid(u)
            values(U - 1)
        all_rounds(pe, "pe", body)

    def act_body(act):
        def body(i, amid):
            for u, un in enumerate(units):
                wait_apart(act, S_bias, i * U + u + 1, prep["settled"])
                if sink:
                    nc.scalar.activation(esink[:, u:u + 1], sink_of(i, u), ACT.Exp, bias=bias[:, u:u + 1])
                nc.scalar.activation(probs[u % SB][:, 0:un["n"]], score_bank(u)[:, 0:un["n"]], ACT.Exp,
                                     bias=bias[:, u:u + 1], scale=scale, accum_out=total[:, u:u + 1]).then_inc(S_pr, 1)
                amid(u)
        all_rounds(act, "act", body)

    def dve_body(dve):
        ch = Chain(dve, S_dve)
        nc.vector.memset(inv[:], 0.0).then_inc(S_ofree, 1)
        with dve.Fori(0, rounds) as i:
            ch.round(i * PER)

            def biases(u):
                un, b = units[u], score_bank(u)
                dve.wait_ge(S_sc, i * U + u + 1)
                for cols, mask in un["masks"]:
                    ch.step(nc.vector.tensor_tensor(b[:, cols], b[:, cols], mask, ALU.add))
                ch.step(nc.vector.tensor_reduce(top[:, u:u + 1], b[:, 0:un["n"]], AX_X, ALU.max))
                if sink:
                    ch.step(nc.vector.tensor_scalar(top[:, u:u + 1], top[:, u:u + 1], scale, sink_of(i, u), ALU.mult, ALU.max))
                nc.vector.tensor_scalar(bias[:, u:u + 1], top[:, u:u + 1], -1.0 if sink else -scale, None,
                                        ALU.mult).then_inc(S_bias, 1)

            def outputs(u):
                dve.wait_ge(S_ops, i * U + u + 1)
                if sink:
                    ch.step(nc.vector.tensor_tensor(total[:, u:u + 1], total[:, u:u + 1], esink[:, u:u + 1], ALU.add))
                ch.step(nc.vector.reciprocal(inv[:, u:u + 1], total[:, u:u + 1]))
                nc.vector.tensor_scalar(out_of(i, u), out_bank[:, 0:HD], inv[:, u:u + 1], None, ALU.mult).then_inc(S_ofree, 1)

            biases(0)
            biases(1)
            for u, un in enumerate(units):
                if u + 2 < U:
                    biases(u + 2)
                dve.wait_ge(S_ptps, i * U + u + 1)
                nc.vector.tensor_copy(probsT[u % 2][:, 0:un["n"]], turned_bank(u)[:, 0:un["n"]]).then_inc(S_pt, 1)
                if u:
                    outputs(u - 1)
            outputs(U - 1)
            ch.end(PER)

    return pool_body, pe_body, act_body, dve_body


def mla_prompt(nc, a, sbuf, sem, bank, ident, q, ckvT, kT, wuk, wuv, o_tok):
    s = ExitStack()
    v = sbuf(s, "at_v", [P, NTP, H * HD])
    qs = sbuf(s, "at_qs", [P, NTP, QH])
    wks = sbuf(s, "at_wks", [P, 2, NOPE])
    qT = [sbuf(s, f"at_qT{i}", [QH, SEQ]) for i in range(2)]
    kTs = [kT, sbuf(s, "at_kT1", [QH, SEQ])]
    causal = sbuf(s, "at_causal", [P, P])
    S_in, S_copied, S_qkps, S_qk, S_vps, S_v = [sem("at_" + n) for n in "mask_in copied qk_ps qk_ready v_ps v_ready".split()]
    S_kpe = sem("at_kpe_copied")

    def pool_prep(pool, h, odd):
        pool.wait_ge(S_qkps, h + START)
        nc.gpsimd.tensor_copy(qs[:], q[:, 0:NTP, bass.ds(h * QH, QH)])
        nc.gpsimd.tensor_copy(wks[:], wuk[:, :, bass.ds(h * NOPE, NOPE)]).then_inc(S_copied, 1)

    def pe_prep(pe, h, odd):
        pe.wait_ge(S_copied, h + 1)
        for t in range(NTP):
            pe.transpose(bank[0][0:QH, t * P:(t + 1) * P], qs[:, t, :], ident[:])
        for c in range(2):
            last = pe.matmul(bank[1][0:NOPE, :], wks[:, c, :], ckvT[:, c, 0:SEQ], start=(c == 0), stop=(c == 1))
        last.then_inc(S_qkps, 1)

    def act_prep(act, h, odd):
        act.wait_ge(S_qkps, h + 1 + START)
        nc.scalar.copy(qT[odd][:], bank[0][0:QH, :]).then_inc(S_qk, 1)
        nc.scalar.copy(kTs[odd][0:NOPE, 0:SEQ], bank[1][0:NOPE, :]).then_inc(S_qk, 1)

    def ready(pe, h):
        wait_apart(pe, S_qk, 2 * h + 2, (S_in, 16))

    units = [dict(head=g, t=n, q=qT[g][:, n * P:(n + 1) * P], k=kTs[g][:, 0:(n + 1) * P], n=(n + 1) * P,
                  masks=[(slice(n * P, (n + 1) * P), causal[:])], keys=list(range(n + 1))) for g in range(2) for n in range(NTP)]
    pool_body, pe_body, act_body, dve_body = attend(
        nc, sbuf, sem, bank, s, "at_", H // 2, units, MLA_SCALE,
        dict(pool=pool_prep, pe=pe_prep, act=act_prep, ready=ready, sets=2, ident=ident[:], settled=(S_in, 16)),
        v_of=lambda i, u, kt: v[:, kt, bass.ds((2 * i + units[u]["head"]) * HD, HD)],
        out_of=lambda i, u: o_tok[:, units[u]["t"], bass.ds((2 * i + units[u]["head"]) * HD, HD)])
    with nc.Block() as block:
        @block.sync
        def _(sp):
            sp.dma_start(causal[:], a["k_causal"]).then_inc(S_in, 16)
            sp.wait_ge(S_in, 16)

        @block.gpsimd
        def _(pool):
            nc.gpsimd.tensor_copy(kTs[1][NOPE:QH, :], kT[NOPE:QH, 0:SEQ]).then_inc(S_kpe, 1)
            pool.wait_ge(S_kpe, 1)
            pool.sem_inc(S_qkps, START)
            pool_body(pool)

        @block.tensor
        def _(pe):
            for kt in range(NTP):
                for half in range(2):
                    for c in range(2):
                        last = pe.matmul(bank[2 * (kt % 4) + half][:], ckvT[:, c, kt * P:(kt + 1) * P],
                                         wuv[:, c, half * 512:(half + 1) * 512], start=(c == 0), stop=(c == 1))
                    last.then_inc(S_vps, 1)
            pe.wait_ge(S_v, 8)
            pe.wait_ge(S_kpe, 1)
            pe_body(pe)

        @block.scalar
        def _(act):
            for n in range(8):
                act.wait_ge(S_vps, n + 1)
                nc.scalar.copy(v[:, n // 2, (n % 2) * 512:(n % 2 + 1) * 512], bank[n][:]).then_inc(S_v, 1)
            act_body(act)

        @block.vector
        def _(dve):
            dve.wait_ge(S_in, 16)
            dve_body(dve)
    s.close()


def mla_sample_queries(nc, sbuf, sem, bank, ident, q, kpe, wuk, qlT, qpT, kpeT):
    s = ExitStack()
    wukT = sbuf(s, "sq_wukT", [P, H // 2, KL])
    qn = sbuf(s, "sq_qn", [NS, H, NOPE])
    qp = sbuf(s, "sq_qp", [NS, H, ROPE])
    qnT = sbuf(s, "sq_qnT", [P, H // 2, NS])
    S_cp, S_ps, S_w, S_ps2, S_rd, S_qlps = [sem("sq_" + n) for n in "copied w_ps w_ready q_ps q_ready ql_ps".split()]
    S_out = sem("sq_out")
    with nc.Block() as block:
        @block.gpsimd
        def _(pool):
            qv = q[0:NS, NTP, :].rearrange("p (h r) -> p h r", h=H)
            nc.gpsimd.tensor_copy(qn[:], qv[:, :, 0:NOPE]).then_inc(S_cp, 1)
            nc.gpsimd.tensor_copy(qp[:], qv[:, :, NOPE:QH]).then_inc(S_cp, 1)

        @block.tensor
        def _(pe):
            for j in range(H // 2):
                for c in range(2):
                    n = 2 * j + c
                    last = pe.transpose(bank[n // 4][:, (n % 4) * P:(n % 4 + 1) * P], wuk[:, c, j * P:(j + 1) * P], ident[:])
            last.then_inc(S_ps, 1)
            pe.wait_ge(S_cp, 2)
            for j in range(H // 2):
                pe.transpose(bank[4][:, j * NS:(j + 1) * NS], qn[:, 2 * j:2 * j + 2, :].rearrange("p h n -> p (h n)"),
                             ident[0:NS, 0:NS])
            for h in range(H):
                pe.transpose(bank[5 + h // 8][0:ROPE, (h % 8) * NS:(h % 8 + 1) * NS], qp[:, h, :], ident[0:NS, 0:NS])
            pe.transpose(bank[7][0:ROPE, 0:NS], kpe[0:NS, NTP, :], ident[0:NS, 0:NS]).then_inc(S_ps2, 1)
            pe.wait_ge(S_w, 4)
            pe.wait_ge(S_rd, 1)
            for h in range(H):
                r = slice((h % 2) * NOPE, (h % 2 + 1) * NOPE)
                for c in range(2):
                    last = pe.matmul(bank[2 * c + h % 2][:, (h // 2) * NS:(h // 2 + 1) * NS], wukT[r, h // 2, c * P:(c + 1) * P],
                                     qnT[r, h // 2, :], start=True, stop=True)
            last.then_inc(S_qlps, 1)

        @block.scalar
        def _(act):
            act.wait_ge(S_ps, 1)
            for n in range(4):
                nc.scalar.copy(wukT[:, 2 * n:2 * n + 2, :].rearrange("p a b -> p (a b)"), bank[n][:]).then_inc(S_w, 1)

        @block.vector
        def _(dve):
            dve.wait_ge(S_ps2, 1)
            nc.vector.tensor_copy(qnT[:], bank[4][:].rearrange("p (j n) -> p j n", j=H // 2)).then_inc(S_rd, 1)
            qpv = qpT[:].rearrange("p b (h t) -> p h b t", h=H)
            for n in range(2):
                nc.vector.tensor_copy(qpv[:, 8 * n:8 * n + 8], bank[5 + n][0:ROPE, :].rearrange("p (h b t) -> p h b t", h=8, b=DB))
            nc.vector.tensor_copy(kpeT[:], bank[7][0:ROPE, 0:NS])
            dve.wait_ge(S_qlps, 1)
            for c in range(2):
                qlv = qlT[:, c].rearrange("p b (h e t) -> p e h b t", e=2, h=H // 2)
                for n in range(2):
                    nc.vector.tensor_copy(qlv[:, n],
                                          bank[2 * c + n][:].rearrange("p (h b t) -> p h b t", h=8, b=DB)).then_inc(S_out, 1)
    s.close()


def mla_sample(nc, a, sbuf, sem, bank, ident, ckv, ckvT, kpeT, qlT, qpT, wuv, o_tok):
    s = ExitStack()
    PC = NG + 1
    S_pages = sem("sa_pages_in")
    KR = NG
    n_pool = a["cache_mla_ckv"].shape[1]
    kv = [sbuf(s, f"sa_kv{i}", [P, GP, KL + ROPE]) for i in range(KR)]
    kt = [sbuf(s, f"sa_kt{i}", [P, 3, GP * P]) for i in range(2)]
    probs = [sbuf(s, f"sa_probs{i}", [P, GP * P]) for i in range(2)]
    probsT = [sbuf(s, f"sa_probsT{i}", [P, GP * P]) for i in range(2)]
    qb = sbuf(s, "sa_qb", [P, 3, P])
    part = sbuf(s, "sa_part", [P, PC, KL])
    ntop = sbuf(s, "sa_ntop", [P, PC])
    bias = sbuf(s, "sa_bias", [P, PC])
    total = sbuf(s, "sa_total", [P, PC])
    wgt = sbuf(s, "sa_wgt", [P, PC])
    one = sbuf(s, "sa_one", [P, 4])
    prod = sbuf(s, "sa_prod", [P, PC, KL])
    olat = sbuf(s, "sa_olat", [P, DB, KL])
    olT = sbuf(s, "sa_olT", [P, 2, H, NS])
    mask = sbuf(s, "sa_mask", [P, DB, NS])
    pages = sbuf(s, "sa_pages", [1, DB * NPG], I32)
    kv_in = [sem(f"sa_kv_in{i}") for i in range(KR)]
    names = "mask_in copied kT_ps kT_dve kT_act scores_ps bias_ready probs_ready probsT_ps probsT_ready part_ps part_done dve_step"
    (S_in, S_cp, S_ktps, S_ktd, S_kta, S_sc, S_bias, S_pr, S_ptps, S_pt, S_pps, S_pd, S_dve) = [sem("sa_" + n) for n in names.split()]
    S_join, S_wgt, S_shares, S_olps, S_olT, S_ops, S_zero, S_joined = [sem("sa_" + n) for n in "join_ready wgt_ready shares_ready olat_ps olatT_ready o_ps zeroed joined".split()]
    PER = PC + 1 + 1 + 2
    JOIN = 5
    with nc.Block() as block:
        @block.sync
        def _(sp):
            sp.dma_start(pages[:], a["page_table"].rearrange("b n -> (b n)").unsqueeze(0)).then_inc(S_pages, 16)
            sp.dma_start(mask[:], a["k_mask_new"]).then_inc(S_in, 16)
            sp.wait_ge(S_pages, 16)
            with sp.Fori(0, DB) as b:
                for g in range(NG):
                    slot = g % KR
                    wait_apart(sp, S_pd, b * PC + (g if g < KR else g + 1) + START, (S_in, 16))
                    for j in range(GP):
                        page = sp.value_load(pages[0:1, bass.ds(b * NPG + g * GP + j, 1)], min_val=0, max_val=n_pool - 1)
                        sp.dma_start(kv[slot][:, j, 0:KL], a["cache_mla_ckv"][0, bass.ds(page, 1)].rearrange("a p l -> p (a l)")).then_inc(kv_in[slot], 16)
                        sp.dma_start(kv[slot][:, j, KL:KL + ROPE], a["cache_mla_kpe"][0, bass.ds(page, 1)].rearrange("a p l -> p (a l)")).then_inc(kv_in[slot], 16)

        @block.gpsimd
        def _(pool):
            nc.gpsimd.memset(o_tok[:, NTP, :], 0.0).then_inc(S_zero, 1)
            pool.sem_inc(S_sc, START)
            ch = Chain(pool, S_joined)

            def queries(b):
                pool.wait_ge(S_sc, b * PC + START)
                nc.gpsimd.tensor_copy(qb[:, 0, :], qlT[:, 0, bass.ds(b, 1), :].rearrange("p a n -> p (a n)"))
                nc.gpsimd.tensor_copy(qb[:, 1, :], qlT[:, 1, bass.ds(b, 1), :].rearrange("p a n -> p (a n)"))
                nc.gpsimd.tensor_copy(qb[0:ROPE, 2, :], qpT[:, bass.ds(b, 1), :].rearrange("p a n -> p (a n)")).then_inc(S_cp, 1)
                pool.wait_ge(S_cp, b + 1)

            def join(b):
                ch.round(b * JOIN + JOIN)
                pool.wait_ge(S_shares, b + 1)
                pool.wait_ge(S_pd, (b + 1) * PC + KR + START)
                ch.step(nc.gpsimd.tensor_tensor(prod[:], part[:], wgt[:].unsqueeze(2).to_broadcast([P, PC, KL]), ALU.mult))
                for n in (4, 2, 1):
                    ch.step(nc.gpsimd.tensor_tensor(prod[:, 0:n], prod[:, 0:n], prod[:, n:2 * n], ALU.add))
                ch.step(nc.gpsimd.tensor_tensor(olat[:, bass.ds(b, 1)], prod[:, 0:1], prod[:, PC - 1:PC], ALU.add))
                assert ch.n == JOIN

            pool.wait_ge(S_zero, 1)
            queries(0)
            with pool.Fori(0, DB - 1) as b:
                queries(b + 1)
                join(b)
            join(DB - 1)

        @block.tensor
        def _(pe):
            with pe.Fori(0, DB) as b:
                def turn(g):
                    slot = g % KR
                    pe.wait_ge(kv_in[slot], (b * (NG // KR) + g // KR + 1) * 2 * GP * 16)
                    for j in range(GP):
                        for c in range(2):
                            pe.transpose(bank[c][:, j * P:(j + 1) * P], kv[slot][:, j, c * P:(c + 1) * P], ident[:])
                        last = pe.transpose(bank[2][0:ROPE, j * P:(j + 1) * P], kv[slot][:, j, KL:KL + ROPE], ident[:])
                    last.then_inc(S_ktps, 1)

                def scores(g):
                    out = bank[6 if g % 2 else 3]
                    if g == 0:
                        pe.wait_ge(S_cp, b + 1)
                    if g < NG:
                        pe.wait_ge(S_ktd, b * NG + g + 1)
                        pe.wait_ge(S_kta, b * NG + g + 1)
                        k = kt[g % 2]
                        pe.matmul(out[:], qb[:, 0, :], k[:, 0, :], start=True, stop=False)
                        pe.matmul(out[:], qb[:, 1, :], k[:, 1, :], start=False, stop=False)
                        pe.matmul(out[:], qb[0:ROPE, 2, :], k[0:ROPE, 2, :], start=False, stop=True).then_inc(S_sc, 1)
                    else:
                        pe.matmul(out[:, 0:NS], qb[:, 0, :], ckvT[:, 0, SEQ:SEQ + NS], start=True, stop=False)
                        pe.matmul(out[:, 0:NS], qb[:, 1, :], ckvT[:, 1, SEQ:SEQ + NS], start=False, stop=False)
                        pe.matmul(out[:, 0:NS], qb[0:ROPE, 2, :], kpeT[:], start=False, stop=True).then_inc(S_sc, 1)

                def turn_probs(g):
                    wait_apart(pe, S_pr, b * PC + g + 1, (S_in, 16))
                    wait_apart(pe, S_pt, b * PC + g + START, (S_in, 16))
                    if g < NG:
                        for j in range(GP):
                            last = pe.transpose(bank[4][:, j * P:(j + 1) * P], probs[g % 2][:, j * P:(j + 1) * P], ident[:])
                    else:
                        last = pe.transpose(bank[4][0:NS, 0:P], probs[g % 2][:, 0:NS], ident[:])
                    last.then_inc(S_ptps, 1)

                def values(g):
                    out = bank[7 if g % 2 else 5]
                    pe.wait_ge(S_pt, b * PC + g + 1 + START)
                    if g >= 2:
                        pe.wait_ge(S_pd, b * PC + g - 1 + KR + START)
                    if g < NG:
                        for j in range(GP):
                            last = pe.matmul(out[:, 0:KL], probsT[g % 2][:, j * P:(j + 1) * P], kv[g % KR][:, j, 0:KL],
                                             start=(j == 0), stop=(j == GP - 1))
                    else:
                        last = pe.matmul(out[:, 0:KL], probsT[g % 2][0:NS, 0:P], ckv[0:NS, NTP, :], start=True, stop=True)
                    last.then_inc(S_pps, 1)

                turn(0)
                scores(0)
                turn(1)
                for g in range(PC):
                    if g + 1 < PC:
                        scores(g + 1)
                    if g + 2 < NG:
                        turn(g + 2)
                    turn_probs(g)
                    if g:
                        values(g - 1)
                values(NG)
            pe.wait_ge(S_joined, DB * JOIN + JOIN)
            for b in range(DB):
                for c in range(2):
                    n = 2 * b + c
                    last = pe.transpose(bank[n // 4][:, (n % 4) * P:(n % 4 + 1) * P], olat[:, b, c * P:(c + 1) * P], ident[:])
            last.then_inc(S_olps, 1)
            pe.wait_ge(S_olT, 1)
            for h in range(H):
                for c in range(2):
                    last = pe.matmul(bank[h // 8][0:NS, (h % 8) * HD:(h % 8 + 1) * HD], olT[:, c, h, :], wuv[:, c, h * HD:(h + 1) * HD],
                                     start=(c == 0), stop=(c == 1))
                if h % 8 == 7:
                    last.then_inc(S_ops, 1)

        @block.scalar
        def _(act):
            with act.Fori(0, DB) as b:
                def keys(g):
                    act.wait_ge(S_ktps, b * NG + g + 1)
                    nc.scalar.copy(kt[g % 2][:, 1, :], bank[1][:])
                    nc.scalar.copy(kt[g % 2][0:ROPE, 2, :], bank[2][0:ROPE, :]).then_inc(S_kta, 1)

                def exps(g):
                    n = GP * P if g < NG else NS
                    act.wait_ge(S_bias, b * PC + g + 1)
                    nc.scalar.activation(probs[g % 2][:, 0:n], bank[6 if g % 2 else 3][:, 0:n], ACT.Exp, bias=bias[:, g:g + 1],
                                         scale=MLA_SCALE, accum_out=total[:, g:g + 1]).then_inc(S_pr, 1)

                keys(0)
                exps(0)
                keys(1)
                for g in range(PC - 1):
                    exps(g + 1)
                    if g + 2 < NG:
                        keys(g + 2)
                act.wait_ge(S_join, b + 1)
                nc.scalar.activation(wgt[:], ntop[:], ACT.Exp, bias=one[:, 0:1], scale=-MLA_SCALE).then_inc(S_wgt, 1)
            act.wait_ge(S_olps, 1)
            for b in range(DB):
                for c in range(2):
                    n = 2 * b + c
                    last = nc.scalar.copy(olT[:, c, :, b * DS:(b + 1) * DS],
                                          bank[n // 4][:, (n % 4) * P:(n % 4 + 1) * P].rearrange("p (h t) -> p h t", h=H))
            last.then_inc(S_olT, 1)
            act.wait_ge(S_ops, 2)
            act.wait_ge(S_zero, 1)
            for n in range(2):
                nc.scalar.copy(o_tok[0:NS, NTP, n * 512:(n + 1) * 512], bank[n][0:NS, :])

        @block.vector
        def _(dve):
            ch = Chain(dve, S_dve)
            dve.wait_ge(S_in, 16)
            nc.vector.memset(one[:], 0.0).then_inc(S_pd, KR + START)
            dve.sem_inc(S_pt, START)
            dve.sem_inc(S_joined, JOIN)
            with dve.Fori(0, DB) as b:
                ch.round(b * PER)

                def keys(g):
                    dve.wait_ge(S_ktps, b * NG + g + 1)
                    nc.vector.tensor_copy(kt[g % 2][:, 0, :], bank[0][:]).then_inc(S_ktd, 1)

                def biases(g):
                    src = bank[6 if g % 2 else 3]
                    n = GP * P if g < NG else NS
                    dve.wait_ge(S_sc, b * PC + g + 1 + START)
                    if g == NG:
                        ch.step(nc.vector.tensor_tensor(src[:, 0:n], src[:, 0:n], mask[:, bass.ds(b, 1), :].rearrange("p a n -> p (a n)"), ALU.add))
                    ch.step(nc.vector.tensor_reduce(ntop[:, g:g + 1], src[:, 0:n], AX_X, ALU.max, negate=True))
                    nc.vector.tensor_scalar(bias[:, g:g + 1], ntop[:, g:g + 1], MLA_SCALE, None, ALU.mult).then_inc(S_bias, 1)

                def parts(g):
                    dve.wait_ge(S_pps, b * PC + g + 1)
                    if g == 0:
                        dve.wait_ge(S_joined, b * JOIN + 1)
                    nc.vector.tensor_copy(part[:, g, :], bank[7 if g % 2 else 5][:, 0:KL]).then_inc(S_pd, 1)

                keys(0)
                biases(0)
                keys(1)
                for g in range(PC):
                    if g + 1 < PC:
                        biases(g + 1)
                    if g + 1 == NG:
                        ch.step(nc.vector.tensor_reduce(one[:, 1:2], ntop[:], AX_X, ALU.min))
                        nc.vector.tensor_scalar(one[:, 0:1], one[:, 1:2], MLA_SCALE, None, ALU.mult).then_inc(S_join, 1)
                    if g + 2 < NG:
                        keys(g + 2)
                    n = GP * P if g < NG else P
                    r = P if g < NG else NS
                    dve.wait_ge(S_ptps, b * PC + g + 1)
                    nc.vector.tensor_copy(probsT[g % 2][0:r, 0:n], bank[4][0:r, 0:n]).then_inc(S_pt, 1)
                    if g:
                        parts(g - 1)
                dve.wait_ge(S_wgt, b + 1)
                ch.step(nc.vector.scalar_tensor_tensor(out=total[:], in0=total[:], scalar=1.0, in1=wgt[:], op0=ALU.mult, op1=ALU.mult,
                                                       accum_out=one[:, 2:3]))
                ch.step(nc.vector.reciprocal(one[:, 3:4], one[:, 2:3]))
                nc.vector.tensor_scalar(wgt[:], wgt[:], one[:, 3:4], None, ALU.mult).then_inc(S_shares, 1)
                parts(NG)
                ch.end(PER)
    s.close()


def project_out(nc, w_o, tag, sbuf, sem, bank, x, ident, mod, junk, tiles, o_tok):
    s = ExitStack()
    w = sbuf(s, tag + "w", [P, DC, D])
    oT = sbuf(s, tag + "oT", [P, DC, NT * P])
    S_tps, S_t, S_yps, S_scaled, S_added = [sem(tag + n) for n in "oT_ps oT_ready y_ps scaled added".split()]
    w_in = [sem(tag + f"w_in{i}") for i in range(2)]
    turned_bank = lambda t, half: bank[2 * (t % 2) + half]
    product_bank = lambda t, n: bank[4 + 2 * (t % 2) + n]
    with nc.Block() as block:
        @block.sync
        def _(sp):
            src = w_o.rearrange("(c p) n -> p c n", p=P)
            for n in range(2):
                sp.dma_start(w[:, :, n * 512:(n + 1) * 512], src[:, :, n * 512:(n + 1) * 512]).then_inc(w_in[n], 16)

        @block.tensor
        def _(pe):
            for t in range(NT):
                if t >= 2:
                    pe.wait_ge(S_t, 2 * (t - 1))
                for half in range(2):
                    for c in range(4):
                        last = pe.transpose(turned_bank(t, half)[:, c * P:(c + 1) * P],
                                            o_tok[:, t, (4 * half + c) * P:(4 * half + c + 1) * P], ident[:])
                    last.then_inc(S_tps, 1)
            for t in range(NT):
                pe.wait_ge(S_t, 2 * t + 2)
                if t >= 2:
                    pe.wait_ge(S_scaled, 2 * (t - 1))
                for n in range(2):
                    if t == 0:
                        pe.wait_ge(w_in[n], 16)
                    for c in range(DC):
                        last = pe.matmul(product_bank(t, n)[:], oT[:, c, t * P:(t + 1) * P], w[:, c, n * 512:(n + 1) * 512],
                                         start=(c == 0), stop=(c == DC - 1))
                    last.then_inc(S_yps, 1)

        @block.scalar
        def _(act):
            for t in range(NT):
                for half in range(2):
                    act.wait_ge(S_tps, 2 * t + half + 1)
                    nc.scalar.copy(oT[:, 4 * half:4 * half + 4, t * P:(t + 1) * P],
                                   turned_bank(t, half)[:].rearrange("p (c n) -> p c n", c=4)).then_inc(S_t, 1)

        @block.vector
        def _(dve):
            for t in range(NT):
                if t:
                    dve.wait_ge(S_added, t)
                for n in range(2):
                    dve.wait_ge(S_yps, 2 * t + n + 1)
                    nc.vector.tensor_tensor(junk[:, n * 512:(n + 1) * 512], product_bank(t, n)[:],
                                            mod[:, t // NTP, 2 * D + n * 512:2 * D + (n + 1) * 512], ALU.mult).then_inc(S_scaled, 1)
                dve.wait_ge(S_scaled, 2 * t + 2)
                nc.vector.tensor_tensor(x[:, t, :], x[:, t, :], junk[:], ALU.add).then_inc(S_added, 1)
    s.close()


def swa(nc, a, o, scratch, sbuf, sem, bank, x, ident, mod, stat, rstd, junk, tiles):
    s = ExitStack()
    o_tok = sbuf(s, "o_tok1", [P, NT, D])
    qkv = sbuf(s, "qkv", [P, NT, SWA_N])
    swa_project(nc, a, o, sbuf, sem, bank, x, ident, mod, stat, rstd, junk, tiles, qkv)
    swa_prompt(nc, a, sbuf, sem, bank, ident, qkv, o_tok)
    swa_sample(nc, a, o, scratch, sbuf, sem, bank, ident, qkv, o_tok)
    project_out(nc, a["swa_w_o"][0], "so_", sbuf, sem, bank, x, ident, mod, junk, tiles, o_tok)
    s.close()


def swa_project(nc, a, o, sbuf, sem, bank, x, ident, mod, stat, rstd, junk, tiles, qkv):
    s = ExitStack()
    w = sbuf(s, "sp_w", [P, DC, SWA_N])
    bq = sbuf(s, "sp_b", [P, SWA_N])
    cos = sbuf(s, "sp_cos", [P, NT, ROT])
    sin = sbuf(s, "sp_sin", [P, NT, ROT])
    h = sbuf(s, "sp_h", [P, D])
    squares = sbuf(s, "sp_squares", [P, NT])
    rms_inv = sbuf(s, "sp_rms_inv", [P, NT])
    hT = sbuf(s, "sp_hT", [P, DC, P])
    NR = H + KVH
    ta = sbuf(s, "sp_ta", [P, NR, ROT])
    tb = sbuf(s, "sp_tb", [P, NR, ROT])
    names = "w_in vec_in x_ss hT_ps hT_ready z_ps dve_step stored x_rms rms_step norm_step biased"
    S_w, S_vec, S_xss, S_hTps, S_hT, S_zps, S_dve, S_st, S_xr, S_x2, S_h, S_biased = [sem("sp_s_" + n) for n in names.split()]
    HB = ROT // 2
    PER = 2 + 4
    KC, VC, NKV = H * HD, (H + KVH) * HD, KVH * HD
    keep = SEQ - P
    with nc.Block() as block:
        @block.sync
        def _(sp):
            sp.dma_start(bq[:], a["swa_b_qkv"][0:1, :].to_broadcast([P, SWA_N])).then_inc(S_vec, 16)
            sp.dma_start(cos[:], a["k_cos16"]).then_inc(S_vec, 16)
            sp.dma_start(sin[:], a["k_sin16"]).then_inc(S_vec, 16)
            sp.dma_start(w[:], a["swa_w_qkv"][0].rearrange("(c p) n -> p c n", p=P)).then_inc(S_w, 16)
            for name, src in (("swk_s", a["cache_swa_k"]), ("swv_s", a["cache_swa_v"])):
                sp.dma_start(o[name][0][:, 0:P - DS].rearrange("b t g d -> b (t g d)"),
                             src[0][:, DS:P].rearrange("b t g d -> b (t g d)")).then_inc(S_st, 16)
            sp.wait_ge(S_dve, NT * PER)
            for name, c in (("p", KC), ("p", VC)):
                out = o["swk_p" if c == KC else "swv_p"][0, 0].rearrange("t g d -> t (g d)")
                sp.dma_start(out, qkv[:, NTP - 1, c:c + NKV]).then_inc(S_st, 16)
            for b in range(DB):
                for name, c in (("swk_s", KC), ("swv_s", VC)):
                    sp.dma_start(o[name][0, b, P - DS:P].rearrange("t g d -> t (g d)"),
                                 qkv[b * DS:(b + 1) * DS, NTP, c:c + NKV]).then_inc(S_st, 16)
            sp.wait_ge(S_st, 16 * (4 + 2 * DB))

        @block.gpsimd
        def _(pool):
            rms_of_tiles(nc, rms_inv, squares, stat, S_xss, S_x2, S_xr)

        @block.scalar
        def _(act):
            squares_of_tiles(nc, x, junk, squares, S_xss)

            def body(t, kind):
                for half in range(2):
                    act.wait_ge(S_hTps, 2 * t + half + 1)
                    nc.scalar.copy(hT[:, 4 * half:4 * half + 4, :],
                                   bank[half][:].rearrange("p (c n) -> p c n", c=4)).then_inc(S_hT, 1)
            tiles(act, body)

        @block.vector
        def _(dve):
            ch = Chain(dve, S_dve)
            dve.wait_ge(S_vec, 48)

            normed = Chain(dve, S_h)
            dve.sem_inc(S_biased, START)

            def norm(t, kind):
                normed.round(2 * t)
                norm_steps(nc, normed, x, mod, rms_inv[:, bass.ds(t, 1)], h, t, kind)

            def body(t, next_kind):
                ch.round(t * PER)
                if next_kind is not None:
                    dve.wait_ge(S_hTps, 2 * t + 2)
                    norm(t + 1, next_kind)
                dve.wait_ge(S_zps, t + 1)
                for n in range(3):
                    add = nc.vector.tensor_tensor(qkv[:, t, n * 512:(n + 1) * 512], bank[2 + n][:], bq[:, n * 512:(n + 1) * 512], ALU.add)
                    add.then_inc(S_biased, 1) if n == 2 else ch.inc(add)
                dve.wait_ge(S_biased, t + 1 + START)
                v = qkv[:, t, 0:NR * HD].rearrange("p (h r) -> p h r", h=NR)[:, :, 0:ROT]
                c, sn = cos[:, bass.ds(t, 1), :], sin[:, bass.ds(t, 1), :]
                ch.inc(nc.vector.tensor_tensor(ta[:], v, c.to_broadcast([P, NR, ROT]), ALU.mult))
                ch.inc(nc.vector.tensor_tensor(tb[:, :, 0:HB], v[:, :, HB:ROT], sn[:, :, 0:HB].to_broadcast([P, NR, HB]), ALU.mult))
                ch.step(nc.vector.tensor_tensor(tb[:, :, HB:ROT], v[:, :, 0:HB], sn[:, :, HB:ROT].to_broadcast([P, NR, HB]), ALU.mult))
                ch.inc(nc.vector.tensor_tensor(v, ta[:], tb[:], ALU.add))
                ch.end(PER)

            dve.wait_ge(S_xr, 1)
            norm(0, 0)
            with dve.Fori(0, NTP - 1) as t:
                body(t, 0)
            body(NTP - 1, 1)
            body(NTP, None)

        @block.tensor
        def _(pe):
            pe.wait_ge(S_w, 16)

            def body(t, kind):
                pe.wait_ge(S_h, 2 * t + 2)
                for half in range(2):
                    for c in range(4):
                        last = pe.transpose(bank[half][:, c * P:(c + 1) * P],
                                            h[:, (4 * half + c) * P:(4 * half + c + 1) * P], ident[:])
                    last.then_inc(S_hTps, 1)
                pe.wait_ge(S_hT, 2 * t + 2)
                pe.wait_ge(S_biased, t + START)
                for n in range(3):
                    for c in range(DC):
                        last = pe.matmul(bank[2 + n][:], hT[:, c, :], w[:, c, n * 512:(n + 1) * 512],
                                         start=(c == 0), stop=(c == DC - 1))
                last.then_inc(S_zps, 1)
            tiles(pe, body)
    s.close()


def swa_prompt(nc, a, sbuf, sem, bank, ident, qkv, o_tok):
    s = ExitStack()
    qs = sbuf(s, "wt_qs", [P, NTP, GRP * HD])
    ks = sbuf(s, "wt_ks", [P, NTP, HD])
    qT = sbuf(s, "wt_qT", [HD, GRP, SEQ])
    kT = sbuf(s, "wt_kT", [HD, SEQ])
    band = sbuf(s, "wt_band", [P, 2 * P])
    sinks = sbuf(s, "wt_sinks", [P, H])
    S_in, S_cp, S_ps, S_rd = [sem("wt_" + n) for n in "mask_in copied qk_ps qk_ready".split()]

    def pool_prep(pool, i, odd):
        pool.wait_ge(S_ps, i + START)
        nc.gpsimd.tensor_copy(qs[:], qkv[:, 0:NTP, bass.ds(i * GRP * HD, GRP * HD)])
        nc.gpsimd.tensor_copy(ks[:], qkv[:, 0:NTP, bass.ds(i * HD + H * HD, HD)]).then_inc(S_cp, 1)

    def pe_prep(pe, i, odd):
        wait_apart(pe, S_cp, i + 1, (S_in, 32))
        for t in range(NTP):
            pe.transpose(bank[0][0:HD, t * P:(t + 1) * P], ks[:, t, :], ident[:])
        for j in range(GRP):
            for t in range(NTP):
                last = pe.transpose(bank[1 + j][0:HD, t * P:(t + 1) * P], qs[:, t, j * HD:(j + 1) * HD], ident[:])
        last.then_inc(S_ps, 1)

    def ready(pe, i):
        wait_apart(pe, S_rd, i + 1, (S_in, 32))

    def act_prep(act, i, odd):
        act.wait_ge(S_ps, i + 1 + START)
        nc.scalar.copy(kT[:], bank[0][0:HD, :])
        for j in range(GRP):
            last = nc.scalar.copy(qT[:, j, :], bank[1 + j][0:HD, :])
        last.then_inc(S_rd, 1)

    units = []
    for j in range(GRP):
        for n in range(NTP):
            k0 = max(n - 1, 0)
            m = band[:] if n else band[:, P:2 * P]
            units.append(dict(j=j, t=n, q=qT[:, j, n * P:(n + 1) * P], k=kT[:, k0 * P:(n + 1) * P], n=(n + 1 - k0) * P,
                              masks=[(slice(0, (n + 1 - k0) * P), m)], keys=list(range(k0, n + 1))))
    pool_body, pe_body, act_body, dve_body = attend(
        nc, sbuf, sem, bank, s, "wt_", KVH, units, SWA_SCALE,
        dict(pool=pool_prep, pe=pe_prep, act=act_prep, ready=ready, sets=1, ident=ident[:], settled=(S_in, 32)),
        v_of=lambda i, u, kt: qkv[:, kt, bass.ds(i * HD + (H + KVH) * HD, HD)],
        out_of=lambda i, u: o_tok[:, units[u]["t"], bass.ds(i * GRP * HD + units[u]["j"] * HD, HD)],
        sink_of=lambda i, u: sinks[:, bass.ds(i * GRP + units[u]["j"], 1)])
    with nc.Block() as block:
        @block.sync
        def _(sp):
            sp.dma_start(band[:], a["k_band"]).then_inc(S_in, 16)
            sp.dma_start(sinks[:], a["swa_sinks"][0:1, :].to_broadcast([P, H])).then_inc(S_in, 16)

        @block.gpsimd
        def _(pool):
            pool.sem_inc(S_ps, START)
            pool_body(pool)

        @block.tensor
        def _(pe):
            pe_body(pe)

        @block.scalar
        def _(act):
            act_body(act)

        @block.vector
        def _(dve):
            dve.wait_ge(S_in, 32)
            dve_body(dve)
    s.close()


def swa_sample(nc, a, o, scratch, sbuf, sem, bank, ident, qkv, o_tok):
    s = ExitStack()
    NKV = KVH * HD
    TK = P + DS
    qt = sbuf(s, "ws_qt", [NS, 2, GRP, 2, HD])
    qbd = sbuf(s, "ws_qbd", [P, DB, 2, KVH, GRP, DS])
    qb = sbuf(s, "ws_qb", [P, 2, P])
    ka = [sbuf(s, f"ws_ka{i}", [P, NKV]) for i in range(2)]
    va = [sbuf(s, f"ws_va{i}", [P, NKV]) for i in range(2)]
    kb = [sbuf(s, f"ws_kb{i}", [DS, NKV]) for i in range(2)]
    vb = [sbuf(s, f"ws_vb{i}", [DS, NKV]) for i in range(2)]
    kT = sbuf(s, "ws_kT", [P, 2, TK])
    mask = sbuf(s, "ws_mask", [P, TK])
    snk = sbuf(s, "ws_sink", [P, 1])
    probs = sbuf(s, "ws_probs", [P, TK])
    pT = sbuf(s, "ws_pT", [P, 2 * P])
    st = sbuf(s, "ws_st", [P, 6])
    ow = [sbuf(s, f"ws_o{i}", [P, HD]) for i in range(2)]
    names = "const_in qt_ready q_ps q_ready zeroed qb_ready kT_ps kT_ready scores_ps bias_ready probs_ready pT_ps pT_ready o_ps o_ready dve_step joined"
    (S_in, S_qt, S_qps, S_q, S_z, S_qb, S_ktps, S_kt, S_sc, S_bias, S_pr, S_ptps, S_pt, S_ops, S_o, S_dve, S_join) = [
        sem("ws_" + n) for n in names.split()]
    kv_in = [sem(f"ws_kv_in{i}") for i in range(2)]
    stored = [sem(f"ws_stored{i}") for i in range(2)]
    PER = 6
    with nc.Block() as block:
        @block.sync
        def _(sp):
            sp.dma_start(mask[:], a["k_mask_win"]).then_inc(S_in, 16)
            sp.dma_start(snk[:], a["swa_sinks"].rearrange("a (h u) -> (a h) u", u=1).to_broadcast([H, DS]).rearrange("h (t u) -> h t u", u=1)).then_inc(S_in, 16)
            sp.sem_inc(S_ops, START)

            def load(i, p):
                b = i * 2 + p
                for dst, src in ((ka, o["swk_s"]), (va, o["swv_s"])):
                    sp.dma_start(dst[p][:], src[0, bass.ds(b, 1)].rearrange("b t g d -> (b t) (g d)")).then_inc(kv_in[p], 16)
                for dst, src in ((kb, a["cache_swa_k"]), (vb, a["cache_swa_v"])):
                    sp.dma_start(dst[p][:], src[0, bass.ds(b, 1), 0:DS].rearrange("b t g d -> (b t) (g d)")).then_inc(kv_in[p], 16)

            def store(i, p):
                b = i * 2 + p
                sp.wait_ge(S_o, b + 1)
                sp.dma_start(scratch[bass.ds(b, 1)].rearrange("b t h d -> h (b t) d"), ow[p][:]).then_inc(stored[p], 16)

            load(0, 0)
            load(0, 1)
            with sp.Fori(0, DB // 2 - 1) as i:
                for p in range(2):
                    sp.wait_ge(S_ops, i * 2 + p + 1 + START)
                    load(i + 1, p)
                    store(i, p)
            for p in range(2):
                store(DB // 2 - 1, p)
            sp.wait_ge(stored[0], 16 * DB // 2 + START)
            sp.wait_ge(stored[1], 16 * DB // 2 + START)
            sp.dma_start(o_tok[0:NS, NTP, :], scratch.rearrange("b t h d -> (b t) (h d)")).then_inc(S_join, 16)
            sp.wait_ge(S_join, 16)

        @block.gpsimd
        def _(pool):
            qv = qkv[0:NS, NTP, 0:H * HD].rearrange("p (c e j d) -> p c e j d", c=2, e=2, j=GRP)
            for c in range(2):
                for e in range(2):
                    nc.gpsimd.tensor_copy(qt[:, c, :, e, :], qv[:, c, e]).then_inc(S_qt, 1)
            nc.gpsimd.memset(qbd[:], 0.0).then_inc(S_z, 1)
            pool.wait_ge(S_q, 4)
            pool.sem_inc(S_sc, START)
            with pool.Fori(0, DB) as b:
                pool.wait_ge(S_sc, b + START)
                nc.gpsimd.tensor_copy(qb[:], qbd[:, bass.ds(b, 1)].rearrange("p b c g j t -> p (b c) (g j t)")).then_inc(S_qb, 1)

        @block.tensor
        def _(pe):
            pe.wait_ge(S_qt, 4)
            for c in range(2):
                for j in range(GRP):
                    n = c * GRP + j
                    last = pe.transpose(bank[0][:, n * NS:(n + 1) * NS], qt[:, c, j, :, :].rearrange("p e d -> p (e d)"), ident[0:NS, 0:NS])
            last.then_inc(S_qps, 1)
            pe.wait_ge(S_q, 4)
            with pe.Fori(0, DB // 2) as i:
                for p in range(2):
                    b = i * 2 + p
                    pe.wait_ge(kv_in[p], (i + 1) * 64)
                    for c in range(2):
                        pe.transpose(bank[1][:, c * P:(c + 1) * P], ka[p][:, c * P:(c + 1) * P], ident[:])
                        last = pe.transpose(bank[1][:, 2 * P + c * DS:2 * P + (c + 1) * DS], kb[p][:, c * P:(c + 1) * P], ident[0:DS, 0:DS])
                    last.then_inc(S_ktps, 1)
                    pe.wait_ge(S_kt, b + 1)
                    pe.wait_ge(S_qb, b + 1)
                    for c in range(2):
                        last = pe.matmul(bank[2][:, 0:TK], qb[:, c, :], kT[:, c, :], start=(c == 0), stop=(c == 1))
                    last.then_inc(S_sc, 1)
                    pe.wait_ge(S_pr, b + 1)
                    pe.transpose(bank[3][:, 0:P], probs[:, DS:TK], ident[:])
                    pe.transpose(bank[3][0:DS, P:2 * P], probs[:, 0:DS], ident[:]).then_inc(S_ptps, 1)
                    pe.wait_ge(S_pt, b + 1)
                    pe.matmul(bank[4][:, 0:NKV], pT[:, 0:P], va[p][:], start=True, stop=False)
                    pe.matmul(bank[4][:, 0:NKV], pT[0:DS, P:2 * P], vb[p][:], start=False, stop=True).then_inc(S_ops, 1)

        @block.scalar
        def _(act):
            with act.Fori(0, DB) as b:
                act.wait_ge(S_ktps, b + 1)
                nc.scalar.copy(kT[:, :, DS:TK], bank[1][:, 0:2 * P].rearrange("p (c n) -> p c n", c=2))
                nc.scalar.copy(kT[:, :, 0:DS], bank[1][:, 2 * P:2 * P + 2 * DS].rearrange("p (c n) -> p c n", c=2)).then_inc(S_kt, 1)
                act.wait_ge(S_bias, b + 1)
                nc.scalar.activation(st[:, 3:4], snk[:], ACT.Exp, bias=st[:, 1:2])
                nc.scalar.activation(probs[:], bank[2][:, 0:TK], ACT.Exp, bias=st[:, 1:2], scale=SWA_SCALE,
                                     accum_out=st[:, 2:3]).then_inc(S_pr, 1)

        @block.vector
        def _(dve):
            ch = Chain(dve, S_dve)
            nc.vector.memset(o_tok[NS:P, NTP, :], 0.0)
            dve.sem_inc(stored[0], START)
            dve.sem_inc(stored[1], START)
            dve.wait_ge(S_z, 1)
            dve.wait_ge(S_qps, 1)
            for c in range(2):
                for e in range(2):
                    src = bank[0][e * HD:(e + 1) * HD, c * GRP * NS:(c + 1) * GRP * NS].rearrange("p (j b t) -> p b j t", j=GRP, b=DB)
                    nc.vector.tensor_copy(qbd[e * HD:(e + 1) * HD, :, c, 2 * c + e], src).then_inc(S_q, 1)
            dve.wait_ge(S_in, 32)
            with dve.Fori(0, DB // 2) as i:
                ch.round(i * 2 * PER)
                for p in range(2):
                    b = i * 2 + p
                    dve.wait_ge(S_sc, b + 1 + START)
                    sc = bank[2][:, 0:TK]
                    ch.step(nc.vector.tensor_tensor(sc, sc, mask[:], ALU.add))
                    ch.step(nc.vector.tensor_reduce(st[:, 0:1], sc, AX_X, ALU.max))
                    ch.step(nc.vector.tensor_scalar(st[:, 0:1], st[:, 0:1], SWA_SCALE, snk[:], ALU.mult, ALU.max))
                    nc.vector.tensor_scalar(st[:, 1:2], st[:, 0:1], -1.0, None, ALU.mult).then_inc(S_bias, 1)
                    dve.wait_ge(S_ptps, b + 1)
                    ch.inc(nc.vector.tensor_copy(pT[:, 0:P], bank[3][:, 0:P]))
                    nc.vector.tensor_copy(pT[0:DS, P:2 * P], bank[3][0:DS, P:2 * P]).then_inc(S_pt, 1)
                    ch.step(nc.vector.tensor_tensor(st[:, 4:5], st[:, 2:3], st[:, 3:4], ALU.add))
                    ch.step(nc.vector.reciprocal(st[:, 5:6], st[:, 4:5]))
                    dve.wait_ge(S_ops, b + 1 + START)
                    dve.wait_ge(stored[p], i * 16 + START)
                    for g in range(KVH):
                        rows = slice(g * GRP * DS, (g + 1) * GRP * DS)
                        last = nc.vector.tensor_scalar(ow[p][rows, :], bank[4][rows, g * HD:(g + 1) * HD], st[rows, 5:6], None, ALU.mult)
                    last.then_inc(S_o, 1)
                    dve.wait_ge(S_o, b + 1)
                ch.end(2 * PER)
    s.close()


def peer(nc, a, sbuf, sem, bank, x, ident, mod, stat, rstd, junk, tiles, layer, ahead=None):
    s = ExitStack()
    h2 = sbuf(s, f"h2_{layer}", [P, NT, D])
    best = sbuf(s, f"best{layer}", [P, NT, 2 * PH, TOPK])
    key = sbuf(s, f"key{layer}", [P, NT, 2 * PH, TOPK])
    ranks = dict(cand=sbuf(s, f"cand{layer}", [P, TOPK, TOPK]), rest=sbuf(s, f"rest{layer}", [P, TOPK * TOPK]),
                 best=sbuf(s, f"head_best{layer}", [P, TOPK]), place=sbuf(s, f"head_place{layer}", [P, TOPK], U32),
                 all_best=sbuf(s, f"all_best{layer}", [P, HK]), all_places=sbuf(s, f"all_places{layer}", [P, HK], U32))
    peer_keys(nc, a, sbuf, sem, bank, x, ident, mod, stat, rstd, junk, tiles, layer, h2, best, key, ranks)
    peer_mix(nc, a, sbuf, sem, bank, x, ident, mod, layer, h2, best, key, ranks, ahead)
    s.close()


def rank_head(nc, ch, settled, halves, ranks, hd):
    def ranked(ins):
        ch.inc(ins)
        wait_apart(ch.eng, ch.done, ch.base + ch.n, settled)
    cand, rest, best, place = ranks["cand"], ranks["rest"], ranks["best"], ranks["place"]
    flat = cand[:].rearrange("p i j -> p (i j)")
    ranked(nc.vector.tensor_tensor(cand[:], halves[0].unsqueeze(2).to_broadcast([P, TOPK, TOPK]),
                                   halves[1].unsqueeze(1).to_broadcast([P, TOPK, TOPK]), ALU.add))
    ranked(nc.vector.max(best[:, 0:8], flat))
    ranked(nc.vector.max_index(place[:, 0:8], best[:, 0:8], flat))
    ranked(nc.vector.match_replace(rest[:], best[:, 0:8], flat, -3e38))
    ranked(nc.vector.max(best[:, 8:16], rest[:]))
    ranked(nc.vector.max_index(place[:, 8:16], best[:, 8:16], rest[:]))
    ch.inc(nc.vector.tensor_copy(ranks["all_best"][:, bass.ds(hd * TOPK, TOPK)], best[:]))
    ch.inc(nc.vector.tensor_copy(ranks["all_places"][:, bass.ds(hd * TOPK, TOPK)], place[:]))
    wait_apart(ch.eng, ch.done, ch.base + ch.n, settled)


def peer_keys(nc, a, sbuf, sem, bank, x, ident, mod, stat, rstd, junk, tiles, layer, h2, best, key, ranks):
    tag = f"pk{layer}_"
    s = ExitStack()
    squares = sbuf(s, tag + "squares", [P, NT])
    rms_inv = sbuf(s, tag + "rms_inv", [P, NT])
    hT = sbuf(s, tag + "hT", [P, DC, NT * P])
    w = [sbuf(s, tag + f"w{i}", [P, DC, HALF]) for i in range(2)]
    sk = [sbuf(s, tag + f"sk{i}", [NK, HALF]) for i in range(2)]
    skT = [sbuf(s, tag + f"skT{i}", [HALF, NK]) for i in range(2)]
    qT = [sbuf(s, tag + f"qT{i}", [HALF, NT * P]) for i in range(2)]
    sc = [sbuf(s, tag + f"sc{i}", [P, NT, NK]) for i in range(2)]
    sc2 = sbuf(s, tag + "sc2", [P, NT, NK])
    bv = [sbuf(s, tag + f"bv{i}", [P, NT, TOPK]) for i in range(2)]
    bi = [sbuf(s, tag + f"bi{i}", [P, NT, TOPK], U32) for i in range(2)]
    names = "x_ss hT_ps hT_ready norm_step q_ps q_ready scores_ps scores_ready dve_step x_rms added twin"
    S_xss, S_hTps, S_hT, S_n, S_qps, S_q, S_sps, S_s, S_dve, S_xr, S_add, S_twin = [sem(tag + n) for n in names.split()]
    w_in = [sem(tag + f"w_in{i}") for i in range(2)]
    PAIR = 2 * 5 * NT + HEAD
    turned_bank = lambda t, half: bank[2 * (t % 2) + half]
    q_banks = [(bank[1], bank[2]), (bank[5], bank[6])]
    wq = a["peer_w_q"][layer].rearrange("(c p) n -> p c n", p=P)
    skeys = a["peer_sub_keys"][layer].rearrange("h s k d -> (h s) k d")
    with nc.Block() as block:
        @block.sync
        def _(sp):
            sp.dma_start(x[NS:P, NTP, :], x[0:NS, NTP, :]).then_inc(S_twin, 16)
            sp.sem_inc(S_qps, 2 * START)
            with sp.Fori(0, PH) as i:
                for p in range(2):
                    sp.wait_ge(S_qps, 2 * i + p + START)
                    sp.dma_start(w[p][:], wq[:, :, bass.ds((2 * i + p) * HALF, HALF)]).then_inc(w_in[p], 16)
                    sp.dma_start(sk[p][:], skeys[bass.ds(2 * i + p, 1)].rearrange("a k d -> (a k) d")).then_inc(w_in[p], 16)

        @block.gpsimd
        def _(pool):
            pool.wait_ge(S_xss, NT)
            nc.gpsimd.tensor_tensor(rms_inv[:], squares[:], stat[:, 3:4].to_broadcast([P, NT]), ALU.add).then_inc(S_add, 1)
            pool.wait_ge(S_add, 1)
            nc.gpsimd.tensor_tensor(rms_inv[:], rms_inv[:], stat[:, 4:5].to_broadcast([P, NT]), ALU.pow).then_inc(S_xr, 1)

        @block.scalar
        def _(act):
            for t in range(NT):
                if t == NTP:
                    act.wait_ge(S_twin, 16)
                if t:
                    act.wait_ge(S_xss, t)
                nc.scalar.activation(junk[:], x[:, t, :], ACT.Square, scale=D ** -0.5,
                                     accum_out=squares[:, t:t + 1]).then_inc(S_xss, 1)
            for t in range(NT):
                for half in range(2):
                    act.wait_ge(S_hTps, 2 * t + half + 1)
                    nc.scalar.copy(hT[:, 4 * half:4 * half + 4, t * P:(t + 1) * P],
                                   turned_bank(t, half)[:].rearrange("p (c n) -> p c n", c=4)).then_inc(S_hT, 1)
            with act.Fori(0, PH) as i:
                for p in range(2):
                    wide, narrow = q_banks[p]
                    act.wait_ge(S_qps, 2 * i + p + 1 + 2 * START)
                    nc.scalar.copy(skT[p][:], narrow[:, P:2 * P])
                    nc.scalar.copy(qT[p][:, 0:SEQ], wide[:])
                    nc.scalar.copy(qT[p][:, SEQ:NT * P], narrow[:, 0:P]).then_inc(S_q, 1)
                    act.wait_ge(S_sps, 2 * i + p + 1)
                    act.wait_ge(S_dve, i * PAIR + START)
                    nc.scalar.copy(sc[p][:, 0:NTP, :], bank[3][:].rearrange("p (t n) -> p t n", t=NTP))
                    nc.scalar.copy(sc[p][:, NTP, :], bank[4][:, 0:P]).then_inc(S_s, 1)

        @block.vector
        def _(dve):
            ch = Chain(dve, S_n)
            dve.wait_ge(S_xr, 1)
            for t in range(NT):
                norm_steps(nc, ch, x, mod, rms_inv[:, t:t + 1], h2[:, t, :], t, t // NTP)
            ch = Chain(dve, S_dve)
            dve.sem_inc(S_dve, START)
            with dve.Fori(0, PH) as i:
                ch.round(i * PAIR + START)
                for p in range(2):
                    wait_apart(dve, S_s, 2 * i + p + 1 + START, (S_n, 1))

                    def each(f):
                        for t in range(NT):
                            ch.inc(f(t))
                        wait_apart(dve, S_dve, ch.base + ch.n, (S_n, 1))

                    each(lambda t: nc.vector.max(bv[p][:, t, 0:8], sc[p][:, t, :]))
                    each(lambda t: nc.vector.max_index(bi[p][:, t, 0:8], bv[p][:, t, 0:8], sc[p][:, t, :]))
                    each(lambda t: nc.vector.match_replace(sc2[:, t, :], bv[p][:, t, 0:8], sc[p][:, t, :], -3e38))
                    each(lambda t: nc.vector.max(bv[p][:, t, 8:16], sc2[:, t, :]))
                    each(lambda t: nc.vector.max_index(bi[p][:, t, 8:16], bv[p][:, t, 8:16], sc2[:, t, :]))
                    nc.vector.tensor_copy(best[:, :, bass.ds(2 * i + p, 1), :].rearrange("p t a k -> p t (a k)"), bv[p][:])
                    nc.vector.tensor_copy(key[:, :, bass.ds(2 * i + p, 1), :].rearrange("p t a k -> p t (a k)"), bi[p][:])
                rank_head(nc, ch, (S_n, 1), [bv[0][:, 0, :], bv[1][:, 0, :]], ranks, i)
                assert ch.n == PAIR

        @block.tensor
        def _(pe):
            for t in range(NT):
                pe.wait_ge(S_n, 2 * t + 2)
                if t >= 2:
                    pe.wait_ge(S_hT, 2 * t - 2)
                for half in range(2):
                    for c in range(4):
                        last = pe.transpose(turned_bank(t, half)[:, c * P:(c + 1) * P],
                                            h2[:, t, (4 * half + c) * P:(4 * half + c + 1) * P], ident[:])
                    last.then_inc(S_hTps, 1)
            pe.wait_ge(S_hT, 2 * NT)
            pe.sem_inc(S_s, START)

            def queries(i, p):
                wide, narrow = q_banks[p]
                pe.wait_ge(w_in[p], (i + 1) * 32)
                pe.transpose(narrow[:, P:2 * P], sk[p][:], ident[:])
                for c in range(DC):
                    pe.matmul(wide[:], w[p][:, c, :], hT[:, c, 0:SEQ], start=(c == 0), stop=(c == DC - 1))
                for c in range(DC):
                    last = pe.matmul(narrow[:, 0:P], w[p][:, c, :], hT[:, c, SEQ:NT * P], start=(c == 0), stop=(c == DC - 1))
                last.then_inc(S_qps, 1)

            def scores(i, p):
                pe.wait_ge(S_q, 2 * i + p + 1)
                pe.wait_ge(S_s, 2 * i + p + START)
                for t in range(NT):
                    last = pe.matmul(bank[3 + t // 4][:, (t % 4) * P:(t % 4 + 1) * P], qT[p][:, t * P:(t + 1) * P], skT[p][:],
                                     start=True, stop=True)
                last.then_inc(S_sps, 1)

            queries(0, 0)
            with pe.Fori(0, PH - 1) as i:
                queries(i, 1)
                scores(i, 0)
                queries(i + 1, 0)
                scores(i, 1)
            queries(PH - 1, 1)
            scores(PH - 1, 0)
            scores(PH - 1, 1)
    s.close()


def peer_mix(nc, a, sbuf, sem, bank, x, ident, mod, layer, h2, best, key, ranks, ahead):
    tag = f"px{layer}_"
    s = ExitStack()
    ND = 2 * RING
    ur = [sbuf(s, tag + f"u{i}", [P, D]) for i in range(RING)]
    v_ring = sbuf(s, tag + "v", [P, RING, D])
    vr = [v_ring[:, i, :] for i in range(RING)]
    if ahead:
        cT, mod_rows = ahead
        NCH = 6 * D // 512
        w = [v_ring[:, i * RING // 2:(i + 1) * RING // 2, :].rearrange("p a (b n) -> p (a b) n", n=512) for i in range(2)]
        rows = [sbuf(s, tag + f"rows{i}", [DB + 1, 512]) for i in range(2)]
        w_in = [sem(tag + f"w_in{i}") for i in range(2)]
        stored = [sem(tag + f"rows_stored{i}") for i in range(2)]
        S_rps, S_row = sem(tag + "rows_ps"), sem(tag + "rows_ready")
        w_src = a["w_mod"][layer + 1].rearrange("(c p) n -> p c n", p=P)
    diag = [sbuf(s, tag + f"d{i}", [P, P]) for i in range(ND)]
    uid = [sbuf(s, tag + f"uid{i}", [P, RING], I32) for i in range(2)]
    vid = [sbuf(s, tag + f"vid{i}", [P, RING], I32) for i in range(2)]
    experts = sbuf(s, tag + "experts", [P, NT * HK], I32)
    e = sbuf(s, tag + "e", [P, NT, HK])
    dots = sbuf(s, tag + "dots", [P, NT, HK])
    gelus = sbuf(s, tag + "gelus", [P, HK])
    coef = sbuf(s, tag + "coef", [P, HK])
    esum = sbuf(s, tag + "esum", [P, PH, 1])
    zero = sbuf(s, tag + "zero", [P, 512])
    y = sbuf(s, tag + "y", [P, D])
    bvt, bpt = ranks["all_best"], ranks["all_places"]
    ij = sbuf(s, tag + "ij", [P, 2, HK], U32)
    ijf = sbuf(s, tag + "ijf", [P, 2, HK])
    iota = sbuf(s, tag + "iota", [P, 1, TOPK])
    pair = sbuf(s, tag + "pair", [P, NS])
    hot = sbuf(s, tag + "hot", [P, HK, TOPK])
    num = sbuf(s, tag + "num", [P, 2, HK])
    u_in = [sem(tag + f"u_in{i}") for i in range(RING)]
    v_in = [sem(tag + f"v_in{i}") for i in range(RING)]
    names = "zeroed u_free v_free uid_ready vid_ready gelu coef diag_ready out_ps out_step experts_ready rank_step iota_in shifted exp_ready gate_step"
    (S_z, S_uf, S_vf, S_uid, S_vid, S_g, S_c, S_d, S_ops, S_out, S_ex, S_rank, S_in, S_sub, S_exp, S_gate) = [
        sem(tag + n) for n in names.split()]
    u_tab, v_tab = a["peer_u"].rearrange("l e d -> (l e) d"), a["peer_v"].rearrange("l e d -> (l e) d")
    offset = bass.IndirectOffsetOnAxis
    OUT_FREE = 2 * 3
    WHOLE = [(slice(0, P), HK, 0)]
    HALVES = [(slice(0, NS), PAIRED, 0), (slice(NS, P), PAIRED, PAIRED)]
    PER = HEAD * PH + 2 + 1 + 2 * 3 + 1
    bestv = best[:].rearrange("p t h k -> p (t h) k")
    with nc.Block() as block:
        @block.sync
        def _(sp):
            sp.dma_start(iota[:], a["k_iota"]).then_inc(S_in, 16)
            sp.dma_start(pair[:], a["k_pair"]).then_inc(S_in, 16)
            if ahead:
                sp.sem_inc(S_rps, 2 * START)
                sp.sem_inc(S_row, START)
                with sp.Fori(0, NCH // 2) as i:
                    for odd in range(2):
                        n = 2 * i + odd
                        sp.wait_ge(S_rps, n + START)
                        sp.dma_start(w[odd], w_src[:, :, bass.ds(n * 512, 512)]).then_inc(w_in[odd], 16)
                for odd in range(2):
                    sp.wait_ge(stored[odd], NCH // 2 * 16 + START)

        @block.gpsimd
        def _(pool):
            nc.gpsimd.memset(zero[:], 0.0).then_inc(S_z, 1)
            nc.gpsimd.memset(y[:], 0.0).then_inc(S_vf, ND)

            def fetch(table, ring, ids, ready, free, spare, landed, it, odd):
                nc.gpsimd.tensor_copy(ids[odd][:], experts[:, bass.ds(it * RING, RING)]).then_inc(ready, 1)
                wait_apart(pool, ready, it + 1, (S_z, 1))
                for r in range(RING):
                    wait_apart(pool, free, it * RING + r + 1 + spare, (S_z, 1))
                    pool.indirect_dma_start(ring[r][:], None, table,
                                            offset(ap=ids[odd][:, r:r + 1], axis=0)).then_inc(landed[r], 16)

            def u_rows(it, odd):
                fetch(u_tab, ur, uid, S_uid, S_uf, 0, u_in, it, odd)

            def v_rows(it, odd):
                fetch(v_tab, vr, vid, S_vid, S_vf, ND - RING, v_in, it, odd)

            BEHIND = SLOTS + LAG

            def rounds(first, last, u=True, v=True):
                with pool.Fori(first // 2, last // 2) as i:
                    for odd in range(2):
                        if u:
                            u_rows(2 * i + odd, odd)
                        if v:
                            v_rows(2 * i + odd - BEHIND, odd)

            ALL = NTP * SLOTS + PAIRED // RING
            pool.wait_ge(S_ex, 1)
            rounds(0, SLOTS, v=False)
            pool.wait_ge(S_ex, 2)
            rounds(SLOTS, BEHIND, v=False)
            if ahead:
                pool.wait_ge(S_rps, NCH + 2 * START)
            rounds(BEHIND, 2 * SLOTS)
            for t in range(2, NTP):
                pool.wait_ge(S_ex, t + 1)
                rounds(t * SLOTS, (t + 1) * SLOTS)
            pool.wait_ge(S_ex, NT)
            rounds(NTP * SLOTS, ALL)
            rounds(ALL, ALL + BEHIND, u=False)

        @block.vector
        def _(dve):
            nc.vector.memset(coef[:], 0.0).then_inc(S_uf, RING)
            dve.sem_inc(S_d, START)
            dve.wait_ge(S_in, 32)
            ch = Chain(dve, S_rank)
            dve.sem_inc(S_rank, PH * HEAD)

            def dot(t, j):
                for r in range(RING):
                    dve.wait_ge(u_in[r], (t * SLOTS + j + 1) * 16)
                    nc.vector.scalar_tensor_tensor(out=ur[r][:], in0=ur[r][:], scalar=1.0, in1=h2[:, t, :],
                                                   op0=ALU.mult, op1=ALU.mult,
                                                   accum_out=dots[:, t, bass.ds(j * RING + r, 1)]).then_inc(S_uf, 1)

            def rank(t, hd):
                ch.round(t * PER + hd * HEAD)
                rank_head(nc, ch, (S_in, 32), [bestv[:, bass.ds(t * 2 * PH + hd * 2 + half, 1), :].rearrange("p a k -> p (a k)")
                                               for half in range(2)], ranks, hd)

            def key_numbers(t, half):
                if half == 0:
                    ch.round(t * PER + PH * HEAD)
                    ch.inc(nc.vector.tensor_scalar(ij[:, 0, :], bpt[:], 4, None, ALU.logical_shift_right))
                    ch.step(nc.vector.tensor_scalar(ij[:, 1, :], bpt[:], TOPK - 1, None, ALU.bitwise_and))
                    ch.step(nc.vector.tensor_copy(ijf[:], ij[:]))
                kt = key[:, bass.ds(t, 1)].rearrange("p a (h s) k -> p (a h) s k", s=2)
                pos = ijf[:, half, :].unsqueeze(2).to_broadcast([P, HK, TOPK])
                hotv = hot[:].rearrange("p (h k) i -> p h k i", h=PH)
                ch.step(nc.vector.tensor_tensor(hot[:], pos, iota[:].to_broadcast([P, HK, TOPK]), ALU.is_equal))
                ch.step(nc.vector.tensor_tensor(hotv, hotv, kt[:, :, half, :].unsqueeze(2).to_broadcast([P, PH, TOPK, TOPK]), ALU.mult))
                ch.step(nc.vector.tensor_reduce(num[:, half, :], hot[:], AX_X, ALU.add))

            def number(t):
                bt = bvt[:].rearrange("p (h k) -> p h k", h=PH)
                nc.vector.tensor_tensor(e[:, t, :].rearrange("p (h k) -> p h k", h=PH), bt,
                                        bt[:, :, 0:1].to_broadcast([P, PH, TOPK]), ALU.subtract).then_inc(S_sub, 1)
                ch.step(nc.vector.scalar_tensor_tensor(out=num[:, 0, :], in0=num[:, 0, :], scalar=float(NK), in1=num[:, 1, :],
                                                       op0=ALU.mult, op1=ALU.add))
                assert ch.n == PER - PH * HEAD
                at = t * HK
                for rows, n, first in HALVES if t == NTP else WHOLE:
                    last = nc.vector.tensor_scalar(experts[rows, at:at + n], num[rows, 0, first:first + n],
                                                   float(layer * NK * NK), None, ALU.add)
                last.then_inc(S_ex, 1)

            def gate(t):
                ev = e[:, t, :].rearrange("p (h k) -> p h k", h=PH)
                dve.wait_ge(S_exp, t + 1)
                nc.vector.tensor_reduce(esum[:, :, 0], ev, AX_X, ALU.add).then_inc(S_gate, 1)
                dve.wait_ge(S_gate, t * 3 + 1)
                nc.vector.reciprocal(esum[:], esum[:]).then_inc(S_gate, 1)
                dve.wait_ge(S_gate, t * 3 + 2)
                nc.vector.tensor_tensor(ev, ev, esum[:].to_broadcast([P, PH, TOPK]), ALU.mult).then_inc(S_gate, 1)
                dve.wait_ge(S_gate, t * 3 + 3)
                dve.wait_ge(S_g, t + 1)
                dve.wait_ge(S_d, t * HK + START)
                for rows, n, first in HALVES if t == NTP else WHOLE:
                    last = nc.vector.tensor_tensor(coef[rows, 0:n], gelus[rows, 0:n], e[rows, t, first:first + n], ALU.mult)
                last.then_inc(S_c, 1)

            def add(t, kind, rows):
                banks = 2 * (t % 2)
                dve.wait_ge(S_ops, t + 1)
                for n in range(2):
                    nc.vector.tensor_tensor(y[0:rows, n * 512:(n + 1) * 512], bank[banks + n][0:rows, :],
                                            mod[0:rows, kind, 2 * D + n * 512:2 * D + (n + 1) * 512], ALU.mult).then_inc(S_out, 1)
                dve.wait_ge(S_out, 3 * t + 2 + OUT_FREE)
                nc.vector.tensor_tensor(x[0:rows, t, :], x[0:rows, t, :], y[0:rows, :], ALU.add).then_inc(S_out, 1)
                dve.wait_ge(S_out, 3 * t + 3 + OUT_FREE)

            def tile(t):
                dot(t, 0)
                if t >= 1:
                    gate(t - 1)
                with dve.Fori(0, PH) as hd:
                    dot(t, hd + 1)
                    rank(t + 1, hd)
                dot(t, PH + 1)
                if t >= 2:
                    add(t - 2, 0, P)
                key_numbers(t + 1, 0)
                dot(t, PH + 2)
                key_numbers(t + 1, 1)
                dot(t, PH + 3)
                number(t + 1)
                with dve.Fori(PH + 4, SLOTS) as j:
                    dot(t, j)

            key_numbers(0, 0)
            key_numbers(0, 1)
            number(0)
            for t in range(NTP):
                tile(t)
            dot(NTP, 0)
            gate(NTP - 1)
            with dve.Fori(1, PAIRED // RING) as j:
                dot(NTP, j)
            add(NTP - 2, 0, P)
            gate(NTP)
            add(NTP - 1, 0, P)
            add(NTP, 1, NS)

        @block.scalar
        def _(act):
            def rows_ahead():
                act.sem_inc(stored[0], START)
                act.sem_inc(stored[1], START)
                with act.Fori(0, NCH // 2) as i:
                    for odd in range(2):
                        act.wait_ge(S_rps, 2 * i + odd + 1 + 2 * START)
                        wait_apart(act, stored[odd], 16 * i + START, (S_z, 1))
                        nc.scalar.copy(rows[odd][:], bank[4 + odd][0:DB + 1, :]).then_inc(S_row, 1)
                        wait_apart(act, S_row, 2 * i + odd + 1 + START, (S_z, 1))
                        act.dma_start(mod_rows[:, bass.ds((2 * i + odd) * 512, 512)], rows[odd][:]).then_inc(stored[odd], 16)

            def exps(t):
                act.wait_ge(S_sub, t + 1)
                nc.scalar.activation(e[:, t, :], e[:, t, :], ACT.Exp).then_inc(S_exp, 1)

            def gelu(t, n):
                act.wait_ge(S_uf, t * HK + n + RING)
                nc.scalar.activation(gelus[:, 0:n], dots[:, t, 0:n], ACT.Gelu).then_inc(S_g, 1)

            def diagonals(t, n, shape):
                act.wait_ge(S_c, t + 1)
                with act.Fori(0, n // ND) as j:
                    for r in range(ND):
                        wait_apart(act, S_vf, t * HK + j * ND + r + 1, (S_z, 1))
                        nc.scalar.activation(diag[r][:, 0:shape.shape[1]], shape[:], ACT.Copy,
                                             scale=coef[:, bass.ds(j * ND + r, 1)]).then_inc(S_d, 1)

            if ahead:
                rows_ahead()
            exps(0)
            with act.Fori(0, NTP) as t:
                exps(t + 1)
                gelu(t, HK)
                diagonals(t, HK, ident)
            gelu(NTP, PAIRED)
            act.wait_ge(S_in, 32)
            diagonals(NTP, PAIRED, pair)

        @block.tensor
        def _(pe):
            pe.wait_ge(S_z, 1)
            pe.sem_inc(S_out, OUT_FREE)
            if ahead:
                with pe.Fori(0, NCH // 2) as i:
                    for odd in range(2):
                        pe.wait_ge(w_in[odd], 16 * i + 16)
                        wait_apart(pe, S_row, 2 * i + START, (S_z, 1))
                        for c in range(DC):
                            last = pe.matmul(bank[4 + odd][0:DB + 1, :], cT[:, c, :], w[odd][:, c, :], start=(c == 0), stop=(c == DC - 1))
                        last.then_inc(S_rps, 1)

            def mix(t, n, rows, banks):
                lo, hi = bank[banks], bank[banks + 1]
                pe.wait_ge(S_out, 3 * t + OUT_FREE - 3)
                for b in (lo, hi):
                    pe.matmul(b[0:rows, :], zero[:, 0:rows], zero[:], start=True, stop=False)
                with pe.Fori(0, n // ND) as j:
                    for r in range(ND):
                        v = r % RING
                        d_at = t * HK + j * ND + r + 1 + START
                        v_at = (t * SLOTS + j * (ND // RING) + r // RING + 1) * 16
                        d_at, v_at = pe.to_reg(d_at), pe.to_reg(v_at)
                        pe.wait_ge(S_z, 1)
                        pe.wait_ge(S_d, d_at)
                        pe.wait_ge(v_in[v], v_at)
                        pe.matmul(lo[0:rows, :], diag[r][:, 0:rows], vr[v][:, 0:512], start=False, stop=False)
                        pe.matmul(hi[0:rows, :], diag[r][:, 0:rows], vr[v][:, 512:D], start=False, stop=False).then_inc(S_vf, 1)
                for b in (lo, hi):
                    last = pe.matmul(b[0:rows, :], zero[:, 0:rows], zero[:], start=False, stop=True)
                last.then_inc(S_ops, 1)

            with pe.Fori(0, NTP, 2) as t:
                mix(t, HK, P, 0)
                mix(t + 1, HK, P, 2)
            mix(NTP, PAIRED, NS, 0)
    s.close()


def final_norm(nc, a, o, sbuf, sem, x, stat, rstd, junk, tiles):
    s = ExitStack()
    g = sbuf(s, "fn_g", [P, D])
    y = [sbuf(s, f"fn_y{i}", [P, D]) for i in range(2)]
    S_in, S_ss, S_r, S_dve, S_st, S_add = [sem("fn_" + n) for n in "gain_in x_ss x_rms dve_step stored added".split()]
    with nc.Block() as block:
        @block.sync
        def _(sp):
            sp.dma_start(g[:], a["final_g"].rearrange("(a d) -> a d", a=1).to_broadcast([P, D])).then_inc(S_in, 16)
            for t in range(NT):
                sp.wait_ge(S_dve, t + 1)
                if t < NTP:
                    sp.dma_start(o["y_p"][0, t * P:(t + 1) * P, :], y[t % 2][:]).then_inc(S_st, 16)
                else:
                    sp.dma_start(o["y_s"].rearrange("b t d -> (b t) d"), y[t % 2][0:NS, :]).then_inc(S_st, 16)
                sp.wait_ge(S_st, 16 * (t + 1))

        @block.scalar
        def _(act):
            for t in range(NT):
                act.wait_ge(S_r, t)
                nc.scalar.activation(junk[:], x[:, t, :], ACT.Square, scale=D ** -0.5, accum_out=stat[:, 0:1]).then_inc(S_ss, 1)

        @block.gpsimd
        def _(pool):
            for t in range(NT):
                pool.wait_ge(S_ss, t + 1)
                pool.wait_ge(S_dve, t)
                rms(nc, rstd, stat, slice(0, 1), S_add, t + 1).then_inc(S_r, 1)

        @block.vector
        def _(dve):
            dve.wait_ge(S_in, 16)
            for t in range(NT):
                dve.wait_ge(S_r, t + 1)
                if t >= 2:
                    dve.wait_ge(S_st, 16 * (t - 1))
                nc.vector.scalar_tensor_tensor(out=y[t % 2][:], in0=x[:, t, :], scalar=rstd[:, 0:1], in1=g[:],
                                               op0=ALU.mult, op1=ALU.mult).then_inc(S_dve, 1)
    s.close()


def constants():
    f = np.float32
    c = {"k_ident": np.eye(P, dtype=f), "k_iota": np.tile(np.arange(TOPK, dtype=f), (P, 1)).reshape(P, 1, TOPK)}
    r = np.arange(P)
    sel = np.zeros((DB + 1, 2, P), f)
    sel[0, 0, :] = 1
    for b in range(DB):
        sel[1 + b, 1, b * DS:(b + 1) * DS] = 1
        sel[1 + b, 1, NS + b * DS:NS + (b + 1) * DS] = 1
    c["k_sel"] = sel
    c["k_pair"] = np.tile(np.eye(NS, dtype=f), (2, 1))
    c["k_causal"] = np.where(r[None, :] <= r[:, None], 0, NEG).astype(f)
    c["k_band"] = np.concatenate([np.where(r[None, :] > r[:, None], 0, NEG), c["k_causal"]], axis=1).astype(f)
    step = (r % DS)[:, None, None]
    new = np.arange(NS)[None, None, :]
    c["k_mask_new"] = np.where((new // DS == np.arange(DB)[None, :, None]) & (new % DS <= step), 0, NEG).astype(f)
    j = np.arange(P + DS)[None, :]
    t = (r % DS)[:, None]
    c["k_mask_win"] = np.where((j <= P + t) & (j > t), 0, NEG).astype(f)
    pos = np.concatenate([np.arange(SEQ), PAST + r % DS]).astype(f)
    for n in (ROPE, ROT):
        half = n // 2
        e = (-np.arange(half, dtype=f) * f(2.0) / f(n)).astype(np.float64)
        inv = np.power(500000.0, e).astype(f)
        ang = (pos[:, None] * inv[None, :]).astype(f).astype(np.float64)
        cos, sin = np.cos(ang).astype(f), np.sin(ang).astype(f)
        lay = lambda v: np.ascontiguousarray(v.reshape(NT, P, n).transpose(1, 0, 2))
        c[f"k_cos{n}"] = lay(np.concatenate([cos, cos], 1))
        c[f"k_sin{n}"] = lay(np.concatenate([-sin, sin], 1))
    return c


_INS = ['x_prompt', 'x_sample', 'cache_mla_ckv', 'cache_mla_kpe', 'cache_swa_k', 'cache_swa_v', 'page_table',
        'c_prompt', 'c_sample', 'ln1_g', 'ln2_g', 'w_mod', 'b_mod', 'mla_w_in', 'mla_q_norm', 'mla_kv_norm',
        'mla_w_uq', 'mla_w_uk', 'mla_w_uv', 'mla_w_o', 'swa_w_qkv', 'swa_b_qkv', 'swa_sinks', 'swa_w_o',
        'peer_w_q', 'peer_sub_keys', 'peer_u', 'peer_v', 'final_g']
_OUTS = [('y_p', (1, SEQ, D)), ('y_s', (DB, DS, D)), ('ckv_p', (1, 1, SEQ, KL)), ('kpe_p', (1, 1, SEQ, ROPE)),
         ('ckv_s', (1, DB, DS, KL)), ('kpe_s', (1, DB, DS, ROPE)), ('swk_p', (1, 1, P, KVH, HD)),
         ('swv_p', (1, 1, P, KVH, HD)), ('swk_s', (1, DB, P, KVH, HD)), ('swv_s', (1, DB, P, KVH, HD))]


def kernel(**inputs):
    import concourse.bacc as _bacc
    from concourse.bass_utils import run_bass_kernel_spmd as _run

    nc = _bacc.Bacc("TRN2", target_bir_lowering=False, num_devices=1)
    arrays = {name: np.ascontiguousarray(inputs[name]) for name in _INS}
    arrays.update(constants())
    args = {name: nc.dram_tensor(f"in_{name}", v.shape, mybir.dt.from_np(v.dtype), kind="ExternalInput").ap()
            for name, v in arrays.items()}
    outs = {name: nc.dram_tensor(f"out_{name}", shape, F32, kind="ExternalOutput").ap() for name, shape in _OUTS}
    build(nc, args, outs)
    r = _run(nc, [{f"in_{name}": v for name, v in arrays.items()}], core_ids=[0])
    return tuple(r.results[0][f"out_{name}"] for name, _ in _OUTS)
```
